# Optimizing a Trainium2 kernel written in Bass

```python
import math
import jax, jax.numpy as jnp
from jax import lax
import numpy as np

D_MODEL = 1024
BATCH = 1
SEQ = 256
DEPTH = 1

A_HEADS = 4
A_HEAD_DIM = 128
A_WIDTH = A_HEADS * A_HEAD_DIM
A_CHUNK = 128
B_WIDTH = 512
B_KERNEL = 31
C_HEADS = 8
C_NOPE = 64
C_ROPE = 32
C_QK_DIM = C_NOPE + C_ROPE
C_VDIM = 64
C_Q_RANK = 384
C_KV_RANK = 256
Q_BLOCK = 128
ROPE_THETA = 10000.0
N_BRANCHES = 3
N_EXPERTS = 16
EXPERT_FF = 1536
CAPACITY_FACTOR = 2
EPS = 1e-6

IN_SIZES = (
    A_WIDTH,
    A_WIDTH,
    A_WIDTH,
    A_WIDTH,
    4 * A_HEADS,
    2 * B_WIDTH,
    C_Q_RANK,
    C_KV_RANK,
    C_ROPE,
    N_BRANCHES * D_MODEL,
)
IN_WIDTH = int(sum(IN_SIZES))
IN_OFFSETS = tuple(int(o) for o in np.cumsum(IN_SIZES)[:-1])


def _rmsnorm(x, g):
    xf = x.astype(jnp.float32)
    y = xf * lax.rsqrt(jnp.mean(xf * xf, axis=-1, keepdims=True) + EPS)
    return (y * g.astype(jnp.float32)).astype(x.dtype)

def _layernorm(x, g, b):
    xf = x.astype(jnp.float32)
    mu = jnp.mean(xf, axis=-1, keepdims=True)
    xc = xf - mu
    y = xc * lax.rsqrt(jnp.mean(xc * xc, axis=-1, keepdims=True) + EPS)
    return (y * g.astype(jnp.float32) + b.astype(jnp.float32)).astype(x.dtype)

def _mlstm_chunkwise(q, k, v, i_pre, f_pre):
    B, H, S, Dh = q.shape
    nc = S // A_CHUNK
    f32 = jnp.float32

    def chunks(t):
        return jnp.moveaxis(t.astype(f32).reshape(B, H, nc, A_CHUNK, *t.shape[3:]), 2, 0)

    qc = chunks(q)
    kc = chunks(k) * (Dh ** -0.5)
    vc = chunks(v)
    ic = chunks(i_pre)
    lfc = chunks(jax.nn.log_sigmoid(f_pre.astype(f32)))
    tril = jnp.tril(jnp.ones((A_CHUNK, A_CHUNK), dtype=bool))

    def step(carry, inp):
        C, n, m = carry
        qb, kb, vb, ib, lfb = inp
        bcum = jnp.cumsum(lfb, axis=-1)
        dlog = bcum[..., :, None] - bcum[..., None, :] + ib[..., None, :]
        dlog = jnp.where(tril, dlog, -jnp.inf)
        m_inter = bcum + m[..., None]
        m_t = jnp.maximum(m_inter, jnp.max(dlog, axis=-1))
        w_inter = jnp.exp(m_inter - m_t)
        scores = jnp.einsum('bhtd,bhsd->bhts', qb, kb) * jnp.exp(dlog - m_t[..., None])
        num = (w_inter[..., None] * jnp.einsum('bhtd,bhde->bhte', qb, C)
               + jnp.einsum('bhts,bhse->bhte', scores, vb))
        den = w_inter * jnp.einsum('bhtd,bhd->bht', qb, n) + jnp.sum(scores, axis=-1)
        h = num / jnp.maximum(jnp.abs(den), jnp.exp(-m_t))[..., None]
        g_tot = bcum[..., -1]
        a = g_tot[..., None] - bcum + ib
        m_new = jnp.maximum(g_tot + m, jnp.max(a, axis=-1))
        decay = jnp.exp(g_tot + m - m_new)
        wk = jnp.exp(a - m_new[..., None])
        C_new = decay[..., None, None] * C + jnp.einsum('bhs,bhsd,bhse->bhde', wk, kb, vb)
        n_new = decay[..., None] * n + jnp.einsum('bhs,bhsd->bhd', wk, kb)
        return (C_new, n_new, m_new), h

    init = (jnp.zeros((B, H, Dh, Dh), f32), jnp.zeros((B, H, Dh), f32), jnp.zeros((B, H), f32))
    _, h = lax.scan(step, init, (qc, kc, vc, ic, lfc))
    return jnp.moveaxis(h, 0, 2).reshape(B, H, S, Dh)

def _rope_tail(t, cos, sin):
    nope, r = t[..., :C_NOPE], t[..., C_NOPE:]
    r1, r2 = jnp.split(r, 2, axis=-1)
    c = cos[:, None, :].astype(t.dtype)
    s = sin[:, None, :].astype(t.dtype)
    return jnp.concatenate([nope, r1 * c - r2 * s, r2 * c + r1 * s], axis=-1)

def _dense_attention(q, k, v):
    B, H, S, Dq = q.shape
    nq = S // Q_BLOCK
    qb = jnp.moveaxis(q.reshape(B, H, nq, Q_BLOCK, Dq), 2, 0)
    scale = Dq ** -0.5

    def block(qi):
        s = jnp.einsum('bhqd,bhkd->bhqk', qi, k).astype(jnp.float32) * scale
        p = jax.nn.softmax(s, axis=-1).astype(v.dtype)
        return jnp.einsum('bhqk,bhkd->bhqd', p, v)

    o = lax.map(block, qb)
    return jnp.moveaxis(o, 0, 2).reshape(B, H, S, v.shape[-1])

def _mixer(x, cos, sin, norm_g, w_in, b_if, a_norm_g, w_a_out, conv_w, conv_b,
           conv_ln_g, conv_ln_b, w_b_out, cq_norm_g, w_uq, ckv_norm_g, w_ukv,
           q_norm_g, k_norm_g, w_c_out, w_out):
    B, S, _ = x.shape
    xn = _rmsnorm(x, norm_g)
    z = xn @ w_in
    a_q, a_k, a_v, a_o, a_g, b_glu, c_q, c_kv, c_kr, gts = jnp.split(z, IN_OFFSETS, axis=-1)

    def heads(t):
        return t.reshape(B, S, A_HEADS, A_HEAD_DIM).transpose(0, 2, 1, 3)
    q, k, v = heads(a_q), heads(a_k), heads(a_v)
    gate_pre = (a_g + b_if).reshape(B, S, 4, A_HEADS).transpose(2, 0, 3, 1)
    i_fw, f_fw, i_bw, f_bw = gate_pre[0], gate_pre[1], gate_pre[2], gate_pre[3]
    rev = lambda t: jnp.flip(t, axis=2)
    h_fw = _mlstm_chunkwise(q, k, v, i_fw, f_fw)
    h_bw = rev(_mlstm_chunkwise(rev(q), rev(k), rev(v), rev(i_bw), rev(f_bw)))
    h = _rmsnorm(h_fw + h_bw, a_norm_g[:, None, :])
    h = h.transpose(0, 2, 1, 3).reshape(B, S, A_WIDTH) * jax.nn.sigmoid(a_o)
    y_a = h @ w_a_out

    u_a, u_g = jnp.split(b_glu, 2, axis=-1)
    u = u_a * jax.nn.sigmoid(u_g)
    u = lax.conv_general_dilated(
        u, conv_w[:, None, :].astype(u.dtype), window_strides=(1,),
        padding=[(B_KERNEL // 2, B_KERNEL // 2)],
        dimension_numbers=('NWC', 'WIO', 'NWC'),
        feature_group_count=B_WIDTH) + conv_b
    u = jax.nn.silu(_layernorm(u, conv_ln_g, conv_ln_b))
    y_b = u @ w_b_out

    qh = (_rmsnorm(c_q, cq_norm_g) @ w_uq).reshape(B, S, C_HEADS, C_QK_DIM)
    kv = (_rmsnorm(c_kv, ckv_norm_g) @ w_ukv).reshape(B, S, C_HEADS, C_NOPE + C_VDIM)
    k_nope, v_c = kv[..., :C_NOPE], kv[..., C_NOPE:]
    k_r = jnp.broadcast_to(c_kr[:, :, None, :], (B, S, C_HEADS, C_ROPE))
    kh = jnp.concatenate([k_nope, k_r], axis=-1)
    qh = _rope_tail(_rmsnorm(qh, q_norm_g), cos, sin)
    kh = _rope_tail(_rmsnorm(kh, k_norm_g), cos, sin)
    o = _dense_attention(qh.transpose(0, 2, 1, 3), kh.transpose(0, 2, 1, 3),
                         v_c.transpose(0, 2, 1, 3))
    y_c = o.transpose(0, 2, 1, 3).reshape(B, S, C_HEADS * C_VDIM) @ w_c_out

    g = jax.nn.sigmoid(gts).reshape(B, S, N_BRANCHES, D_MODEL)
    merged = g[..., 0, :] * y_a + g[..., 1, :] * y_b + g[..., 2, :] * y_c
    return merged @ w_out

def _expert_choice_ffn(x, norm_g, w_router, w_e_gate, w_e_up, w_e_down):
    B, S, D = x.shape
    xn = _rmsnorm(x, norm_g)
    aff = jax.nn.softmax((xn @ w_router).astype(jnp.float32), axis=-1)
    cap = CAPACITY_FACTOR * S // N_EXPERTS
    gate, idx = lax.top_k(jnp.swapaxes(aff, 1, 2), cap)
    bidx = jnp.arange(B)[:, None, None]
    xg = xn[bidx, idx]
    h = (jax.nn.silu(jnp.einsum('becd,edf->becf', xg, w_e_gate))
         * jnp.einsum('becd,edf->becf', xg, w_e_up))
    yo = jnp.einsum('becf,efd->becd', h, w_e_down) * gate[..., None].astype(xg.dtype)
    return jnp.zeros((B, S, D), yo.dtype).at[bidx, idx].add(yo)

def first_inputs(seed: int = 0) -> dict:
    key = jax.random.key(seed)
    ks = jax.random.split(key, 32)
    L, D, H = DEPTH, D_MODEL, A_HEADS
    f32 = jnp.float32

    def nrm(k, shape, scale):
        return jax.random.normal(k, shape, f32) * scale

    def gain(k, shape):
        return 1.0 + 0.02 * jax.random.normal(k, shape, f32)

    b_i = 0.1 * jax.random.normal(ks[3], (L, 2, H), f32)
    b_f = 3.0 + 3.0 * jax.random.uniform(ks[4], (L, 2, H), f32)
    b_if = jnp.stack([b_i[:, 0], b_f[:, 0], b_i[:, 1], b_f[:, 1]], axis=1).reshape(L, 4 * H)

    return {
        "x": jax.random.normal(ks[0], (BATCH, SEQ, D), f32),
        "mix_norm_g": gain(ks[1], (L, D)),
        "w_in": nrm(ks[2], (L, D, IN_WIDTH), D ** -0.5),
        "b_if": b_if,
        "a_norm_g": gain(ks[5], (L, H, A_HEAD_DIM)),
        "w_a_out": nrm(ks[6], (L, A_WIDTH, D), A_WIDTH ** -0.5),
        "conv_w": nrm(ks[7], (L, B_KERNEL, B_WIDTH), B_KERNEL ** -0.5),
        "conv_b": 0.02 * jax.random.normal(ks[8], (L, B_WIDTH), f32),
        "conv_ln_g": gain(ks[9], (L, B_WIDTH)),
        "conv_ln_b": 0.02 * jax.random.normal(ks[10], (L, B_WIDTH), f32),
        "w_b_out": nrm(ks[11], (L, B_WIDTH, D), B_WIDTH ** -0.5),
        "cq_norm_g": gain(ks[12], (L, C_Q_RANK)),
        "w_uq": nrm(ks[13], (L, C_Q_RANK, C_HEADS * C_QK_DIM), C_Q_RANK ** -0.5),
        "ckv_norm_g": gain(ks[14], (L, C_KV_RANK)),
        "w_ukv": nrm(ks[15], (L, C_KV_RANK, C_HEADS * (C_NOPE + C_VDIM)), C_KV_RANK ** -0.5),
        "q_norm_g": gain(ks[16], (L, C_QK_DIM)),
        "k_norm_g": gain(ks[17], (L, C_QK_DIM)),
        "w_c_out": nrm(ks[18], (L, C_HEADS * C_VDIM, D), (C_HEADS * C_VDIM) ** -0.5),
        "w_out": nrm(ks[19], (L, D, D), D ** -0.5),
        "ffn_norm_g": gain(ks[20], (L, D)),
        "w_router": nrm(ks[21], (L, D, N_EXPERTS), D ** -0.5),
        "w_e_gate": nrm(ks[22], (L, N_EXPERTS, D, EXPERT_FF), D ** -0.5),
        "w_e_up": nrm(ks[23], (L, N_EXPERTS, D, EXPERT_FF), D ** -0.5),
        "w_e_down": nrm(ks[24], (L, N_EXPERTS, EXPERT_FF, D), EXPERT_FF ** -0.5),
    }

def first_block(x, mix_norm_g, w_in, b_if, a_norm_g, w_a_out, conv_w, conv_b, conv_ln_g,
              conv_ln_b, w_b_out, cq_norm_g, w_uq, ckv_norm_g, w_ukv, q_norm_g, k_norm_g,
              w_c_out, w_out, ffn_norm_g, w_router, w_e_gate, w_e_up, w_e_down):
    S = x.shape[1]
    pos = jnp.arange(S, dtype=jnp.float32)
    inv_freq = ROPE_THETA ** (-jnp.arange(0, C_ROPE, 2, dtype=jnp.float32) / C_ROPE)
    ang = pos[:, None] * inv_freq[None, :]
    cos, sin = jnp.cos(ang), jnp.sin(ang)
    for l in range(DEPTH):
        x = x + _mixer(x, cos, sin, mix_norm_g[l], w_in[l], b_if[l], a_norm_g[l], w_a_out[l],
                       conv_w[l], conv_b[l], conv_ln_g[l], conv_ln_b[l], w_b_out[l],
                       cq_norm_g[l], w_uq[l], ckv_norm_g[l], w_ukv[l], q_norm_g[l],
                       k_norm_g[l], w_c_out[l], w_out[l])
        x = x + _expert_choice_ffn(x, ffn_norm_g[l], w_router[l], w_e_gate[l], w_e_up[l],
                                   w_e_down[l])
    return x


DEPTH_2 = 2

N_A = DEPTH_2 // 2
N_B = DEPTH_2 - N_A
CHUNK = 128
D_GATE = D_MODEL
N_GROUPS = 8
GROUP_DIM = D_GATE // N_GROUPS
N_HEADS = 8
HEAD_DIM = 64
V_DIM = 2 * HEAD_DIM
QK_WIDTH = N_HEADS * 2 * HEAD_DIM
V_WIDTH = N_HEADS * V_DIM
D_FF = int(math.ceil(8 * D_MODEL / 3 / 256) * 256)


def _alibi_slopes(n):
    return np.array([2.0 ** (-8.0 * (i + 1) / n) for i in range(n)], dtype=np.float32)

def _lambda_init(layer_idx):
    return 0.8 - 0.6 * math.exp(-0.3 * layer_idx)

def rms_norm(x, g):
    xf = x.astype(jnp.float32)
    y = xf * lax.rsqrt(jnp.mean(xf * xf, axis=-1, keepdims=True) + EPS)
    return (y * g.astype(jnp.float32)).astype(x.dtype)

def layer_norm_gain(x, g):
    xf = x.astype(jnp.float32)
    mu = jnp.mean(xf, axis=-1, keepdims=True)
    var = jnp.mean(jnp.square(xf - mu), axis=-1, keepdims=True)
    return ((xf - mu) * lax.rsqrt(var + EPS) * g.astype(jnp.float32)).astype(x.dtype)

def swiglu(h, w_gu, w_down):
    gu = h @ w_gu
    g, u = jnp.split(gu, 2, axis=-1)
    return (jax.nn.silu(g) * u) @ w_down

def gmlp_mixer(h, w_in, v_gain, w_sp, b_sp, w_out):
    B, S, _ = h.shape
    uv = jax.nn.gelu(h @ w_in)
    u, v = jnp.split(uv, 2, axis=-1)
    v = layer_norm_gain(v, v_gain)
    v = v.reshape(B, S // CHUNK, CHUNK, N_GROUPS, GROUP_DIM)
    causal = jnp.tril(jnp.ones((CHUNK, CHUNK), dtype=w_sp.dtype))
    z = jnp.einsum('gts,bcsgd->bctgd', w_sp * causal, v)
    z = z + b_sp.T[None, None, :, :, None]
    return (u * z.reshape(B, S, D_GATE)) @ w_out

def shared_kv(x, g, w_kv):
    B, S, _ = x.shape
    kv = rms_norm(x, g) @ w_kv
    k = kv[..., :QK_WIDTH].reshape(B, S, N_HEADS, 2, HEAD_DIM).transpose(0, 2, 3, 1, 4)
    v = kv[..., QK_WIDTH:].reshape(B, S, N_HEADS, V_DIM).transpose(0, 2, 1, 3)
    return k, v

def diff_attention(h, k, v, w_q, lam_vecs, subln, w_o, lambda_init):
    B, S, _ = h.shape
    n_blk = S // Q_BLOCK
    q = (h @ w_q).reshape(B, S, N_HEADS, 2, HEAD_DIM)
    q = q.reshape(B, n_blk, Q_BLOCK, N_HEADS, 2, HEAD_DIM).transpose(1, 0, 3, 4, 2, 5)
    lf = lam_vecs.astype(jnp.float32)
    lam = jnp.exp(jnp.sum(lf[0] * lf[1])) - jnp.exp(jnp.sum(lf[2] * lf[3])) + lambda_init
    slopes = jnp.asarray(_alibi_slopes(N_HEADS))
    scale = HEAD_DIM ** -0.5
    kf = k.astype(jnp.float32)
    vf = v.astype(jnp.float32)
    key_pos = jnp.arange(S, dtype=jnp.int32)

    def block(args):
        qb, bi = args
        q_pos = bi * Q_BLOCK + jnp.arange(Q_BLOCK, dtype=jnp.int32)
        dist = (q_pos[:, None] - key_pos[None, :]).astype(jnp.float32)
        bias = -slopes[:, None, None] * dist[None]
        s = jnp.einsum('bhitd,bhisd->bhits', qb.astype(jnp.float32), kf) * scale
        s = s + bias[None, :, None]
        s = jnp.where((dist >= 0)[None, None, None], s, -jnp.inf)
        p = jax.nn.softmax(s, axis=-1)
        a = p[:, :, 0] - lam * p[:, :, 1]
        return jnp.einsum('bhts,bhsd->bhtd', a, vf)

    o = lax.map(block, (q, jnp.arange(n_blk, dtype=jnp.int32)))
    o = o.transpose(1, 0, 3, 2, 4).reshape(B, S, N_HEADS, V_DIM).astype(h.dtype)
    o = rms_norm(o, subln) * (1.0 - lambda_init)
    return o.reshape(B, S, V_WIDTH) @ w_o

def second_inputs(seed: int = 0) -> dict:
    key = jax.random.key(seed)
    ks = jax.random.split(key, 20)
    f32 = jnp.float32

    def w(k, shape, fan_in):
        return jax.random.normal(k, shape, f32) * (fan_in ** -0.5)

    def gain(k, shape):
        return 1.0 + 0.05 * jax.random.normal(k, shape, f32)

    return {
        "x": jax.random.normal(ks[0], (BATCH, SEQ, D_MODEL), f32),
        "a_norm": gain(ks[1], (N_A, D_MODEL)),
        "a_w_in": w(ks[2], (N_A, D_MODEL, 2 * D_GATE), D_MODEL),
        "a_v_norm": gain(ks[3], (N_A, D_GATE)),
        "a_w_sp": w(ks[4], (N_A, N_GROUPS, CHUNK, CHUNK), CHUNK),
        "a_b_sp": 1.0 + 0.1 * jax.random.normal(ks[5], (N_A, N_GROUPS, CHUNK), f32),
        "a_w_out": w(ks[6], (N_A, D_GATE, D_MODEL), D_GATE),
        "ffn_norm": gain(ks[7], (DEPTH_2, D_MODEL)),
        "ffn_w_gu": w(ks[8], (DEPTH_2, D_MODEL, 2 * D_FF), D_MODEL),
        "ffn_w_down": w(ks[9], (DEPTH_2, D_FF, D_MODEL), D_FF),
        "kv_norm": gain(ks[10], (D_MODEL,)),
        "kv_w": w(ks[11], (D_MODEL, QK_WIDTH + V_WIDTH), D_MODEL),
        "b_norm": gain(ks[12], (N_B, D_MODEL)),
        "b_w_q": w(ks[13], (N_B, D_MODEL, QK_WIDTH), D_MODEL),
        "b_lambda": 0.1 * jax.random.normal(ks[14], (N_B, 4, HEAD_DIM), f32),
        "b_subln": gain(ks[15], (N_B, V_DIM)),
        "b_w_o": w(ks[16], (N_B, V_WIDTH, D_MODEL), V_WIDTH),
        "final_norm": gain(ks[17], (D_MODEL,)),
    }

def second_block(x, a_norm, a_w_in, a_v_norm, a_w_sp, a_b_sp, a_w_out, ffn_norm, ffn_w_gu, ffn_w_down,
              kv_norm, kv_w, b_norm, b_w_q, b_lambda, b_subln, b_w_o, final_norm):
    k = v = None
    for l in range(DEPTH_2):
        if l < N_A:
            x = x + gmlp_mixer(rms_norm(x, a_norm[l]), a_w_in[l], a_v_norm[l],
                               a_w_sp[l], a_b_sp[l], a_w_out[l])
        else:
            j = l - N_A
            if j == 0:
                k, v = shared_kv(x, kv_norm, kv_w)
            x = x + diff_attention(rms_norm(x, b_norm[j]), k, v, b_w_q[j], b_lambda[j],
                                   b_subln[j], b_w_o[j], _lambda_init(l))
        x = x + swiglu(rms_norm(x, ffn_norm[l]), ffn_w_gu[l], ffn_w_down[l])
    return rms_norm(x, final_norm)


def setup_inputs(seed=0):
    out = dict(first_inputs(seed))
    for name, value in second_inputs(seed + 1).items():
        if name != "x":
            out[name + "_2"] = value
    return out


def reference(
    x, mix_norm_g, w_in, b_if, a_norm_g, w_a_out, conv_w, conv_b, conv_ln_g, conv_ln_b, w_b_out,
    cq_norm_g, w_uq, ckv_norm_g, w_ukv, q_norm_g, k_norm_g, w_c_out, w_out, ffn_norm_g,
    w_router, w_e_gate, w_e_up, w_e_down, a_norm_2, a_w_in_2, a_v_norm_2, a_w_sp_2, a_b_sp_2,
    a_w_out_2, ffn_norm_2, ffn_w_gu_2, ffn_w_down_2, kv_norm_2, kv_w_2, b_norm_2, b_w_q_2,
    b_lambda_2, b_subln_2, b_w_o_2, final_norm_2,
):
    x = first_block(
        x, mix_norm_g, w_in, b_if, a_norm_g, w_a_out, conv_w, conv_b, conv_ln_g, conv_ln_b,
        w_b_out, cq_norm_g, w_uq, ckv_norm_g, w_ukv, q_norm_g, k_norm_g, w_c_out, w_out,
        ffn_norm_g, w_router, w_e_gate, w_e_up, w_e_down,
    )
    return second_block(
        x, a_norm_2, a_w_in_2, a_v_norm_2, a_w_sp_2, a_b_sp_2, a_w_out_2, ffn_norm_2,
        ffn_w_gu_2, ffn_w_down_2, kv_norm_2, kv_w_2, b_norm_2, b_w_q_2, b_lambda_2, b_subln_2,
        b_w_o_2, final_norm_2,
    )


_drawn_inputs = setup_inputs


def setup_inputs(seed=0):
    import zlib

    import numpy as np

    out = dict(_drawn_inputs(seed))
    spreads = {}
    factors = {'a_norm_g': 25.452,
     'conv_ln_g': 19.686,
     'conv_ln_b': 19.896,
     'cq_norm_g': 8.0,
     'ckv_norm_g': 8.0,
     'q_norm_g': 8.0,
     'k_norm_g': 5.775,
     'a_v_norm_2': 66.96,
     'b_norm_2': 11.618,
     'b_lambda_2': 6.084,
     'b_subln_2': 95.764,
     'conv_b': 3.9,
     'ffn_norm_g': 8.0,
     'a_b_sp_2': 23.208,
     'ffn_norm_2': 3.753,
     'a_norm_2': 6.074,
     'kv_norm_2': 2.894}
    for name, (base, spread) in spreads.items():
        noise = np.random.default_rng([zlib.crc32(name.encode()), seed]).standard_normal(out[name].shape)
        drawn = base * np.exp(spread * noise) if base else spread * noise
        out[name] = __import__('jax').numpy.asarray(drawn.astype(out[name].dtype))
    for name, factor in factors.items():
        out[name] = (out[name] * factor).astype(out[name].dtype)
    return out
```

```python
from contextlib import ExitStack

import concourse.bass as bass
from concourse import mybir

F32 = mybir.dt.float32
F32R = mybir.dt.float32r
ALU = mybir.AluOpType
ACT = mybir.ActivationFunctionType
AX = mybir.AxisListType

P = 128
SEQ = 256
T = SEQ // P
D = 1024
DC = D // P
EPS = 1e-6
BANK = 512

A_HEADS, A_DIM = 4, 128
A_W = A_HEADS * A_DIM
B_W, B_TAPS = 512, 31
B_PAD = B_TAPS // 2
C_HEADS, C_NOPE, C_ROPE, C_V = 8, 64, 32, 64
C_QK = C_NOPE + C_ROPE
C_QR, C_KVR = 384, 256
N_EXP, E_FF = 16, 1536
CAP = 2 * SEQ // N_EXP

Z_Q = 0
Z_K = Z_Q + A_W
Z_V = Z_K + A_W
Z_O = Z_V + A_W
Z_G = Z_O + A_W
Z_UA = Z_G + 4 * A_HEADS
Z_UG = Z_UA + B_W
Z_CQ = Z_UG + B_W
Z_CKV = Z_CQ + C_QR
Z_GTS = Z_CKV + C_KVR + C_ROPE

D_FF = 2816
LAMBDA_INIT = 0.8 - 0.6 * 0.7408182206817179
NEG = -1e30

G_GROUPS = 8
D_HEADS, D_DIM, D_V = 8, 64, 128

COLS = {}
_at = 0
for _name, _n in (("mix", DC), ("a_norm", A_HEADS), ("conv_w", B_TAPS * 4), ("conv_b", 4),
                  ("ln_g", 4), ("ln_b", 4), ("cq", C_QR // P), ("ckv", C_KVR // P), ("ffn", DC),
                  ("gmlp", DC), ("ffn0", DC), ("ffn1", DC), ("kv", DC), ("bq", DC),
                  ("b_sp", G_GROUPS), ("subln", 1)):
    COLS[_name] = (_at, _n)
    _at += _n
N_COLS = _at
ROWS = {"b_if": (0, 16), "q_g": (16, C_QK), "k_g": (16 + C_QK, C_QK)}
N_ROWS = 16 + 2 * C_QK
N_LAM = 4 * D_DIM
CONSTS = {}
_at = 0
for _name, _n in (("ident", P), ("upto", P), ("from", P), ("ones", P), ("causal", 2 * P),
                  ("anti", 2 * P), ("cos", T * 16), ("sin", T * 16), ("half", 8)):
    CONSTS[_name] = (_at, _n)
    _at += _n
N_CONSTS = _at


class Shared:
    pass


class Stream:

    def __init__(self, m, ctx, nc, name, slots, bufs):
        self.slots, self.bufs = slots, bufs
        self.ring = ctx.enter_context(nc.sbuf_tensor(f"{name}_ring", [P, slots, 2048], F32))
        self.hi = ctx.enter_context(nc.sbuf_tensor(f"{name}_whi", [P, bufs, 2048], F32R))
        self.lo = ctx.enter_context(nc.sbuf_tensor(f"{name}_wlo", [P, bufs, 2048], F32R))
        self.landed = [ctx.enter_context(nc.semaphore(f"{name}_landed{i}")) for i in range(slots)]
        self.hi_ready = ctx.enter_context(nc.semaphore(f"{name}_hi_ready"))
        self.lo_pool = ctx.enter_context(nc.semaphore(f"{name}_lo_pool"))
        self.lo_dve = ctx.enter_context(nc.semaphore(f"{name}_lo_dve"))
        self.used = ctx.enter_context(nc.semaphore(f"{name}_used"))
        self.pieces, self.arrive, self.lows = [], [], []
        self.n_pool = self.n_dve = 0
        self.slot_sum = [0] * slots

    def add(self, pieces, by_dve=False):
        g = len(self.pieces)
        self.pieces.append(pieces)
        self.slot_sum[g % self.slots] += 16 * len(pieces)
        self.arrive.append(self.slot_sum[g % self.slots])
        if by_dve:
            self.n_dve += 1
            self.lows.append((self.lo_dve, self.n_dve))
        else:
            self.n_pool += 1
            self.lows.append((self.lo_pool, self.n_pool))
        return g

    def size(self, g):
        return sum(nk * n for _, nk, n, _ in self.pieces[g])

    def load(self, sp, g):
        if g >= self.slots:
            sp.wait_ge(*self.lows[g - self.slots])
        for off, nk, n, src in self.pieces[g]:
            dst = self.ring[:, g % self.slots, off:off + nk * n].rearrange("p (k n) -> p k n", n=n)
            sp.dma_start(dst, src).then_inc(self.landed[g % self.slots], 16)

    def split_hi(self, act, g):
        n = self.size(g)
        act.wait_ge(self.landed[g % self.slots], self.arrive[g])
        if g >= self.bufs:
            act.wait_ge(self.used, g - self.bufs + 1)
        act.activation(self.hi[:, g % self.bufs, 0:n], self.ring[:, g % self.slots, 0:n],
                       ACT.Copy).then_inc(self.hi_ready, 1)

    def split_lo(self, eng, g):
        n = self.size(g)
        eng.wait_ge(self.hi_ready, g + 1)
        eng.tensor_tensor(self.lo[:, g % self.bufs, 0:n], self.ring[:, g % self.slots, 0:n],
                          self.hi[:, g % self.bufs, 0:n].bitcast(F32),
                          ALU.subtract).then_inc(self.lows[g][0], 1)

    def views(self, g, n):
        nk = self.size(g) // n
        return [x[:, g % self.bufs, 0:nk * n].rearrange("p (k n) -> p k n", n=n) for x in (self.hi, self.lo)]


def three_products(pe, out, hi, lo, whi, wlo, start, stop):
    pe.matmul(out, hi, whi, start=start, stop=False)
    pe.matmul(out, hi, wlo, start=False, stop=False)
    return pe.matmul(out, lo, whi, start=False, stop=stop)


def dense_granule(pe, st, g, outs, hi, lo, k0, n, first, last, turned=None):
    pe.wait_ge(*st.lows[g])
    whi, wlo = st.views(g, n)
    nk = whi.shape[1]
    for k in range(nk):
        if turned is not None:
            pe.wait_ge(turned[0], turned[1] + k0 + k + 1)
        for t in range(T):
            mm = three_products(pe, outs[t], hi[:, k0 + k, t * P:(t + 1) * P], lo[:, k0 + k, t * P:(t + 1) * P],
                                whi[:, k, :], wlo[:, k, :], first and k == 0, last and k == nk - 1)
    mm.then_inc(st.used, 1)



def norm_act(act, m, n):
    for t in range(T):
        act.activation(m.xs[:, t, :], m.x[:, t, :], ACT.Square,
                       accum_out=m.sumsq[:, t:t + 1]).then_inc(m.sumsq_ready, 1)


def norm_pool(pool, m, n):
    pool.wait_ge(m.sumsq_ready, T * (n + 1))
    pool.tensor_scalar(m.meansq[:, :], m.sumsq[:, :], 1.0 / D, EPS, ALU.mult, ALU.add).then_inc(m.meansq_ready, 1)
    pool.wait_ge(m.meansq_ready, n + 1)
    pool.tensor_tensor(m.rstd[:, :], m.meansq[:, :], m.half[:, 0:T], ALU.pow).then_inc(m.rstd_ready, 1)


def norm_dve(dve, m, n):
    dve.wait_ge(m.rstd_ready, n + 1)
    for t in range(T):
        dve.tensor_scalar(m.xs[:, t, :], m.x[:, t, :], m.rstd[:, t:t + 1], None,
                          ALU.mult).then_inc(m.xs_ready, 1)


def norm_pe(pe, m, n, banks):
    pe.wait_ge(m.xs_ready, T * (n + 1))
    for b in range(DC // 2):
        for cc in range(2):
            for t in range(T):
                c = 2 * b + cc
                mm = pe.transpose(m.ps[:, banks[b], cc * SEQ + t * P:cc * SEQ + (t + 1) * P],
                                  m.xs[:, t, c * P:(c + 1) * P], m.ident)
        mm.then_inc(m.xturn_ps, 1)


def turned_ps(m, banks, c):
    return m.ps[:, banks[c // 2], (c % 2) * SEQ:(c % 2 + 1) * SEQ]


def norm_hi_act(act, m, n, banks, hi, gain, ready, base):
    for c in range(DC):
        act.wait_ge(m.xturn_ps, (DC // 2) * n + c // 2 + 1)
        act.activation(hi[:, c, :], turned_ps(m, banks, c), ACT.Copy, scale=gain[:, c:c + 1]).then_inc(ready, 1)


def norm_lo_dve(dve, m, n, banks, hi, lo, gain, hi_ready, lo_ready, base):
    for c in range(DC):
        dve.wait_ge(hi_ready, base + 2 * (c // 2) + 2)
        dve.scalar_tensor_tensor(lo[:, c, :], turned_ps(m, banks, c), gain[:, c:c + 1],
                                 hi[:, c, :].bitcast(F32), ALU.mult, ALU.subtract).then_inc(lo_ready, 1)


def chunks(w, k0, nk, n0, n):
    return w[k0 * P:(k0 + nk) * P, n0:n0 + n].rearrange("(k p) n -> p k n", p=P)


def col(m, name):
    a, n = COLS[name]
    return m.cols[:, a:a + n]


def row(m, name):
    a, n = ROWS[name]
    return m.rows[:, a:a + n]


def const(m, name):
    a, n = CONSTS[name]
    return m.consts[:, a:a + n]



def mixer(nc, m, I):
    with ExitStack() as ctx:
        def sb(name, shape, dt=F32):
            return ctx.enter_context(nc.sbuf_tensor("sb_" + name, shape, dt))

        def sem(name):
            return ctx.enter_context(nc.semaphore(name))

        st = Stream(m, ctx, nc, "mix", 3, 2)
        ps = m.ps

        blocks = {}

        def dense(name, w, k_chunks, per, n0, n):
            blocks[name] = [(st.add([(0, per, n, chunks(w, k, per, n0, n))]), k, per, n)
                            for k in range(0, k_chunks, per)]

        w_in = I["w_in"][0]
        dense("g", w_in, DC, 8, Z_G, 4 * A_HEADS)
        dense("cq", w_in, DC, 4, Z_CQ, C_QR)
        dense("ckv", w_in, DC, 4, Z_CKV, C_KVR + C_ROPE)
        dense("ug", w_in, DC, 4, Z_UG, B_W)
        dense("o", w_in, DC, 4, Z_O, A_W)
        dense("ua", w_in, DC, 4, Z_UA, B_W)
        dense("q", w_in, DC, 4, Z_Q, A_W)
        dense("k", w_in, DC, 4, Z_K, A_W)
        for j in range(2):
            dense(f"uq{j}", I["w_uq"][0], C_QR // P, 3, j * 384, 384)
        for j in range(2):
            dense(f"ukv{j}", I["w_ukv"][0], C_KVR // P, 2, j * 512, 512)
        dense("v", w_in, DC, 4, Z_V, A_W)
        for j in range(6):
            dense(f"gt{j}", w_in, DC, 4, Z_GTS + j * 512, 512)
        for h in range(2):
            for br, w in (("a", I["w_a_out"][0]), ("b", I["w_b_out"][0]), ("c", I["w_c_out"][0])):
                dense(f"y{br}{h}", w, 4, 4, h * 512, 512)
        for h in range(2):
            dense(f"out{h}", I["w_out"][0], DC, 4, h * 512, 512)
        order = list(blocks)
        n_gran = len(st.pieces)

        m.sel = sb("sel", [8, 8, P])
        xhi, xlo = sb("xhi", [P, DC, SEQ], F32R), sb("xlo", [P, DC, SEQ], F32R)
        gates = sb("gates", [P, T, 2, 2, A_HEADS])
        fabs = sb("fabs", [P, T * 2 * A_HEADS])
        fexp = sb("fexp", [P, T * 2 * A_HEADS])
        logf = sb("logf", [P, T, 2, A_HEADS])
        fcum = sb("fcum", [P, A_HEADS, 2, T])
        ir = sb("ir", [P, T, 2, A_HEADS])
        irow = sb("irow", [2 * A_HEADS, SEQ])
        merged = m.xs
        flat = m.xs[:, :, :].rearrange("p t d -> p (t d)")
        cq = flat[:, 0:T * C_QR].rearrange("p (t n) -> p t n", t=T)
        ckv = flat[:, T * C_QR:T * (C_QR + C_KVR + C_ROPE)].rearrange("p (t n) -> p t n", t=T)
        cstat, crstd = sb("cstat", [P, 4]), sb("crstd", [P, 4])
        csum = sb("csum", [P, 4])
        chi, clo = sb("chi", [P, 5, SEQ], F32R), sb("clo", [P, 5, SEQ], F32R)
        u = sb("u", [P, T, B_W])
        o_gate = sb("o_gate", [P, T, A_W])
        qtok, ktok, vtok = sb("qtok", [P, T, A_W]), sb("ktok", [P, T, A_W]), sb("vtok", [P, T, A_W])
        upad = sb("upad", [P, 4, SEQ + 2 * B_PAD])
        conv = sb("conv", [P, 4, SEQ])
        bst, bmv, brstd = sb("bst", [P, T, 6]), sb("bmv", [P, T, 2]), sb("brstd", [P, T])
        bvar = sb("bvar", [P, T])
        gt = sb("gt", [P, T, 3, D])
        qh, kv = sb("qh", [P, T, C_HEADS, C_QK]), sb("kv", [P, T, C_HEADS, C_NOPE + C_V])
        kh = sb("kh", [P, T, C_HEADS, C_QK])
        hss, hrs = sb("hss", [P, 2, T, C_HEADS]), sb("hrs", [P, 2, T, C_HEADS])
        hms, krss = sb("hms", [P, 2, T, C_HEADS]), sb("krss", [P, T])
        yhi = [sb("yahi", [P, 4, SEQ], F32R), xhi, chi]
        ylo = [sb("yalo", [P, 4, SEQ], F32R), xlo, clo]
        qkT = sb("qkT", [P, 2, SEQ])
        decay = sb("decay", [P, 6 * P])
        smat = decay
        amat, amatT = sb("amat", [P, T, SEQ]), sb("amatT", [P, T, SEQ])
        mx, den, mstat = sb("mx", [P, 4]), sb("den", [P, 4]), sb("mstat", [P, 4, 4])
        hst = sb("hst", [P, 3, T])
        hn = sb("hn", [P, T, A_DIM])
        cT = sb("cT", [C_QK, 2, SEQ])
        pr, prT = sb("pr", [P, T, SEQ]), sb("prT", [P, T, SEQ])
        cmx, csm = sb("cmx", [P, 2, T]), sb("csm", [P, 2, T])
        ytmp = u
        rope = u[:, :, :].rearrange("p t (i h f) -> p t i h f", i=4, f=16)
        silu = conv
        xscr = smat
        hscr = hn
        gflat = gt[:, :, :, :].rearrange("p t b d -> p (t b d)")
        qsq = gflat[:, 0:T * C_HEADS * C_QK].rearrange("p (t h d) -> p t h d", t=T, h=C_HEADS)
        xsq = gflat[:, 2048:2048 + T * C_HEADS * C_NOPE].rearrange("p (t h d) -> p t h d", t=T, h=C_HEADS)
        parts = [(0, P), (P, 2 * P), (3 * P, 2 * P), (5 * P, P)]

        x_in, const_in = sem("x_in"), sem("const_in")
        xhi_ready, xlo_ready = sem("xhi_ready"), sem("xlo_ready")
        dve_step, act_step, pool_step = sem("mix_dve_step"), sem("mix_act_step"), sem("mix_pool_step")
        z_act, z_dve = sem("z_act"), sem("z_dve")
        gates_ready, fabs_ready, fexp_ready, logl_ready = (sem(s) for s in ("gates_ready", "fabs_ready", "fexp_ready", "logl_ready"))
        logf_ready, fcum_ps, ir_ready, irow_ps, irow_ready = (
            sem(s) for s in ("logf_ready", "fcum_ps", "ir_ready", "irow_ps", "irow_ready"))
        csum_ready, crstd_ready, cnorm_ready, cturn_ps, chi_ready, clo_ready = (
            sem(s) for s in ("csum_ready", "crstd_ready", "cnorm_ready", "cturn_ps", "chi_ready", "clo_ready"))
        pad_ready, u_ready, uturn_ps, upad_ready, conv_ready = (
            sem(s) for s in ("pad_ready", "u_ready", "uturn_ps", "upad_ready", "conv_ready"))
        ctok_ps, bvar_ready, brstd_ready, bn_ready, bturn_ps, silu_ready, ybhi, yblo = (
            sem(s) for s in ("ctok_ps", "bvar_ready", "brstd_ready", "bn_ready", "bturn_ps", "silu_ready", "ybhi", "yblo"))
        sq_ready, hss_ready, hrs_ready, ckh_ready = (sem(s) for s in ("sq_ready", "hss_ready", "hrs_ready", "ckh_ready"))
        qk_ps, qkT_ready, ib_ps, mneg_ready, decay_ready, emt_ready, score_ps, amat_ready, amT_ps, amT_ready, h_ps, hsum_ready, hrstd_ready, hn_ready, hturn_ps, yahi, yalo = (
            sem(s) for s in ("qk_ps", "qkT_ready", "ib_ps", "mneg_ready", "decay_ready", "emt_ready", "score_ps",
                             "amat_ready", "amT_ps", "amT_ready", "h_ps", "hsum_ready", "hrstd_ready", "hn_ready",
                             "hturn_ps", "yahi", "yalo"))
        cqk_ps, cT_ready, cs_ps, cmx_ready, cexp_ready, pr_ready, prT_ps, prT_ready, co_ps, ychi, yclo = (
            sem(s) for s in ("cqk_ps", "cT_ready", "cs_ps", "cmx_ready", "cexp_ready", "pr_ready", "prT_ps",
                             "prT_ready", "co_ps", "ychi", "yclo"))
        y_read, merged_ready, mturn_ps, x1_ready = (sem(s) for s in ("y_read", "merged_ready", "mturn_ps", "x1_ready"))
        m.mixer_sems = range(st.landed[0].num, x1_ready.num + 1)

        steps = [("norm", 0)]

        def gran(name):
            for i in range(len(blocks[name])):
                steps.append(("gran", (name, i)))
            steps.append(("evac", name))

        gran("g"); steps.append(("gate1", 0))
        gran("cq"); steps.append(("gate2", 0))
        gran("ckv"); steps.append(("gate3", 0)); steps.append(("cnorm", 0))
        gran("ug"); steps.append(("cturn", 0))
        gran("o"); gran("ua"); steps.append(("uturn", 0))
        gran("q"); gran("k")
        gran("uq0"); gran("uq1"); gran("ukv0"); gran("ukv1")
        side = []
        for h in range(A_HEADS):
            side += [("m1", h), ("c1", 2 * h), ("m2", h), ("c2", 2 * h), ("m3", h), ("c3", 2 * h), ("m4", h), ("c4", 2 * h),
                     ("m5", h), ("c1", 2 * h + 1), ("c2", 2 * h + 1), ("c3", 2 * h + 1), ("c4", 2 * h + 1)]
        steps.append(("conv", 0)); steps.append(("chead", 0)); steps.append(("conv", 1))
        gran("v")
        steps.append(("conv", 2)); steps.append(("conv", 3))
        dense_part = []
        for j in range(6):
            dense_part += [("gran", (f"gt{j}", 0)), ("gran", (f"gt{j}", 1)), ("evac", f"gt{j}")]
        per = -(-len(side) // 12)
        while side or dense_part:
            steps += side[:per]
            del side[:per]
            while dense_part:
                steps.append(dense_part.pop(0))
                if steps[-1][0] == "gran" and not (dense_part and dense_part[0][0] == "evac"):
                    break
                if steps[-1][0] == "evac":
                    break
        for s in ("b1", "b2", "b3", "b4"):
            steps.append((s, 0))
        for h in range(2):
            for br in "abc":
                steps.append(("gran", (f"y{br}{h}", 0)))
                steps.append(("evac", f"y{br}{h}"))
        steps.append(("mturn", 0))
        gran("out0"); gran("out1")

        parity = {name: i % 2 for i, name in enumerate(order)}

        def zbanks(name):
            return [2 * parity[name] + t for t in range(T)]

        def last_gran(name):
            return blocks[name][-1][0]

        by_dve = {"g"} | {f"y{b}{h}" for b in "abc" for h in range(2)} | {"out0", "out1"}
        evac_at, na, nd = {}, 0, 0
        for name in order:
            if name in by_dve:
                nd += 1
                evac_at[name] = (z_dve, nd)
            elif name == "ua":
                evac_at[name] = (u_ready, T)
            else:
                na += 1
                evac_at[name] = (z_act, na)

        SA, SB, SC, SD = 4, 5, 6, 7
        NB4 = [0, 1, 2, 3]
        lookahead = 2

        def cslot(c):
            return ps[:, (SA, SA, SC, SC, SD)[c], (c % 2) * SEQ:(c % 2 + 1) * SEQ]

        gran_steps = [blocks[v[0]][v[1]][0] for s, v in steps if s == "gran"]
        assert gran_steps == list(range(n_gran))

        def sq(t):
            return slice(t * P, (t + 1) * P)

        block = ctx.enter_context(nc.Block())

        @block.sync
        def _(sp):
            sp.dma_start(m.x[:, :, :], I["x"][0].rearrange("(t p) d -> p t d", p=P)).then_inc(x_in, 16)
            for g in range(n_gran):
                st.load(sp, g)

        @block.scalar
        def _(act):
            act.dma_start(m.consts[:, :], I["c_consts"]).then_inc(const_in, 16)
            act.dma_start(m.cols[:, :], I["v_cols"]).then_inc(const_in, 16)
            act.dma_start(m.rows[:, :], I["v_rows"]).then_inc(const_in, 16)
            act.dma_start(m.sel[:, :, :], I["c_sel"]).then_inc(const_in, 16)
            act.wait_ge(x_in, 16)
            act_n = [0]
            norm_act(act, m, 0)
            act.wait_ge(const_in, 64)
            for g in range(min(lookahead, n_gran)):
                st.split_hi(act, g)
            norm_hi_act(act, m, 0, NB4, xhi, col(m, "mix"), xhi_ready, 0)

            for what, v in steps:
                if what == "gran":
                    g = blocks[v[0]][v[1]][0]
                    if g + lookahead < n_gran:
                        st.split_hi(act, g + lookahead)
                elif what == "evac" and v not in by_dve and v != "ua":
                    b = zbanks(v)
                    n = blocks[v][0][3]
                    act.wait_ge(st.used, last_gran(v) + 1)
                    if v in ("cq", "ckv"):
                        i = 0 if v == "cq" else 2
                        w = C_QR if v == "cq" else C_KVR
                        dst = cq if v == "cq" else ckv
                        for t in range(T):
                            act.activation(xscr[:, 0:w], ps[:, b[t], 0:w], ACT.Square,
                                           accum_out=csum[:, i + t:i + t + 1]).then_inc(act_step, 1)
                            act_n[0] += 1
                            act.wait_ge(act_step, act_n[0])
                        for t in range(T):
                            ins = act.activation(dst[:, t, :], ps[:, b[t], 0:n], ACT.Copy)
                            ins.then_inc(csum_ready if t == 0 else z_act, 1)
                    else:
                        if v == "q":
                            dsts, f, s = [qtok[:, t, :] for t in range(T)], ACT.Copy, float(A_DIM) ** -0.5
                        elif v == "k":
                            dsts, f, s = [ktok[:, t, :] for t in range(T)], ACT.Copy, 1.0
                        elif v == "v":
                            dsts, f, s = [vtok[:, t, :] for t in range(T)], ACT.Copy, 1.0
                        elif v == "ug":
                            dsts, f, s = [u[:, t, :] for t in range(T)], ACT.Sigmoid, 1.0
                        elif v == "o":
                            dsts, f, s = [o_gate[:, t, :] for t in range(T)], ACT.Sigmoid, 1.0
                        elif v[:2] == "uq":
                            j = int(v[2:])
                            dsts = [qh[:, t, 4 * j:4 * j + 4, :].rearrange("p h d -> p (h d)") for t in range(T)]
                            f, s = ACT.Copy, 1.0
                        elif v[:3] == "ukv":
                            j = int(v[3:])
                            dsts = [kv[:, t, 4 * j:4 * j + 4, :].rearrange("p h d -> p (h d)") for t in range(T)]
                            f, s = ACT.Copy, 1.0
                        else:
                            j = int(v[2:])
                            act.wait_ge(hss_ready, 1)
                            dsts = [gt[:, t, j // 2, (j % 2) * BANK:(j % 2 + 1) * BANK] for t in range(T)]
                            f, s = ACT.Tanh, 0.5
                        for t in range(T):
                            ins = act.activation(dsts[t], ps[:, b[t], 0:n], f, scale=s)
                        ins.then_inc(z_act, 1)
                elif what == "gate1":
                    act.wait_ge(fabs_ready, 1)
                    act.activation(fexp[:, :], fabs[:, :], ACT.Exp, scale=-1.0).then_inc(fexp_ready, 1)
                    act.wait_ge(fexp_ready, 1)
                    act.activation(fabs[:, :], fexp[:, :], ACT.Ln, bias=1.0).then_inc(logl_ready, 1)
                elif what == "cturn":
                    for c in range(5):
                        act.wait_ge(cturn_ps, 1)
                        gain = (col(m, "cq")[:, c:c + 1] if c < 3 else col(m, "ckv")[:, c - 3:c - 2])
                        act.activation(chi[:, c, :], cslot(c), ACT.Copy, scale=gain).then_inc(chi_ready, 1)
                elif what == "uturn":
                    act.wait_ge(pad_ready, 1)
                    act.wait_ge(uturn_ps, 1)
                    for c in range(4):
                        act.activation(upad[:, c, B_PAD:B_PAD + SEQ],
                                       ps[:, (SC, SD)[c // 2], (c % 2) * SEQ:(c % 2 + 1) * SEQ],
                                       ACT.Copy).then_inc(upad_ready, 1)
                elif what == "m1":
                    act.wait_ge(qk_ps, v + 1)
                    act.activation(qkT[:, :, :].rearrange("p a s -> p (a s)"), ps[:, SA, :], ACT.Copy).then_inc(qkT_ready, 1)
                    act.wait_ge(mneg_ready, v + 1)
                    for j, (a, n) in enumerate(parts):
                        ins = act.activation(decay[:, a:a + n], decay[:, a:a + n], ACT.Exp, bias=mstat[:, 0, j:j + 1])
                    ins.then_inc(decay_ready, 1)
                    act.activation(mstat[:, 2, :], mstat[:, 1, :], ACT.Exp, scale=-1.0).then_inc(emt_ready, 1)
                elif what == "m3":
                    act.wait_ge(amT_ps, v + 1)
                    act.activation(amatT[:, :, :].rearrange("p a s -> p (a s)"), ps[:, SB, :], ACT.Copy).then_inc(amT_ready, 1)
                elif what == "m4":
                    act.wait_ge(h_ps, v + 1)
                    for t in range(T):
                        act.activation(hscr[:, t, :], ps[:, SA, sq(t)], ACT.Square,
                                       accum_out=hst[:, 0, t:t + 1]).then_inc(hsum_ready, 1)
                elif what == "m5":
                    act.wait_ge(hturn_ps, v + 1)
                    act.activation(yhi[0][:, v, :], ps[:, SA, SEQ:2 * SEQ], ACT.Copy,
                                   scale=col(m, "a_norm")[:, v:v + 1]).then_inc(yahi, 1)
                elif what == "c1":
                    act.wait_ge(cqk_ps, v + 1)
                    act.activation(cT[:, :, :].rearrange("p a s -> p (a s)"), ps[0:C_QK, SC, :], ACT.Copy).then_inc(cT_ready, 1)
                elif what == "c2":
                    act.wait_ge(cmx_ready, v + 1)
                    for t in range(T):
                        ins = act.activation(pr[:, t, :], ps[:, SD, t * SEQ:(t + 1) * SEQ], ACT.Exp,
                                             bias=cmx[:, 1, t:t + 1], scale=float(C_QK) ** -0.5,
                                             accum_out=csm[:, 0, t:t + 1])
                    ins.then_inc(cexp_ready, 1)
                elif what == "c3":
                    act.wait_ge(prT_ps, v + 1)
                    act.activation(prT[:, :, :].rearrange("p a s -> p (a s)"), ps[:, SC, :], ACT.Copy).then_inc(prT_ready, 1)
                elif what == "c4":
                    r = slice(64 * (v % 2), 64 * (v % 2) + 64)
                    act.wait_ge(co_ps, v + 1)
                    act.activation(yhi[2][r, v // 2, :], ps[r, SD, 0:SEQ], ACT.Copy).then_inc(ychi, 1)
                elif what == "b4":
                    act.wait_ge(bturn_ps, 1)
                    act.wait_ge(ctok_ps, 1)
                    for c in range(4):
                        act.activation(silu[:, c, :], ps[:, (SC, SD)[c // 2], (c % 2) * SEQ:(c % 2 + 1) * SEQ], ACT.Silu,
                                       bias=col(m, "ln_b")[:, c:c + 1],
                                       scale=col(m, "ln_g")[:, c:c + 1]).then_inc(silu_ready, 1)
                    for c in range(4):
                        act.wait_ge(silu_ready, c + 1)
                        act.activation(yhi[1][:, c, :], silu[:, c, :], ACT.Copy).then_inc(ybhi, 1)
                elif what == "mturn":
                    for c in range(DC):
                        act.wait_ge(mturn_ps, c // 2 + 1)
                        act.activation(xhi[:, c, :], turned_ps(m, [SA, SB, SC, SD], c), ACT.Copy,
                                       scale=0.5).then_inc(xhi_ready, 1)

        @block.tensor
        def _(pe):
            pe.wait_ge(const_in, 64)
            norm_pe(pe, m, 0, NB4)
            for what, v in steps:
                if what == "gran":
                    name, i = v
                    g, k0, nk, n = blocks[name][i]
                    b = zbanks(name)
                    if i == 0:
                        at = order.index(name)
                        if at >= 2:
                            pe.wait_ge(*evac_at[order[at - 2]])
                        if at < 2:
                            pe.wait_ge(xlo_ready, DC)
                    hi, lo, kk = xhi, xlo, k0
                    if name[:2] == "uq":
                        hi, lo = chi, clo
                        pe.wait_ge(clo_ready, 3)
                    elif name[:3] == "ukv":
                        hi, lo, kk = chi, clo, 3
                        pe.wait_ge(clo_ready, 5)
                    elif name[0] == "y":
                        br = "abc".index(name[1])
                        hi, lo = yhi[br], ylo[br]
                        pe.wait_ge((yalo, yblo, yclo)[br], (A_HEADS, 4, C_HEADS)[br])
                    turned = {"g": (xlo_ready, 0), "out0": (xlo_ready, DC)}.get(name)
                    dense_granule(pe, st, g, [ps[:, b[t], 0:n] for t in range(T)], hi, lo, kk, n,
                                  i == 0, i == len(blocks[name]) - 1, turned)
                elif what == "gate2":
                    pe.wait_ge(logf_ready, 1)
                    for d, tri in ((0, const(m, "upto")), (1, const(m, "from"))):
                        for t in range(T):
                            out = ps[:, SB, (d * T + t) * A_HEADS:(d * T + t + 1) * A_HEADS]
                            other = (t == 1) if d == 0 else (t == 0)
                            mm = pe.matmul(out, tri, logf[:, t, d, :], start=True, stop=not other)
                            if other:
                                mm = pe.matmul(out, const(m, "ones"), logf[:, 1 - t, d, :], start=False, stop=True)
                    mm.then_inc(fcum_ps, 1)
                elif what == "gate3":
                    pe.wait_ge(ir_ready, 1)
                    for t in range(T):
                        mm = pe.transpose(ps[0:2 * A_HEADS, SB, SEQ + t * P:SEQ + (t + 1) * P],
                                          ir[:, t, :, :].rearrange("p d h -> p (d h)"), m.ident)
                    mm.then_inc(irow_ps, 1)
                elif what == "cturn":
                    pe.wait_ge(cnorm_ready, 2 * T)
                    for c in range(5):
                        for t in range(T):
                            src = cq[:, t, c * P:(c + 1) * P] if c < 3 else ckv[:, t, (c - 3) * P:(c - 2) * P]
                            mm = pe.transpose(cslot(c)[:, t * P:(t + 1) * P], src, m.ident)
                    mm.then_inc(cturn_ps, 1)
                elif what == "uturn":
                    pe.wait_ge(u_ready, T)
                    pe.wait_ge(clo_ready, 5)
                    for c in range(4):
                        for t in range(T):
                            mm = pe.transpose(ps[:, (SC, SD)[c // 2], (c % 2) * SEQ + t * P:(c % 2) * SEQ + (t + 1) * P],
                                              u[:, t, c * P:(c + 1) * P], m.ident)
                    mm.then_inc(uturn_ps, 1)
                elif what == "m1":
                    if v == 0:
                        pe.wait_ge(*evac_at["q"])
                        pe.wait_ge(*evac_at["k"])
                        pe.wait_ge(irow_ready, 1)
                        pe.wait_ge(clo_ready, 5)
                    else:
                        pe.wait_ge(yalo, v)
                    for a, src in ((0, qtok), (1, ktok)):
                        for t in range(T):
                            mm = pe.transpose(ps[:, SA, a * SEQ + t * P:a * SEQ + (t + 1) * P],
                                              src[:, t, v * P:(v + 1) * P], m.ident)
                    mm.then_inc(qk_ps, 1)
                    if v >= 1:
                        pe.wait_ge(amT_ready, v)
                    for d in range(2):
                        mm = pe.matmul(ps[:, SB, d * SEQ:(d + 1) * SEQ], m.sel[:, d * A_HEADS + v, :], irow[:, :],
                                       start=True, stop=True)
                    mm.then_inc(ib_ps, 1)
                elif what == "m2":
                    pe.wait_ge(qkT_ready, v + 1)
                    for t in range(T):
                        mm = pe.matmul(ps[:, SA, t * SEQ:(t + 1) * SEQ], qkT[:, 0, sq(t)], qkT[:, 1, :],
                                       start=True, stop=True)
                    mm.then_inc(score_ps, 1)
                elif what == "m3":
                    pe.wait_ge(amat_ready, v + 1)
                    for s in range(T):
                        for t in range(T):
                            mm = pe.transpose(ps[:, SB, s * SEQ + t * P:s * SEQ + (t + 1) * P], amat[:, t, sq(s)], m.ident)
                    mm.then_inc(amT_ps, 1)
                elif what == "m4":
                    if v == 0:
                        pe.wait_ge(*evac_at["v"])
                    pe.wait_ge(amT_ready, v + 1)
                    for t in range(T):
                        for s in range(T):
                            mm = pe.matmul(ps[:, SA, sq(t)], amatT[:, s, sq(t)], vtok[:, s, v * P:(v + 1) * P],
                                           start=s == 0, stop=s == T - 1)
                    mm.then_inc(h_ps, 1)
                elif what == "m5":
                    pe.wait_ge(hn_ready, T * (v + 1))
                    for t in range(T):
                        mm = pe.transpose(ps[:, SA, SEQ + t * P:SEQ + (t + 1) * P], hn[:, t, :], m.ident)
                    mm.then_inc(hturn_ps, 1)
                elif what == "c1":
                    if v == 0:
                        pe.wait_ge(ckh_ready, 2)
                        pe.wait_ge(upad_ready, 4)
                    else:
                        pe.wait_ge(prT_ready, v)
                    for a, src in ((0, qh), (1, kh)):
                        for t in range(T):
                            mm = pe.transpose(ps[0:C_QK, SC, a * SEQ + t * P:a * SEQ + (t + 1) * P], src[:, t, v, :], m.ident)
                    mm.then_inc(cqk_ps, 1)
                elif what == "c2":
                    pe.wait_ge(cT_ready, v + 1)
                    if v >= 1:
                        pe.wait_ge(yclo, v)
                    for t in range(T):
                        mm = pe.matmul(ps[:, SD, t * SEQ:(t + 1) * SEQ], cT[:, 0, sq(t)], cT[:, 1, :], start=True, stop=True)
                    mm.then_inc(cs_ps, 1)
                elif what == "c3":
                    pe.wait_ge(pr_ready, v + 1)
                    for s in range(T):
                        for t in range(T):
                            mm = pe.transpose(ps[:, SC, s * SEQ + t * P:s * SEQ + (t + 1) * P], pr[:, t, sq(s)], m.ident)
                    mm.then_inc(prT_ps, 1)
                elif what == "c4":
                    pe.wait_ge(prT_ready, v + 1)
                    r = slice(64 * (v % 2), 64 * (v % 2) + 64)
                    for s in range(T):
                        mm = pe.matmul(ps[r, SD, 0:SEQ], kv[:, s, v, C_NOPE:], prT[:, s, :], start=s == 0, stop=s == T - 1)
                    mm.then_inc(co_ps, 1)
                elif what == "b1":
                    pe.wait_ge(conv_ready, 4)
                    pe.wait_ge(yclo, C_HEADS)
                    for t in range(T):
                        for c in range(4):
                            mm = pe.transpose(ps[:, (SC, SD)[t], c * P:(c + 1) * P], conv[:, c, sq(t)], m.ident)
                    mm.then_inc(ctok_ps, 1)
                elif what == "b4":
                    pe.wait_ge(bn_ready, T)
                    for c in range(4):
                        for t in range(T):
                            mm = pe.transpose(ps[:, (SC, SD)[c // 2], (c % 2) * SEQ + t * P:(c % 2) * SEQ + (t + 1) * P],
                                              u[:, t, c * P:(c + 1) * P], m.ident)
                    mm.then_inc(bturn_ps, 1)
                elif what == "mturn":
                    pe.wait_ge(merged_ready, 2)
                    pe.wait_ge(yalo, A_HEADS)
                    pe.wait_ge(amT_ready, A_HEADS)
                    pe.wait_ge(silu_ready, 4)
                    banks = [SA, SB, SC, SD]
                    for b in range(4):
                        for cc in range(2):
                            for t in range(T):
                                c = 2 * b + cc
                                mm = pe.transpose(ps[:, banks[b], cc * SEQ + t * P:cc * SEQ + (t + 1) * P],
                                                  merged[:, t, c * P:(c + 1) * P], m.ident)
                        mm.then_inc(mturn_ps, 1)

        @block.vector
        def _(dve):
            n_step = [0]

            def link(ins):
                n_step[0] += 1
                ins.then_inc(dve_step, 1)
                dve.wait_ge(dve_step, n_step[0])

            dve.memset(upad[:, :, 0:B_PAD], 0.0)
            dve.memset(upad[:, :, B_PAD + SEQ:], 0.0).then_inc(pad_ready, 1)
            dve.wait_ge(x_in, 16)
            norm_dve(dve, m, 0)
            dve.wait_ge(const_in, 64)
            norm_lo_dve(dve, m, 0, NB4, xhi, xlo, col(m, "mix"), xhi_ready, xlo_ready, 0)

            for what, v in steps:
                if what == "evac" and (v in by_dve or v == "ua"):
                    b = zbanks(v)
                    dve.wait_ge(st.used, last_gran(v) + 1)
                    if v == "g":
                        for t in range(T):
                            ins = dve.tensor_tensor(gates[:, t, :, :, :].rearrange("p d i h -> p (d i h)"),
                                                    ps[:, b[t], 0:16], row(m, "b_if"), ALU.add)
                            ins.then_inc(gates_ready if t == 0 else z_dve, 1)
                    elif v == "ua":
                        dve.wait_ge(*evac_at["ug"])
                        for t in range(T):
                            ins = dve.tensor_tensor(u[:, t, :], ps[:, b[t], :], u[:, t, :], ALU.mult)
                            ins.then_inc(u_ready, 1)
                    elif v[0] == "y":
                        br, h = "abc".index(v[1]), int(v[2])
                        for t in range(T):
                            dst = merged[:, t, h * BANK:(h + 1) * BANK]
                            g_t = gt[:, t, br, h * BANK:(h + 1) * BANK]
                            if br == 0:
                                dve.wait_ge(*evac_at["gt5"])
                                ins = dve.scalar_tensor_tensor(dst, g_t, 1.0, ps[:, b[t], :], ALU.add, ALU.mult)
                                if t == 0:
                                    link(ins)
                                else:
                                    ins.then_inc(z_dve, 1)
                                    dve.wait_ge(*evac_at[v])
                            else:
                                ins = dve.scalar_tensor_tensor(ytmp[:, t, :], g_t, 1.0, ps[:, b[t], :], ALU.add, ALU.mult)
                                if t == 0:
                                    link(ins)
                                else:
                                    ins.then_inc(z_dve, 1)
                                    dve.wait_ge(*evac_at[v])
                                ins = dve.tensor_tensor(dst, dst, ytmp[:, t, :], ALU.add)
                                if br == 2 and t == T - 1:
                                    ins.then_inc(merged_ready, 1)
                                else:
                                    link(ins)
                    else:
                        h = int(v[3])
                        for t in range(T):
                            ins = dve.tensor_tensor(m.x[:, t, h * BANK:(h + 1) * BANK], ps[:, b[t], :],
                                                    m.x[:, t, h * BANK:(h + 1) * BANK], ALU.add)
                        ins.then_inc(z_dve, 1)
                elif what == "gate1":
                    dve.wait_ge(*evac_at["g"])
                    dve.wait_ge(gates_ready, 1)
                    f = gates[:, :, :, 1, :].rearrange("p t d h -> p (t d) h")
                    l3 = fabs[:, :].rearrange("p (a h) -> p a h", h=A_HEADS)
                    dve.scalar_tensor_tensor(l3, f, -1.0, f, ALU.mult, ALU.max).then_inc(fabs_ready, 1)
                    dve.wait_ge(logl_ready, 1)
                    dve.scalar_tensor_tensor(logf[:, :, :, :].rearrange("p t d h -> p (t d) h"), f, 0.0, l3,
                                             ALU.min, ALU.subtract).then_inc(logf_ready, 1)
                elif what == "gate2":
                    dve.wait_ge(fcum_ps, 1)
                    fps = ps[:, SB, 0:2 * T * A_HEADS].rearrange("p (d t h) -> p d t h", d=2, t=T)
                    link(dve.tensor_copy(fcum[:, :, :, :].rearrange("p h d t -> p d t h"), fps))
                    for d in range(2):
                        ins = dve.tensor_tensor(ir[:, :, d, :], gates[:, :, d, 0, :], fps[:, d, :, :], ALU.subtract)
                        if d == 0:
                            link(ins)
                    ins.then_inc(ir_ready, 1)
                elif what == "gate3":
                    dve.wait_ge(irow_ps, 1)
                    dve.tensor_copy(irow[:, :], ps[0:2 * A_HEADS, SB, SEQ:2 * SEQ]).then_inc(irow_ready, 1)
                elif what == "cnorm":
                    dve.wait_ge(crstd_ready, 1)
                    dve.wait_ge(*evac_at["ckv"])
                    for i in range(4):
                        a = cq[:, i % 2, :] if i < 2 else ckv[:, i % 2, 0:C_KVR]
                        dve.tensor_scalar(a, a, crstd[:, i:i + 1], None, ALU.mult).then_inc(cnorm_ready, 1)
                elif what == "cturn":
                    for c in range(5):
                        dve.wait_ge(chi_ready, min(5, 2 * (c // 2) + 2))
                        gain = (col(m, "cq")[:, c:c + 1] if c < 3 else col(m, "ckv")[:, c - 3:c - 2])
                        dve.scalar_tensor_tensor(clo[:, c, :], cslot(c), gain, chi[:, c, :].bitcast(F32),
                                                 ALU.mult, ALU.subtract).then_inc(clo_ready, 1)
                elif what == "conv":
                    dve.wait_ge(upad_ready, v + 1)
                    w0, _ = COLS["conv_w"]
                    link(dve.tensor_scalar(conv[:, v, :], upad[:, v, 0:SEQ], m.cols[:, w0 + v:w0 + v + 1],
                                           col(m, "conv_b")[:, v:v + 1], ALU.mult, ALU.add))
                    for tap in range(1, B_TAPS):
                        w = w0 + tap * 4 + v
                        ins = dve.scalar_tensor_tensor(conv[:, v, :], upad[:, v, tap:tap + SEQ], m.cols[:, w:w + 1],
                                                       conv[:, v, :], ALU.mult, ALU.add)
                        if tap < B_TAPS - 1:
                            link(ins)
                    ins.then_inc(conv_ready, 1)
                elif what == "chead":
                    dve.wait_ge(*evac_at["ukv1"])
                    q4, k4, kv4 = qh[:, :, :, :], kh[:, :, :, :], kv[:, :, :, :]

                    def cs(name):
                        return const(m, name).rearrange("p (t a f) -> p t a f", t=T, a=1)

                    dve.wait_ge(sq_ready, 2 * T)
                    for t in range(T):
                        link(dve.tensor_reduce(hss[:, 0, t, :], qsq[:, t, :, :],
                                               AX.X, ALU.add))
                        link(dve.tensor_reduce(hss[:, 1, t, :], xsq[:, t, :, :], AX.X, ALU.add))
                        link(dve.tensor_tensor_reduce(decay[:, t * C_ROPE:(t + 1) * C_ROPE], ckv[:, t, C_KVR:], ckv[:, t, C_KVR:], 1.0, 0.0,
                                                      ALU.mult, ALU.add, krss[:, t:t + 1]))
                        ins = dve.tensor_scalar(hss[:, 1, t, :], hss[:, 1, t, :], krss[:, t:t + 1], None, ALU.add)
                        if t == 0:
                            link(ins)
                    ins.then_inc(hss_ready, 1)
                    dve.wait_ge(hrs_ready, 1)
                    for t in range(T):
                        hb = [hrs[:, a, t, :].unsqueeze(2) for a in range(2)]
                        link(dve.tensor_tensor(q4[:, t], q4[:, t], hb[0].to_broadcast([P, C_HEADS, C_QK]), ALU.mult))
                        link(dve.tensor_tensor(q4[:, t], q4[:, t],
                                               row(m, "q_g").unsqueeze(1).to_broadcast([P, C_HEADS, C_QK]), ALU.mult))
                        link(dve.tensor_tensor(k4[:, t, :, 0:C_NOPE], kv4[:, t, :, 0:C_NOPE],
                                               hb[1].to_broadcast([P, C_HEADS, C_NOPE]), ALU.mult))
                        link(dve.tensor_tensor(k4[:, t, :, C_NOPE:],
                                               ckv[:, t, C_KVR:].unsqueeze(1).to_broadcast([P, C_HEADS, C_ROPE]),
                                               hb[1].to_broadcast([P, C_HEADS, C_ROPE]), ALU.mult))
                        link(dve.tensor_tensor(k4[:, t], k4[:, t],
                                               row(m, "k_g").unsqueeze(1).to_broadcast([P, C_HEADS, C_QK]), ALU.mult))
                    for a in (q4, k4):
                        for t in range(T):
                            r1, r2 = a[:, t, :, C_NOPE:C_NOPE + 16], a[:, t, :, C_NOPE + 16:]
                            c_t = cs("cos")[:, t].to_broadcast([P, C_HEADS, 16])
                            s_t = cs("sin")[:, t].to_broadcast([P, C_HEADS, 16])
                            rp = [rope[:, t, i, :, :] for i in range(4)]
                            dve.tensor_tensor(rp[0], r1, c_t, ALU.mult)
                            dve.tensor_tensor(rp[1], r2, s_t, ALU.mult)
                            dve.tensor_tensor(rp[2], r2, c_t, ALU.mult)
                            link(dve.tensor_tensor(rp[3], r1, s_t, ALU.mult))
                            dve.tensor_tensor(r1, rp[0], rp[1], ALU.subtract)
                            ins = dve.tensor_tensor(r2, rp[2], rp[3], ALU.add)
                            if t < T - 1:
                                link(ins)
                        ins.then_inc(ckh_ready, 1)
                        dve.wait_ge(ckh_ready, 1 if a is q4 else 2)
                elif what == "m1":
                    dve.wait_ge(ib_ps, v + 1)
                    if v >= 1:
                        dve.wait_ge(emt_ready, v)
                    for j, (a, n) in enumerate(parts):
                        d, t = j // 2, j % 2
                        src = ps[:, SB, d * SEQ:d * SEQ + SEQ]
                        msk = const(m, ("causal", "anti")[d])
                        if n == P:
                            src, msk = (src[:, 0:P], msk[:, P:]) if d == 0 else (src[:, P:], msk[:, 0:P])
                        ins = dve.tensor_tensor_reduce(decay[:, a:a + n], src, msk, 1.0, 0.0, ALU.add, ALU.max, mx[:, j:j + 1])
                    link(ins)
                    link(dve.tensor_tensor(mstat[:, 1, :], mx[:, :], fcum[:, v, :, :].rearrange("p d t -> p (d t)"), ALU.add))
                    dve.tensor_scalar(mstat[:, 0, :], mx[:, :], -1.0, None, ALU.mult).then_inc(mneg_ready, 1)
                elif what == "m2":
                    dve.wait_ge(score_ps, v + 1)
                    dve.wait_ge(emt_ready, v + 1)
                    for j, (a, n) in enumerate(parts):
                        d, t = j // 2, j % 2
                        src = ps[:, SA, t * SEQ:(t + 1) * SEQ]
                        if n == P:
                            src = src[:, 0:P] if d == 0 else src[:, P:]
                        ins = dve.tensor_tensor_reduce(smat[:, a:a + n], src, decay[:, a:a + n], 1.0, 0.0,
                                                       ALU.mult, ALU.add, den[:, j:j + 1])
                    link(ins)
                    link(dve.scalar_tensor_tensor(den[:, :], den[:, :], -1.0, den[:, :], ALU.mult, ALU.max))
                    link(dve.tensor_tensor(den[:, :], den[:, :], mstat[:, 2, :], ALU.max))
                    link(dve.reciprocal(mstat[:, 3, :], den[:, :]))
                    f0, f1, b0, b1 = parts
                    rd = [mstat[:, 3, j:j + 1] for j in range(4)]
                    dve.tensor_scalar(amat[:, 1, :], smat[:, f1[0]:f1[0] + f1[1]], rd[1], None, ALU.mult)
                    link(dve.tensor_scalar(amat[:, 0, :], smat[:, b0[0]:b0[0] + b0[1]], rd[2], None, ALU.mult))
                    dve.scalar_tensor_tensor(amat[:, 0, 0:P], smat[:, f0[0]:f0[0] + P], rd[0], amat[:, 0, 0:P],
                                             ALU.mult, ALU.add)
                    dve.scalar_tensor_tensor(amat[:, 1, P:], smat[:, b1[0]:b1[0] + P], rd[3], amat[:, 1, P:],
                                             ALU.mult, ALU.add).then_inc(amat_ready, 1)
                    dve.wait_ge(amat_ready, v + 1)
                elif what == "m4":
                    dve.wait_ge(hrstd_ready, v + 1)
                    if v == 0:
                        dve.wait_ge(*evac_at["o"])
                    for t in range(T):
                        dve.scalar_tensor_tensor(hn[:, t, :], ps[:, SA, sq(t)], hst[:, 2, t:t + 1],
                                                 o_gate[:, t, v * P:(v + 1) * P], ALU.mult, ALU.mult).then_inc(hn_ready, 1)
                elif what == "m5":
                    dve.wait_ge(yahi, v + 1)
                    dve.scalar_tensor_tensor(ylo[0][:, v, :], ps[:, SA, SEQ:2 * SEQ], col(m, "a_norm")[:, v:v + 1],
                                             yhi[0][:, v, :].bitcast(F32), ALU.mult, ALU.subtract).then_inc(yalo, 1)
                elif what == "c2":
                    dve.wait_ge(cs_ps, v + 1)
                    link(dve.tensor_reduce(cmx[:, 0, :], ps[:, SD, :].rearrange("p (t s) -> p t s", t=T), AX.X, ALU.max))
                    dve.tensor_scalar(cmx[:, 1, :], cmx[:, 0, :], -float(C_QK) ** -0.5, None, ALU.mult).then_inc(cmx_ready, 1)
                    dve.wait_ge(cexp_ready, v + 1)
                    link(dve.reciprocal(csm[:, 1, :], csm[:, 0, :]))
                    for t in range(T):
                        ins = dve.tensor_scalar(pr[:, t, :], pr[:, t, :], csm[:, 1, t:t + 1], None, ALU.mult)
                    ins.then_inc(pr_ready, 1)
                elif what == "c4":
                    r = slice(64 * (v % 2), 64 * (v % 2) + 64)
                    dve.wait_ge(ychi, v + 1)
                    dve.tensor_tensor(ylo[2][r, v // 2, :], ps[r, SD, 0:SEQ], yhi[2][r, v // 2, :].bitcast(F32),
                                      ALU.subtract).then_inc(yclo, 1)
                elif what == "b2":
                    dve.wait_ge(ctok_ps, 1)
                    for t in range(T):
                        link(dve.bn_stats(bst[:, t, :], ps[:, (SC, SD)[t], :]))
                        ins = dve.bn_aggr(bmv[:, t, :], bst[:, t, :])
                        if t == 0:
                            link(ins)
                    ins.then_inc(bvar_ready, 1)
                    dve.wait_ge(bvar_ready, 1)
                elif what == "b3":
                    dve.wait_ge(brstd_ready, 1)
                    for t in range(T):
                        dve.tensor_scalar(u[:, t, :], ps[:, (SC, SD)[t], :], bmv[:, t, 0:1], brstd[:, t:t + 1],
                                          ALU.subtract, ALU.mult).then_inc(bn_ready, 1)
                elif what == "b4":
                    for c in range(4):
                        dve.wait_ge(ybhi, c + 1)
                        dve.tensor_tensor(ylo[1][:, c, :], silu[:, c, :], yhi[1][:, c, :].bitcast(F32),
                                          ALU.subtract).then_inc(yblo, 1)
                elif what == "mturn":
                    for c in range(DC):
                        dve.wait_ge(xhi_ready, DC + 2 * (c // 2) + 2)
                        dve.scalar_tensor_tensor(xlo[:, c, :], turned_ps(m, [SA, SB, SC, SD], c), 0.5,
                                                 xhi[:, c, :].bitcast(F32), ALU.mult, ALU.subtract).then_inc(xlo_ready, 1)

        @block.gpsimd
        def _(pool):
            n_step = [0]

            def link(ins):
                n_step[0] += 1
                ins.then_inc(pool_step, 1)
                pool.wait_ge(pool_step, n_step[0])

            pool.wait_ge(const_in, 64)
            norm_pool(pool, m, 0)
            for g in range(min(lookahead, n_gran)):
                st.split_lo(pool, g)
            for what, v in steps:
                if what == "gran":
                    g = blocks[v[0]][v[1]][0]
                    if g + lookahead < n_gran:
                        st.split_lo(pool, g + lookahead)
                elif what == "cnorm":
                    pool.wait_ge(csum_ready, 2)
                    pool.tensor_scalar(cstat[:, 0:2], csum[:, 0:2], 1.0 / C_QR, EPS, ALU.mult, ALU.add)
                    link(pool.tensor_scalar(cstat[:, 2:4], csum[:, 2:4], 1.0 / C_KVR, EPS, ALU.mult, ALU.add))
                    pool.tensor_tensor(crstd[:, :], cstat[:, :], m.half[:, 0:4], ALU.pow).then_inc(crstd_ready, 1)
                elif what == "chead":
                    pool.wait_ge(*evac_at["ukv1"])
                    for t in range(T):
                        pool.tensor_tensor(qsq[:, t, :, :].rearrange("p h d -> p (h d)"), qh[:, t, :, :].rearrange("p h d -> p (h d)"),
                                           qh[:, t, :, :].rearrange("p h d -> p (h d)"), ALU.mult).then_inc(sq_ready, 1)
                        pool.tensor_tensor(xsq[:, t, :, :], kv[:, t, :, 0:C_NOPE], kv[:, t, :, 0:C_NOPE],
                                           ALU.mult).then_inc(sq_ready, 1)
                    pool.wait_ge(hss_ready, 1)
                    h2, ms2, rs2 = (a[:, :, :, :].rearrange("p a t h -> p (a t h)") for a in (hss, hms, hrs))
                    link(pool.tensor_scalar(ms2, h2, 1.0 / C_QK, EPS, ALU.mult, ALU.add))
                    pool.tensor_tensor(rs2, ms2, m.half[:, 0:1].to_broadcast([P, 2 * T * C_HEADS]), ALU.pow).then_inc(hrs_ready, 1)
                elif what == "m4":
                    pool.wait_ge(hsum_ready, T * (v + 1))
                    link(pool.tensor_scalar(hst[:, 1, :], hst[:, 0, :], 1.0 / A_DIM, EPS, ALU.mult, ALU.add))
                    pool.tensor_tensor(hst[:, 2, :], hst[:, 1, :], m.half[:, 0:T], ALU.pow).then_inc(hrstd_ready, 1)
                elif what == "b2":
                    pool.wait_ge(bvar_ready, 1)
                    link(pool.tensor_scalar(bvar[:, :], bmv[:, :, 1], EPS, None, ALU.add))
                    pool.tensor_tensor(brstd[:, :], bvar[:, :], m.half[:, 0:T], ALU.pow).then_inc(brstd_ready, 1)



def experts(nc, m, I):
    with ExitStack() as ctx:
        def sb(name, shape, dt=F32):
            return ctx.enter_context(nc.sbuf_tensor("sb_" + name, shape, dt))

        def sem(name):
            return ctx.enter_context(nc.semaphore(name))

        ps = m.ps
        J = P // CAP
        FJ = E_FF // J
        FB = FJ // P
        NC = 256
        GK = 2
        NS = 12
        ACC = (0, 1, 2, 3)
        GATE, UP, DOWN = 4, 5, (6, 7)
        NBANKS = [4, 5, 6, 7]

        ring = sb("e_ring", [P, NS, GK * E_FF])
        xgT = sb("xgT", [P, DC, N_EXP * CAP])
        xnT = xgT[:, :, 0:SEQ]
        wr = sb("wr", [P, DC, N_EXP])
        late = sb("slots", [P, CAP])
        smx, ssum = sb("smx", [P, 2, T]), sb("ssum", [P, 2, T])
        aff = sb("aff", [P, T, N_EXP])
        affT, work = sb("affT", [N_EXP, SEQ]), sb("work", [N_EXP, SEQ])
        one = sb("one", [N_EXP, SEQ])
        above, equal = sb("above", [N_EXP, SEQ]), sb("equal", [N_EXP, SEQ])
        top8, cnt = sb("top8", [N_EXP, 8]), sb("cnt", [N_EXP, 2])
        hot, hotg = sb("hot", [P, T, N_EXP, CAP]), sb("hotg", [P, T, N_EXP, CAP])
        xgs = sb("xgs", [P, DC, CAP])
        hotgs = sb("hotgs", [P, T, J, CAP])
        gs = sb("gs", [P, SEQ])
        sg, hs, hT = sb("sg", [P, FJ]), sb("hs", [P, FJ]), sb("hT", [P, FB, P])
        ysb = sb("ysb", [P, D])

        wr_in, late_in = sem("wr_in"), sem("late_in")
        landed = [sem(f"e_landed{i}") for i in range(NS)]
        xnT_act, logits_ps, smx_ready, exp_ready, aff_ready, affT_ps, slot_ready, slot_ps, hot_ready, hotg_ready = (
            sem(s) for s in ("xnT_act", "logits_ps", "smx_ready", "exp_ready", "aff_ready", "affT_ps", "slot_ready",
                             "slot_ps", "hot_ready", "hotg_ready"))
        dve_step = sem("e_dve_step")
        gather_ps, xg_act, xg_dve = sem("gather_ps"), sem("xg_act"), sem("xg_dve")
        used, xgs_ready, g_ps, gs_ready, sg_ready, h_ready, hT_ps, hT_ready, y_act, y_dve, scattered = (
            sem(s) for s in ("e_used", "xgs_ready", "g_ps", "gs_ready", "sg_ready", "h_ready", "hT_ps", "hT_ready",
                             "y_act", "y_dve", "scattered"))

        def source(e, i):
            if i < 8:
                w = I["w_e_gate"] if i < 4 else I["w_e_up"]
                r = (i % 4) * GK * P
                return w[0, e, r:r + GK * P, :].rearrange("(k p) n -> p k n", p=P)
            return I["w_e_down"][0, e, :, (i - 8) * NC:(i - 7) * NC].rearrange("(k p) n -> p k n", p=P)

        def place(i):
            n = E_FF if i < 8 else NC
            return ring[:, i, :].rearrange("p (k n) -> p k n", n=n)

        block = ctx.enter_context(nc.Block())

        @block.sync
        def _(sp):
            sp.dma_start(wr[:, :, :], I["w_router"][0].rearrange("(k p) n -> p k n", p=P)).then_inc(wr_in, 16)
            sp.dma_start(late[:, :], I["c_late"][:, 3 * P:]).then_inc(late_in, 16)
            for i in range(NS):
                sp.dma_start(place(i), source(0, i)).then_inc(landed[i], 16)
            sp.sem_clear(m.mixer_sems)
            with sp.Fori(1, N_EXP) as e:
                for i in range(NS):
                    sp.wait_ge(used, e * NS + (i + 1 - NS))
                    sp.dma_start(place(i), source(e, i)).then_inc(landed[i], 16)

        @block.scalar
        def _(act):
            norm_act(act, m, 1)
            gain = col(m, "ffn")
            for c in range(DC):
                act.wait_ge(m.xturn_ps, 4 + c // 2 + 1)
                act.activation(xnT[:, c, :], turned_ps(m, NBANKS, c), ACT.Copy, scale=gain[:, c:c + 1]).then_inc(xnT_act, 1)
            act.wait_ge(smx_ready, 1)
            for t in range(T):
                ins = act.activation(aff[:, t, :], ps[:, 0, t * N_EXP:(t + 1) * N_EXP], ACT.Exp,
                                     bias=smx[:, 1, t:t + 1], accum_out=ssum[:, 0, t:t + 1])
            ins.then_inc(exp_ready, 1)
            for c in range(0, DC, 2):
                act.wait_ge(gather_ps, c + 1)
                act.activation(xgT[:, c, :], ps[:, 4 + c % 4, :], ACT.Copy, scale=gain[:, c:c + 1]).then_inc(xg_act, 1)
            with act.Fori(0, N_EXP) as e:
                act.wait_ge(g_ps, e + 1)
                for t in range(T):
                    ins = act.activation(gs[:, t * P:(t + 1) * P], ps[:, GATE + t, FJ:FJ + P], ACT.Copy)
                ins.then_inc(gs_ready, 1)
                act.wait_ge(used, e * NS + 4)
                act.activation(sg[:, :], ps[:, GATE, 0:FJ], ACT.Silu).then_inc(sg_ready, 1)
                act.wait_ge(used, e * NS + 10)
                act.activation(ysb[:, 0:BANK], ps[:, DOWN[0], :], ACT.Copy).then_inc(y_act, 1)
            act.wait_ge(scattered, N_EXP)
            for h in range(2):
                act.activation(m.x[:, 0, h * BANK:(h + 1) * BANK], ps[:, ACC[h], :], ACT.Copy)

        @block.tensor
        def _(pe):
            norm_pe(pe, m, 1, NBANKS)
            pe.wait_ge(wr_in, 16)
            pe.wait_ge(xnT_act, DC)
            for t in range(T):
                for c in range(DC):
                    mm = pe.matmul(ps[:, 0, t * N_EXP:(t + 1) * N_EXP], xnT[:, c, t * P:(t + 1) * P], wr[:, c, :],
                                   start=c == 0, stop=c == DC - 1)
            mm.then_inc(logits_ps, 1)
            pe.wait_ge(aff_ready, T)
            for t in range(T):
                mm = pe.transpose(ps[0:N_EXP, 1, t * P:(t + 1) * P], aff[:, t, :], m.ident)
            mm.then_inc(affT_ps, 1)
            pe.wait_ge(slot_ready, 1)
            for t in range(T):
                mm = pe.transpose(ps[:, 2, t * N_EXP:(t + 1) * N_EXP], affT[:, t * P:(t + 1) * P], m.ident[0:N_EXP, 0:N_EXP])
            mm.then_inc(slot_ps, 1)
            pe.wait_ge(hot_ready, T)
            for c in range(DC):
                if c >= 4:
                    pe.wait_ge((xg_act, xg_dve)[c % 2], (c - 4) // 2 + 1)
                for t in range(T):
                    mm = pe.matmul(ps[:, 4 + c % 4, :], m.xs[:, t, c * P:(c + 1) * P],
                                   hot[:, t, :, :].rearrange("p e c -> p (e c)"), start=t == 0, stop=t == T - 1)
                mm.then_inc(gather_ps, 1)
            for t in range(T):
                for h in range(2):
                    pe.matmul(ps[:, ACC[2 * t + h], :], m.ident, m.x[:, t, h * BANK:(h + 1) * BANK], start=True, stop=True)
            pe.wait_ge(xg_act, DC // 2)
            pe.wait_ge(xg_dve, DC // 2)
            with pe.Fori(0, N_EXP) as e:
                pe.wait_ge(xgs_ready, e * 2 + 2)
                for t in range(T):
                    mm = pe.transpose(ps[:, GATE + t, FJ:FJ + P], hotgs[:, t, :, :].rearrange("p j c -> p (j c)"), m.ident)
                mm.then_inc(g_ps, 1)
                pe.wait_ge(gs_ready, e + 1)
                for i in range(8):
                    pe.wait_ge(landed[i], e * 16 + 16)
                    for q in range(GK):
                        k = (i % 4) * GK + q
                        for j in range(J):
                            mm = pe.matmul(ps[j * CAP:(j + 1) * CAP, GATE if i < 4 else UP, 0:FJ], xgs[:, k, :],
                                           place(i)[:, q, j * FJ:(j + 1) * FJ], start=k == 0, stop=k == DC - 1)
                    mm.then_inc(used, 1)
                pe.wait_ge(h_ready, e + 1)
                for b in range(FB):
                    mm = pe.transpose(ps[:, GATE, b * P:(b + 1) * P], hs[:, b * P:(b + 1) * P], m.ident)
                mm.then_inc(hT_ps, 1)
                pe.wait_ge(hT_ready, e + 1)
                for i in range(4):
                    pe.wait_ge(landed[8 + i], e * 16 + 16)
                    for b in range(FB):
                        for j in range(J):
                            mm = pe.matmul(ps[j * CAP:(j + 1) * CAP, DOWN[i // 2], (i % 2) * NC:(i % 2 + 1) * NC],
                                           hT[:, b, j * CAP:(j + 1) * CAP], place(8 + i)[:, j * FB + b, :],
                                           start=b == 0, stop=b == FB - 1)
                    mm.then_inc(used, 1)
                pe.wait_ge(y_act, e + 1)
                pe.wait_ge(y_dve, e + 1)
                for t in range(T):
                    for h in range(2):
                        mm = pe.matmul(ps[:, ACC[2 * t + h], :], gs[:, t * P:(t + 1) * P], ysb[:, h * BANK:(h + 1) * BANK],
                                       start=False, stop=True, skip_group_check=True)
                mm.then_inc(scattered, 1)

        @block.vector
        def _(dve):
            n_step = [0]

            def link(ins):
                n_step[0] += 1
                ins.then_inc(dve_step, 1)
                dve.wait_ge(dve_step, n_step[0])

            link(dve.memset(one[:, :], 1.0))
            norm_dve(dve, m, 1)
            gain = col(m, "ffn")
            dve.wait_ge(logits_ps, 1)
            link(dve.tensor_reduce(smx[:, 0, :], ps[:, 0, 0:T * N_EXP].rearrange("p (t e) -> p t e", t=T), AX.X, ALU.max))
            dve.tensor_scalar(smx[:, 1, :], smx[:, 0, :], -1.0, None, ALU.mult).then_inc(smx_ready, 1)
            dve.wait_ge(exp_ready, 1)
            link(dve.reciprocal(ssum[:, 1, :], ssum[:, 0, :]))
            for t in range(T):
                dve.tensor_scalar(aff[:, t, :], aff[:, t, :], ssum[:, 1, t:t + 1], None, ALU.mult).then_inc(aff_ready, 1)
            dve.wait_ge(affT_ps, 1)
            link(dve.tensor_copy(affT[:, :], ps[0:N_EXP, 1, 0:SEQ]))
            src = affT
            for r in range(CAP // 8):
                link(dve.max(top8[:, :], src[:, :]))
                if r < CAP // 8 - 1:
                    link(dve.match_replace(work[:, :], top8[:, :], src[:, :], -1.0))
                    src = work
            link(dve.tensor_scalar(above[:, :], affT[:, :], top8[:, 7:8], None, ALU.is_gt, ALU.add, accum_out=cnt[:, 0:1]))
            link(dve.tensor_scalar(equal[:, :], affT[:, :], top8[:, 7:8], None, ALU.is_equal))
            link(dve.tensor_scalar(cnt[:, 1:2], cnt[:, 0:1], -1.0, float(CAP), ALU.mult, ALU.add))
            link(dve.tensor_tensor_scan(work[:, :], one[:, :], equal[:, :], 0.0, ALU.mult, ALU.add))
            link(dve.scalar_tensor_tensor(equal[:, :], work[:, :], cnt[:, 1:2], equal[:, :], ALU.is_le, ALU.mult))
            link(dve.tensor_tensor(above[:, :], above[:, :], equal[:, :], ALU.add))
            link(dve.tensor_tensor_scan(work[:, :], one[:, :], above[:, :], 0.0, ALU.mult, ALU.add))
            dve.tensor_tensor(affT[:, :], work[:, :], above[:, :], ALU.mult).then_inc(slot_ready, 1)
            dve.wait_ge(slot_ps, 1)
            dve.wait_ge(late_in, 16)
            for t in range(T):
                slots = ps[:, 2, t * N_EXP:(t + 1) * N_EXP].unsqueeze(2).to_broadcast([P, N_EXP, CAP])
                dve.tensor_tensor(hot[:, t, :, :], slots, late[:, :].unsqueeze(1).to_broadcast([P, N_EXP, CAP]),
                                  ALU.is_equal).then_inc(hot_ready, 1)
            dve.wait_ge(hot_ready, T)
            for t in range(T):
                dve.tensor_tensor(hotg[:, t, :, :], hot[:, t, :, :], aff[:, t, :].unsqueeze(2).to_broadcast([P, N_EXP, CAP]),
                                  ALU.mult).then_inc(hotg_ready, 1)
            for c in range(1, DC, 2):
                dve.wait_ge(gather_ps, c + 1)
                dve.tensor_scalar(xgT[:, c, :], ps[:, 4 + c % 4, :], gain[:, c:c + 1], None, ALU.mult).then_inc(xg_dve, 1)
            with dve.Fori(0, N_EXP) as e:
                dve.wait_ge(sg_ready, e + 1)
                dve.wait_ge(used, e * NS + 8)
                dve.tensor_tensor(hs[:, :], ps[:, UP, 0:FJ], sg[:, :], ALU.mult).then_inc(h_ready, 1)
                dve.wait_ge(hT_ps, e + 1)
                dve.tensor_copy(hT[:, :, :].rearrange("p b c -> p (b c)"), ps[:, GATE, 0:FJ]).then_inc(hT_ready, 1)
                dve.wait_ge(used, e * NS + 12)
                dve.tensor_copy(ysb[:, BANK:], ps[:, DOWN[1], :]).then_inc(y_dve, 1)
            dve.wait_ge(scattered, N_EXP)
            for h in range(2):
                dve.tensor_copy(m.x[:, 1, h * BANK:(h + 1) * BANK], ps[:, ACC[2 + h], :])

        @block.gpsimd
        def _(pool):
            norm_pool(pool, m, 1)

            def take(e):
                pool.tensor_copy(xgs[:, :, :], xgT[:, :, bass.ds(e * CAP, CAP)]).then_inc(xgs_ready, 1)
                pool.tensor_copy(hotgs[:, :, :, :],
                                 hotg[:, :, bass.ds(e, 1), :].to_broadcast([P, T, J, CAP])).then_inc(xgs_ready, 1)

            pool.wait_ge(hotg_ready, T)
            pool.wait_ge(xg_act, DC // 2)
            pool.wait_ge(xg_dve, DC // 2)
            take(0)
            with pool.Fori(0, N_EXP - 1) as e:
                pool.wait_ge(used, e * NS + 8)
                take(e + 1)



FW = 256
FN = D_FF // FW
FC = FW // P


def second_stream(m, ctx, nc, I):
    st = Stream(m, ctx, nc, "net", 6, 3)
    at = {}

    def dense(name, w, n0):
        at[name] = [st.add([(0, 4, BANK, chunks(w, k, 4, n0, BANK))]) for k in (0, 4)]

    def ffn(l):
        gu, down = I["ffn_w_gu_2"][l], I["ffn_w_down_2"][l]
        at[f"ffn{l}"] = len(st.pieces)

        def gate_up(b):
            for k in (0, 4):
                st.add([(0, 4, FW, chunks(gu, k, 4, b * FW, FW)), (4 * FW, 4, FW, chunks(gu, k, 4, D_FF + b * FW, FW))])

        for b in range(FN):
            gate_up(b)
            if b >= 1:
                st.add([(0, FC, D, chunks(down, (b - 1) * FC, FC, 0, D))], by_dve=True)
        st.add([(0, FC, D, chunks(down, (FN - 1) * FC, FC, 0, D))], by_dve=True)

    for name, n0 in (("v0", D), ("v1", D + BANK), ("u0", 0), ("u1", BANK)):
        dense(name, I["a_w_in_2"][0], n0)
    for h in range(2):
        dense(f"go{h}", I["a_w_out_2"][0], h * BANK)
    ffn(0)
    for h in range(2):
        dense(f"q{h}", I["b_w_q_2"][0], h * BANK)
    for h in range(4):
        dense(("k0", "k1", "w0", "w1")[h], I["kv_w_2"], h * BANK)
    for h in range(2):
        dense(f"o{h}", I["b_w_o_2"][0], h * BANK)
    ffn(1)
    return st, at


def add_to_x(dve, m, st, at, name, banks, h, done=None):
    dve.wait_ge(st.used, at[name][-1] + 1)
    for t in range(T):
        dst = m.x[:, t, h * BANK:(h + 1) * BANK]
        ins = dve.tensor_tensor(dst, m.ps[:, banks[t], :], dst, ALU.add)
    if done is not None:
        ins.then_inc(done, 1)


def gmlp(nc, m, I, st, at, use):
    with ExitStack() as ctx:
        def sb(name, shape, dt=F32):
            return ctx.enter_context(nc.sbuf_tensor("sb_" + name, shape, dt))

        def sem(name):
            return ctx.enter_context(nc.semaphore(name))

        ps = m.ps
        ut, vt = sb("g_u", [P, T, D]), sb("g_v", [P, T, D])
        wsp, gain = sb("wsp", [P, G_GROUPS, P]), sb("g_gain", [P, D])
        bst, bmv, bvar, brs = sb("g_bst", [P, T, 2, 6]), sb("g_bmv", [P, T, 2]), sb("g_bvar", [P, T]), sb("g_brs", [P, T])
        tmp = sb("g_tmp", [P, 2, T, P])
        wsp_in, gain_in, wsp_ready = sem("wsp_in"), sem("gain_in"), sem("wsp_ready")
        z_act, var_ready, rs_ready, v_ready, sp_ps, mix_ready, mixT_ps, mhi, mlo, out_read = (
            sem(s) for s in ("g_z_act", "g_var_ready", "g_rs_ready", "g_v_ready", "sp_ps", "g_mix_ready", "g_mixT_ps",
                             "g_mhi", "g_mlo", "g_out_read"))
        dve_step = sem("g_dve_step")
        xhi_ready, xlo_ready = sem("g_xhi_ready"), sem("g_xlo_ready")
        order = ["v0", "v1", "u0", "u1"]
        first = at["v0"][0]
        last = at["go1"][-1]
        look = 2
        NB = [4, 5, 6, 7]
        block = ctx.enter_context(nc.Block())

        def zb(i):
            return [2 * (i % 2) + t for t in range(T)]

        @block.sync
        def _(sp):
            sp.dma_start(wsp[:, :, :], I["w_spT"]).then_inc(wsp_in, 16)
            sp.dma_start(gain[:, :], I["a_v_norm_2"][0].partition_broadcast(P)).then_inc(gain_in, 16)
            for g in range(first, last + 1 + st.slots):
                st.load(sp, g)

        @block.scalar
        def _(act):
            norm_act(act, m, use)
            for g in range(first, first + look):
                st.split_hi(act, g)
            norm_hi_act(act, m, use, NB, m.xhi, col(m, "gmlp"), xhi_ready, 0)
            for i, name in enumerate(order):
                for g in at[name]:
                    st.split_hi(act, g + look)
                act.wait_ge(st.used, at[name][-1] + 1)
                for t in range(T):
                    dst = (vt, ut)[i // 2][:, t, (i % 2) * BANK:(i % 2 + 1) * BANK]
                    act.activation(dst, ps[:, zb(i)[t], :], ACT.Gelu_apprx_tanh).then_inc(z_act, 1)
            for c in range(DC):
                act.wait_ge(mixT_ps, c // 2 + 1)
                act.activation(m.xhi[:, c, :], turned_ps(m, [0, 1, 2, 3], c), ACT.Copy).then_inc(mhi, 1)
            for name in ("go0", "go1"):
                for g in at[name]:
                    if g + look <= last:
                        st.split_hi(act, g + look)

        @block.gpsimd
        def _(pool):
            pool.wait_ge(wsp_in, 16)
            pool.tensor_tensor(wsp[:, :, :], wsp[:, :, :],
                               const(m, "upto").unsqueeze(1).to_broadcast([P, G_GROUPS, P]), ALU.mult).then_inc(wsp_ready, 1)
            norm_pool(pool, m, use)
            for g in range(first, first + look):
                st.split_lo(pool, g)
            for i, name in enumerate(order + ["go0", "go1"]):
                for g in at[name]:
                    if g + look <= last:
                        st.split_lo(pool, g + look)
                if name == "v1":
                    pool.wait_ge(var_ready, 1)
                    pool.tensor_scalar(bvar[:, :], bmv[:, :, 1], EPS, None, ALU.add).then_inc(rs_ready, 1)
                    pool.wait_ge(rs_ready, 1)
                    pool.tensor_tensor(brs[:, :], bvar[:, :], m.half[:, 0:T], ALU.pow).then_inc(rs_ready, 1)

        @block.tensor
        def _(pe):
            norm_pe(pe, m, use, NB)
            for i, name in enumerate(order):
                if i >= 2:
                    pe.wait_ge(z_act, T * (i - 1))
                for j, g in enumerate(at[name]):
                    dense_granule(pe, st, g, [ps[:, b, :] for b in zb(i)], m.xhi, m.xlo, 4 * j, BANK, j == 0, j == 1,
                                  (xlo_ready, 0) if i == 0 else None)
            pe.wait_ge(v_ready, T)
            pe.wait_ge(wsp_ready, 1)
            for q in range(G_GROUPS):
                mm = pe.matmul(ps[:, 4 + q // 2, (q % 2) * SEQ:(q % 2 + 1) * SEQ], wsp[:, q, :],
                               vt[:, :, q * P:(q + 1) * P], start=True, stop=True)
                if q % 2:
                    mm.then_inc(sp_ps, 1)
            pe.wait_ge(z_act, 4 * T)
            for b in range(4):
                pe.wait_ge(mix_ready, 2 * b + 2)
                for cc in range(2):
                    for t in range(T):
                        c = 2 * b + cc
                        mm = pe.transpose(ps[:, b, cc * SEQ + t * P:cc * SEQ + (t + 1) * P], ut[:, t, c * P:(c + 1) * P], m.ident)
                mm.then_inc(mixT_ps, 1)
            for h in range(2):
                for j, g in enumerate(at[f"go{h}"]):
                    dense_granule(pe, st, g, [ps[:, 4 + 2 * h + t, :] for t in range(T)], m.xhi, m.xlo, 4 * j, BANK,
                                  j == 0, j == 1, (mlo, 0) if h == 0 else None)

        @block.vector
        def _(dve):
            n_step = [0]

            def link(ins):
                n_step[0] += 1
                ins.then_inc(dve_step, 1)
                dve.wait_ge(dve_step, n_step[0])

            norm_dve(dve, m, use)
            norm_lo_dve(dve, m, use, NB, m.xhi, m.xlo, col(m, "gmlp"), xhi_ready, xlo_ready, 0)
            for i in range(2):
                dve.wait_ge(z_act, T * (i + 1))
                for t in range(T):
                    ins = dve.bn_stats(bst[:, t, i, :], vt[:, t, i * BANK:(i + 1) * BANK])
            link(ins)
            for t in range(T):
                ins = dve.bn_aggr(bmv[:, t, :], bst[:, t, :, :].rearrange("p i s -> p (i s)"))
            ins.then_inc(var_ready, 1)
            dve.wait_ge(rs_ready, 2)
            for t in range(T):
                dve.tensor_scalar(vt[:, t, :], vt[:, t, :], bmv[:, t, 0:1], brs[:, t:t + 1], ALU.subtract,
                                  ALU.mult).then_inc(v_ready, 1)
            dve.wait_ge(gain_in, 16)
            dve.wait_ge(z_act, 4 * T)
            for q in range(G_GROUPS):
                dve.wait_ge(sp_ps, q // 2 + 1)
                sl = slice(q * P, (q + 1) * P)
                link(dve.tensor_tensor(tmp[:, q % 2, :, :],
                                       ps[:, 4 + q // 2, (q % 2) * SEQ:(q % 2 + 1) * SEQ].rearrange("p (t d) -> p t d", t=T),
                                       gain[:, sl].unsqueeze(1).to_broadcast([P, T, P]), ALU.mult))
                dve.scalar_tensor_tensor(ut[:, :, sl], tmp[:, q % 2, :, :], col(m, "b_sp")[:, q:q + 1], ut[:, :, sl],
                                         ALU.add, ALU.mult).then_inc(mix_ready, 1)
            dve.wait_ge(mix_ready, G_GROUPS)
            for c in range(DC):
                dve.wait_ge(mhi, 2 * (c // 2) + 2)
                dve.tensor_tensor(m.xlo[:, c, :], turned_ps(m, [0, 1, 2, 3], c), m.xhi[:, c, :].bitcast(F32),
                                  ALU.subtract).then_inc(mlo, 1)
            for h in range(2):
                add_to_x(dve, m, st, at, f"go{h}", [4 + 2 * h + t for t in range(T)], h)


def swiglu(nc, m, I, st, at, l, use):
    with ExitStack() as ctx:
        def sb(name, shape, dt=F32):
            return ctx.enter_context(nc.sbuf_tensor(f"sb_f{l}_" + name, shape, dt))

        def sem(name):
            return ctx.enter_context(nc.semaphore(f"f{l}_" + name))

        ps = m.ps
        sg, ft = sb("sg", [P, T, FW]), sb("ft", [P, T, FW])
        ahi, alo = sb("ahi", [P, FC, SEQ], F32R), sb("alo", [P, FC, SEQ], F32R)
        xhi_ready, xlo_ready, silu_ready, ft_ready, turn_ps, ahi_ready, alo_ready, sums_ready = (
            sem(s) for s in ("xhi_ready", "xlo_ready", "silu_ready", "ft_ready", "turn_ps", "ahi_ready", "alo_ready", "sums_ready"))
        g0 = at[f"ffn{l}"]
        n_gran = 3 * FN
        gain = col(m, f"ffn{l}")
        ACC, GU, TURN = (0, 1, 2, 3), (4, 5), 6
        NB = list(ACC)
        ROUND, BLOCKS = 6, 2
        TURNS = (FN - 3) // BLOCKS
        look = 2

        def shift(it, n):
            return 0 if isinstance(it, int) and it == 0 else it * n

        def w_hi(act, i, it):
            g = g0 + i
            n = st.size(g)
            act.wait_ge(st.landed[g % st.slots], shift(it, 16 * len(st.pieces[g])) + st.arrive[g])
            act.wait_ge(st.used, shift(it, ROUND) + (g - st.bufs + 1))
            act.activation(st.hi[:, g % st.bufs, 0:n], st.ring[:, g % st.slots, 0:n], ACT.Copy).then_inc(st.hi_ready, 1)

        def is_down(i):
            return i >= 2 and (i - 2) % 3 == 2 or i == n_gran - 1

        def w_lo(eng, i, it):
            g = g0 + i
            n = st.size(g)
            eng.wait_ge(st.hi_ready, shift(it, ROUND) + (g + 1))
            eng.tensor_tensor(st.lo[:, g % st.bufs, 0:n], st.ring[:, g % st.slots, 0:n],
                              st.hi[:, g % st.bufs, 0:n].bitcast(F32), ALU.subtract).then_inc(st.lows[g][0], 1)

        def lo_done(eng, i, it):
            s, n = st.lows[g0 + i]
            eng.wait_ge(s, shift(it, 2 if is_down(i) else 4) + n)

        def gu_index(b):
            return 0 if b == 0 else 2 + 3 * (b - 1)

        def down_index(b):
            return 4 + 3 * b if b < FN - 1 else n_gran - 1

        block = ctx.enter_context(nc.Block())

        @block.sync
        def _(sp):
            def load(i, it):
                g = g0 + i
                lo_done(sp, i - st.slots, it)
                for off, nk, n, src in pieces(i, it):
                    dst = st.ring[:, g % st.slots, off:off + nk * n].rearrange("p (k n) -> p k n", n=n)
                    sp.dma_start(dst, src).then_inc(st.landed[g % st.slots], 16)

            def pieces(i, it):
                if is_down(i):
                    b = (i - 2) // 3
                    src = I["ffn_w_down_2"][l, bass.ds(it * (BLOCKS * FW) + b * FW, FW), :].rearrange("(k p) n -> p k n", p=P)
                    return [(0, FC, D, src)]
                b, k = 1 + (i - 2) // 3, 4 * ((i - 2) % 3)
                rows = I["ffn_w_gu_2"][l, k * P:(k + 4) * P, :]
                return [(a * 4 * FW, 4, FW, rows[:, bass.ds(it * (BLOCKS * FW) + (a * D_FF + b * FW), FW)]
                         .rearrange("(k p) n -> p k n", p=P)) for a in range(2)]

            for i in range(st.slots, 2 + ROUND):
                st.load(sp, g0 + i)
            with sp.Fori(0, TURNS - 1) as it:
                for r in range(ROUND):
                    load(2 + ROUND + r, it)
            for i in range(2 + ROUND * TURNS, n_gran):
                st.load(sp, g0 + i)
            for g in range(g0 + n_gran, min(g0 + n_gran + st.slots, len(st.pieces))):
                st.load(sp, g)

        @block.scalar
        def _(act):
            norm_act(act, m, use)
            w_hi(act, 0, 0)
            w_hi(act, 1, 0)
            norm_hi_act(act, m, use, NB, m.xhi, gain, xhi_ready, 0)

            def part(b, it):
                i = gu_index(b)
                for r in range(3 if b else 2):
                    if i + r + look < n_gran:
                        w_hi(act, i + r + look, it)
                    if r == 1:
                        act.wait_ge(st.used, shift(it, ROUND) + (g0 + i + 2))
                        for t in range(T):
                            act.activation(sg[:, t, :], ps[:, GU[t], 0:FW], ACT.Silu).then_inc(silu_ready, 1)
                act.wait_ge(turn_ps, shift(it, BLOCKS) + (b + 1))
                act.activation(ahi[:, :, :].rearrange("p c s -> p (c s)"), ps[:, TURN, :], ACT.Copy).then_inc(ahi_ready, 1)

            part(0, 0)
            with act.Fori(0, TURNS) as it:
                for b in range(1, 1 + BLOCKS):
                    part(b, it)
            for b in range(FN - 2, FN):
                part(b, 0)

        @block.gpsimd
        def _(pool):
            norm_pool(pool, m, use)
            for i in range(2 + look):
                w_lo(pool, i, 0)
            with pool.Fori(0, TURNS) as it:
                for r in range(ROUND):
                    if not is_down(2 + look + r):
                        w_lo(pool, 2 + look + r, it)
            for i in range(2 + look + ROUND * TURNS, n_gran):
                if not is_down(i):
                    w_lo(pool, i, 0)

        @block.tensor
        def _(pe):
            norm_pe(pe, m, use, NB)

            def gate_up(b, it):
                for j in range(2):
                    i = gu_index(b) + j
                    lo_done(pe, i, it)
                    whi, wlo = [x[:, (g0 + i) % st.bufs, :].rearrange("p (a k n) -> p k a n", a=2, n=FW) for x in (st.hi, st.lo)]
                    for k in range(4):
                        c = 4 * j + k
                        if b == 0:
                            pe.wait_ge(xlo_ready, c + 1)
                        for t in range(T):
                            mm = three_products(pe, ps[:, GU[t], :], m.xhi[:, c, t * P:(t + 1) * P], m.xlo[:, c, t * P:(t + 1) * P],
                                                whi[:, k, :, :], wlo[:, k, :, :], c == 0, c == DC - 1)
                    mm.then_inc(st.used, 1)

            def down(b, it):
                i = down_index(b)
                lo_done(pe, i, it)
                pe.wait_ge(alo_ready, shift(it, BLOCKS) + (b + 1))
                whi, wlo = [x[:, (g0 + i) % st.bufs, :].rearrange("p (k n) -> p k n", n=D) for x in (st.hi, st.lo)]
                for k in range(FC):
                    for t in range(T):
                        for h in range(2):
                            hs = slice(h * BANK, (h + 1) * BANK)
                            at_, al_ = ahi[:, k, t * P:(t + 1) * P], alo[:, k, t * P:(t + 1) * P]
                            out = ps[:, ACC[2 * t + h], :]
                            for a, w in ((at_, whi), (at_, wlo), (al_, whi)):
                                mm = pe.matmul(out, a, w[:, k, hs], start=False, stop=True, skip_group_check=True)
                mm.then_inc(st.used, 1)

            def turn(b, it):
                pe.wait_ge(ft_ready, shift(it, T * BLOCKS) + T * (b + 1))
                for c in range(FC):
                    for t in range(T):
                        mm = pe.transpose(ps[:, TURN, c * SEQ + t * P:c * SEQ + (t + 1) * P], ft[:, t, c * P:(c + 1) * P], m.ident)
                mm.then_inc(turn_ps, 1)

            gate_up(0, 0)
            for t in range(T):
                for h in range(2):
                    pe.matmul(ps[:, ACC[2 * t + h], :], m.ident, m.x[:, t, h * BANK:(h + 1) * BANK], start=True, stop=True)
            turn(0, 0)
            with pe.Fori(0, TURNS) as it:
                for b in range(1, 1 + BLOCKS):
                    gate_up(b, it)
                    down(b - 1, it)
                    turn(b, it)
            for b in range(FN - 2, FN):
                gate_up(b, 0)
                down(b - 1, 0)
                turn(b, 0)
            down(FN - 1, 0)

        @block.vector
        def _(dve):
            norm_dve(dve, m, use)
            norm_lo_dve(dve, m, use, NB, m.xhi, m.xlo, gain, xhi_ready, xlo_ready, 0)

            def part(b, it):
                i = gu_index(b)
                for t in range(T):
                    dve.wait_ge(silu_ready, shift(it, T * BLOCKS) + (T * b + t + 1))
                    dve.tensor_tensor(ft[:, t, :], ps[:, GU[t], FW:], sg[:, t, :], ALU.mult).then_inc(ft_ready, 1)
                for r in range(3 if b else 2):
                    if i + r + look < n_gran and is_down(i + r + look):
                        w_lo(dve, i + r + look, it)
                dve.wait_ge(ahi_ready, shift(it, BLOCKS) + (b + 1))
                dve.tensor_tensor(alo[:, :, :].rearrange("p c s -> p (c s)"), ps[:, TURN, :],
                                  ahi[:, :, :].rearrange("p c s -> p (c s)").bitcast(F32), ALU.subtract).then_inc(alo_ready, 1)

            part(0, 0)
            with dve.Fori(0, TURNS) as it:
                for b in range(1, 1 + BLOCKS):
                    part(b, it)
            for b in range(FN - 2, FN):
                part(b, 0)
            dve.wait_ge(st.used, g0 + n_gran)
            for t in range(T):
                for h in range(2):
                    dve.tensor_copy(m.x[:, t, h * BANK:(h + 1) * BANK], ps[:, ACC[2 * t + h], :])


def diff_attention(nc, m, I, st, at, use):
    with ExitStack() as ctx:
        def sb(name, shape, dt=F32):
            return ctx.enter_context(nc.sbuf_tensor("sb_" + name, shape, dt))

        def sem(name):
            return ctx.enter_context(nc.semaphore(name))

        ps = m.ps
        khi, klo = sb("d_khi", [P, DC, SEQ], F32R), sb("d_klo", [P, DC, SEQ], F32R)
        qt, kt, vt = sb("d_q", [P, T, D]), sb("d_k", [P, T, D]), sb("d_v", [P, T, D])
        dist, lam_in_ = sb("dist", [P, 3 * P]), sb("lam_in", [P, N_LAM])
        lam, lamw = sb("lam", [P, 8]), sb("lamw", [P, 2 * D_DIM])
        sub = sb("sub", [P, 1])
        qkT = sb("d_qkT", [P, 2, SEQ])
        bias = sb("d_bias", [P, 2, 3 * P])
        e = sb("d_e", [P, 2, 3 * P])
        eT = sb("d_eT", [P, 3 * P])
        mx, sm = sb("d_mx", [P, 2, 4]), sb("d_sm", [P, 2, 4])
        ost, on = sb("d_ost", [P, 3, T]), sb("d_on", [P, T, D_V])
        xhi_ready, xlo_ready, z_act, dist_in, lam_in, dve_step, pool_step = (
            sem(s) for s in ("d_xhi_ready", "d_xlo_ready", "d_z_act", "d_dist_in", "d_lam_in", "d_dve_step", "d_pool_step"))
        lsum_ready, lexp_ready, lam_ready = sem("lsum_ready"), sem("lexp_ready"), sem("lam_ready")
        bias_ready, qk_ps, qkT_ready, s_ps, mx_ready, e_ready, a_ready, aT_ps, aT_ready, o_ps, osum_ready, ors_ready, on_ready, oT_ps, ohi, olo = (
            sem(s) for s in ("bias_ready", "d_qk_ps", "d_qkT_ready", "s_ps", "d_mx_ready", "e_ready", "a_ready", "aT_ps",
                             "aT_ready", "o_ps", "osum_ready", "ors_ready", "on_ready", "oT_ps", "ohi", "olo"))
        order = ["q0", "q1", "k0", "k1", "w0", "w1"]
        first, last = at["q0"][0], at["o1"][-1]
        look = 2
        NB = [4, 5, 6, 7]
        SCALE = float(D_DIM) ** -0.5
        slopes = [2.0 ** (-8.0 * (h + 1) / D_HEADS) for h in range(D_HEADS)]
        spans = [slice(0, P), slice(P, 3 * P)]
        block = ctx.enter_context(nc.Block())

        def zb(i):
            return [2 * (i % 2) + t for t in range(T)]

        @block.sync
        def _(sp):
            sp.dma_start(dist[:, :], I["c_late"][:, 0:3 * P]).then_inc(dist_in, 16)
            sp.dma_start(lam_in_[:, :], I["v_lam"]).then_inc(lam_in, 16)
            for g in range(first + st.slots, last + 1 + st.slots):
                st.load(sp, g)

        @block.scalar
        def _(act):
            norm_act(act, m, use)
            for g in range(first, first + look):
                st.split_hi(act, g)
            for b in range(4):
                act.wait_ge(m.xturn_ps, 4 * use + b + 1)
                for hi, name in ((m.xhi, "bq"), (khi, "kv")):
                    for c in (2 * b, 2 * b + 1):
                        act.activation(hi[:, c, :], turned_ps(m, NB, c), ACT.Copy,
                                       scale=col(m, name)[:, c:c + 1]).then_inc(xhi_ready, 1)
            act.wait_ge(lsum_ready, 1)
            act.activation(lam[:, 2:4], lam[:, 0:2], ACT.Exp).then_inc(lexp_ready, 1)
            for i, name in enumerate(order):
                for g in at[name]:
                    st.split_hi(act, g + look)
                act.wait_ge(st.used, at[name][-1] + 1)
                for t in range(T):
                    dst = (qt, kt, vt)[i // 2][:, t, (i % 2) * BANK:(i % 2 + 1) * BANK]
                    act.activation(dst, ps[:, zb(i)[t], :], ACT.Copy).then_inc(z_act, 1)
            for h in range(D_HEADS):
                act.wait_ge(qk_ps, h + 1)
                act.activation(qkT[:, :, :].rearrange("p a s -> p (a s)"), ps[:, 4, :], ACT.Copy).then_inc(qkT_ready, 1)
                act.wait_ge(mx_ready, h + 1)
                for i in range(2):
                    for t in range(T):
                        act.activation(e[:, i, spans[t]], e[:, i, spans[t]], ACT.Exp, bias=mx[:, 1, 2 * i + t:2 * i + t + 1],
                                       scale=SCALE, accum_out=sm[:, 0, 2 * i + t:2 * i + t + 1]).then_inc(e_ready, 1)
                act.wait_ge(aT_ps, h + 1)
                act.activation(eT[:, :], ps[:, 4, 0:3 * P], ACT.Copy).then_inc(aT_ready, 1)
                act.wait_ge(o_ps, h + 1)
                for t in range(T):
                    act.activation(on[:, t, :], ps[:, 7, t * P:(t + 1) * P], ACT.Square,
                                   accum_out=ost[:, 0, t:t + 1]).then_inc(osum_ready, 1)
                act.wait_ge(oT_ps, h + 1)
                act.activation(m.xhi[:, h, :], ps[:, 7, SEQ:], ACT.Copy, scale=sub[:, 0:1]).then_inc(ohi, 1)
            for name in ("o0", "o1"):
                for g in at[name]:
                    if g + look <= last:
                        st.split_hi(act, g + look)

        @block.gpsimd
        def _(pool):
            n_step = [0]

            def link(ins):
                n_step[0] += 1
                ins.then_inc(pool_step, 1)
                pool.wait_ge(pool_step, n_step[0])

            norm_pool(pool, m, use)
            for g in range(first, first + look):
                st.split_lo(pool, g)
            for name in order:
                for g in at[name]:
                    st.split_lo(pool, g + look)
            pool.wait_ge(dist_in, 16)
            for h in range(D_HEADS):
                if h >= 2:
                    pool.wait_ge(a_ready, h - 1)
                pool.tensor_scalar(bias[:, h % 2, :], dist[:, :], slopes[h] / SCALE, None, ALU.mult).then_inc(bias_ready, 1)
                pool.wait_ge(osum_ready, T * (h + 1))
                link(pool.tensor_scalar(ost[:, 1, :], ost[:, 0, :], 1.0 / D_V, EPS, ALU.mult, ALU.add))
                pool.tensor_tensor(ost[:, 2, :], ost[:, 1, :], m.half[:, 0:T], ALU.pow).then_inc(ors_ready, 1)
            for name in ("o0", "o1"):
                for g in at[name]:
                    if g + look <= last:
                        st.split_lo(pool, g + look)

        @block.tensor
        def _(pe):
            norm_pe(pe, m, use, NB)
            for i, name in enumerate(order):
                if i >= 2:
                    pe.wait_ge(z_act, T * (i - 1))
                hi, lo = (m.xhi, m.xlo) if i < 2 else (khi, klo)
                if i == 0:
                    pe.wait_ge(xlo_ready, 2 * DC)
                for j, g in enumerate(at[name]):
                    dense_granule(pe, st, g, [ps[:, b, :] for b in zb(i)], hi, lo, 4 * j, BANK, j == 0, j == 1)
            pe.wait_ge(z_act, 6 * T)
            for h in range(D_HEADS):
                for a, src in ((0, qt), (1, kt)):
                    for t in range(T):
                        mm = pe.transpose(ps[:, 4, a * SEQ + t * P:a * SEQ + (t + 1) * P], src[:, t, h * P:(h + 1) * P], m.ident)
                mm.then_inc(qk_ps, 1)
                pe.wait_ge(qkT_ready, h + 1)
                for i in range(2):
                    r = slice(i * D_DIM, (i + 1) * D_DIM)
                    for t in range(T):
                        mm = pe.matmul(ps[:, 5 + i, spans[t]], qkT[r, 0, t * P:(t + 1) * P], qkT[r, 1, 0:(t + 1) * P],
                                       start=True, stop=True)
                mm.then_inc(s_ps, 1)
                pe.wait_ge(a_ready, h + 1)
                for n in range(3):
                    mm = pe.transpose(ps[:, 4, n * P:(n + 1) * P], e[:, 0, n * P:(n + 1) * P], m.ident)
                mm.then_inc(aT_ps, 1)
                pe.wait_ge(aT_ready, h + 1)
                if h >= 1:
                    pe.wait_ge(olo, h)
                v = [vt[:, s, h * P:(h + 1) * P] for s in range(T)]
                pe.matmul(ps[:, 7, 0:P], eT[:, 0:P], v[0], start=True, stop=True)
                pe.matmul(ps[:, 7, P:2 * P], eT[:, P:2 * P], v[0], start=True, stop=False)
                pe.matmul(ps[:, 7, P:2 * P], eT[:, 2 * P:], v[1], start=False, stop=True).then_inc(o_ps, 1)
                pe.wait_ge(on_ready, T * (h + 1))
                for t in range(T):
                    mm = pe.transpose(ps[:, 7, SEQ + t * P:SEQ + (t + 1) * P], on[:, t, :], m.ident)
                mm.then_inc(oT_ps, 1)
            pe.wait_ge(olo, D_HEADS)
            for h in range(2):
                for j, g in enumerate(at[f"o{h}"]):
                    dense_granule(pe, st, g, [ps[:, 2 * h + t, :] for t in range(T)], m.xhi, m.xlo, 4 * j, BANK, j == 0, j == 1)

        @block.vector
        def _(dve):
            n_step = [0]

            def link(ins):
                n_step[0] += 1
                ins.then_inc(dve_step, 1)
                dve.wait_ge(dve_step, n_step[0])

            norm_dve(dve, m, use)
            dve.wait_ge(lam_in, 16)
            for i in range(2):
                a = lam_in_[:, 2 * i * D_DIM:(2 * i + 1) * D_DIM]
                b = lam_in_[:, (2 * i + 1) * D_DIM:(2 * i + 2) * D_DIM]
                ins = dve.tensor_tensor_reduce(lamw[:, i * D_DIM:(i + 1) * D_DIM], a, b, 1.0, 0.0, ALU.mult, ALU.add, lam[:, i:i + 1])
            ins.then_inc(lsum_ready, 1)
            for b in range(4):
                dve.wait_ge(xhi_ready, 4 * b + 4)
                for hi, lo, name in ((m.xhi, m.xlo, "bq"), (khi, klo, "kv")):
                    for c in (2 * b, 2 * b + 1):
                        dve.scalar_tensor_tensor(lo[:, c, :], turned_ps(m, NB, c), col(m, name)[:, c:c + 1],
                                                 hi[:, c, :].bitcast(F32), ALU.mult, ALU.subtract).then_inc(xlo_ready, 1)
            dve.wait_ge(lexp_ready, 1)
            link(dve.tensor_tensor(lam[:, 4:5], lam[:, 3:4], lam[:, 2:3], ALU.subtract))
            link(dve.tensor_scalar(lam[:, 5:6], lam[:, 4:5], -LAMBDA_INIT, None, ALU.add))
            dve.tensor_scalar(sub[:, :], col(m, "subln"), 1.0 - LAMBDA_INIT, None, ALU.mult).then_inc(lam_ready, 1)
            dve.wait_ge(lam_ready, 1)
            for h in range(D_HEADS):
                dve.wait_ge(s_ps, h + 1)
                dve.wait_ge(bias_ready, h + 1)
                if h >= 1:
                    dve.wait_ge(aT_ps, h)
                for i in range(2):
                    for t in range(T):
                        ins = dve.tensor_tensor_reduce(e[:, i, spans[t]], ps[:, 5 + i, spans[t]], bias[:, h % 2, spans[t]], 1.0,
                                                       -3e38, ALU.add, ALU.max, mx[:, 0, 2 * i + t:2 * i + t + 1])
                link(ins)
                dve.tensor_scalar(mx[:, 1, :], mx[:, 0, :], -SCALE, None, ALU.mult).then_inc(mx_ready, 1)
                dve.wait_ge(e_ready, 4 * (h + 1))
                link(dve.reciprocal(sm[:, 1, :], sm[:, 0, :]))
                link(dve.tensor_scalar(sm[:, 1, 2:4], sm[:, 1, 2:4], lam[:, 5:6], None, ALU.mult))
                for t in range(T):
                    ins = dve.tensor_scalar(e[:, 0, spans[t]], e[:, 0, spans[t]], sm[:, 1, t:t + 1], None, ALU.mult)
                link(ins)
                for t in range(T):
                    ins = dve.scalar_tensor_tensor(e[:, 0, spans[t]], e[:, 1, spans[t]], sm[:, 1, 2 + t:3 + t], e[:, 0, spans[t]],
                                                   ALU.mult, ALU.add)
                ins.then_inc(a_ready, 1)
                dve.wait_ge(a_ready, h + 1)
                dve.wait_ge(ors_ready, h + 1)
                for t in range(T):
                    dve.tensor_scalar(on[:, t, :], ps[:, 7, t * P:(t + 1) * P], ost[:, 2, t:t + 1], None,
                                      ALU.mult).then_inc(on_ready, 1)
                dve.wait_ge(ohi, h + 1)
                dve.scalar_tensor_tensor(m.xlo[:, h, :], ps[:, 7, SEQ:], sub[:, 0:1], m.xhi[:, h, :].bitcast(F32),
                                         ALU.mult, ALU.subtract).then_inc(olo, 1)
            for h in range(2):
                add_to_x(dve, m, st, at, f"o{h}", [2 * h + t for t in range(T)], h)


def final_norm(nc, m, I, out, use):
    with ExitStack() as ctx:
        gain = ctx.enter_context(nc.sbuf_tensor("sb_final_gain", [P, D], F32))
        gain_in, y_ready = ctx.enter_context(nc.semaphore("final_gain_in")), ctx.enter_context(nc.semaphore("y_ready"))
        block = ctx.enter_context(nc.Block())
        dram = out[0].rearrange("(t p) d -> p t d", p=P)

        @block.sync
        def _(sp):
            sp.dma_start(gain[:, :], I["final_norm_2"].partition_broadcast(P)).then_inc(gain_in, 16)
            for t in range(T):
                sp.wait_ge(y_ready, t + 1)
                sp.dma_start(dram[:, t, :], m.xs[:, t, :]).then_inc(m.out_done, 16)
            sp.wait_ge(m.out_done, 16 * T)

        @block.scalar
        def _(act):
            norm_act(act, m, use)

        @block.gpsimd
        def _(pool):
            norm_pool(pool, m, use)

        @block.vector
        def _(dve):
            dve.wait_ge(m.rstd_ready, use + 1)
            dve.wait_ge(gain_in, 16)
            for t in range(T):
                dve.scalar_tensor_tensor(m.xs[:, t, :], m.x[:, t, :], m.rstd[:, t:t + 1], gain[:, :], ALU.mult,
                                         ALU.mult).then_inc(y_ready, 1)



def program(nc, I, out):
    m = Shared()
    with ExitStack() as ctx:
        def sb(name, shape, dt=F32):
            return ctx.enter_context(nc.sbuf_tensor("sb_" + name, shape, dt))

        def sem(name):
            return ctx.enter_context(nc.semaphore(name))

        m.ps = ctx.enter_context(nc.psum_tensor("ps", [P, 8, BANK], F32))
        m.x, m.xs = sb("x", [P, T, D]), sb("xs", [P, T, D])
        m.sumsq, m.meansq, m.rstd = sb("sumsq", [P, T]), sb("meansq", [P, T]), sb("rstd", [P, T])
        m.consts, m.cols, m.rows = sb("consts", [P, N_CONSTS]), sb("cols", [P, N_COLS]), sb("rows", [P, N_ROWS])
        m.ident, m.half = const(m, "ident"), const(m, "half")
        m.sumsq_ready, m.meansq_ready, m.rstd_ready = sem("sumsq_ready"), sem("meansq_ready"), sem("rstd_ready")
        m.xs_ready, m.xturn_ps, m.out_done = sem("xs_ready"), sem("xturn_ps"), sem("out_done")
        mixer(nc, m, I)
        experts(nc, m, I)
        m.xhi, m.xlo = sb("xhi2", [P, DC, SEQ], F32R), sb("xlo2", [P, DC, SEQ], F32R)
        st, at = second_stream(m, ctx, nc, I)
        gmlp(nc, m, I, st, at, 2)
        swiglu(nc, m, I, st, at, 0, 3)
        diff_attention(nc, m, I, st, at, 4)
        swiglu(nc, m, I, st, at, 1, 5)
        final_norm(nc, m, I, out, 6)


_INS = ["x", "w_in", "w_a_out", "w_b_out", "w_uq", "w_ukv", "w_c_out", "w_out", "w_router", "w_e_gate", "w_e_up",
        "w_e_down", "a_w_in_2", "a_v_norm_2", "a_w_out_2", "ffn_w_gu_2", "ffn_w_down_2", "kv_w_2",
        "b_w_q_2", "b_w_o_2", "final_norm_2"]


def constants():
    import numpy as np

    i = np.arange(P)
    a, b = i[:, None], i[None, :]
    z = np.zeros((P, P))
    ang = (np.arange(SEQ, dtype=np.float32)[:, None]
           * (np.float32(10000.0) ** (-np.arange(0, C_ROPE, 2, dtype=np.float32) / C_ROPE))[None, :])
    turn = lambda y: y.reshape(T, P, 16).transpose(1, 0, 2).reshape(P, T * 16)
    c = {
        "ident": a == b, "upto": a <= b, "from": a >= b, "ones": z + 1,
        "causal": np.concatenate([z, np.where(b <= a, 0, NEG)], 1),
        "anti": np.concatenate([np.where(b >= a, 0, NEG), z], 1),
        "cos": turn(np.cos(ang)), "sin": turn(np.sin(ang)),
        "half": z[:, :8] - 0.5,
    }
    dist = np.concatenate([np.where(b <= a, b - a, NEG), b - a - P, np.where(b <= a, b - a, NEG)], 1)
    late = np.concatenate([dist, z[:, :CAP] + np.arange(1, CAP + 1)], 1)
    sel = np.zeros((8, 8, P), np.float32)
    sel[np.arange(8), np.arange(8)] = 1
    return np.concatenate([c[n] for n in CONSTS], 1).astype(np.float32), sel, late.astype(np.float32)


def arrays_of(inputs):
    import numpy as np

    f = {k: np.asarray(v) for k, v in inputs.items()}
    vec = {"mix": f["mix_norm_g"], "a_norm": f["a_norm_g"], "conv_w": f["conv_w"], "conv_b": f["conv_b"],
           "ln_g": f["conv_ln_g"], "ln_b": f["conv_ln_b"], "cq": f["cq_norm_g"], "ckv": f["ckv_norm_g"],
           "ffn": f["ffn_norm_g"], "gmlp": f["a_norm_2"], "ffn0": f["ffn_norm_2"][0], "ffn1": f["ffn_norm_2"][1],
           "kv": f["kv_norm_2"], "bq": f["b_norm_2"], "b_sp": f["a_b_sp_2"], "subln": f["b_subln_2"]}
    rows = {"b_if": f["b_if"], "q_g": f["q_norm_g"], "k_g": f["k_norm_g"]}
    arrays = {n: np.ascontiguousarray(f[n]) for n in _INS}
    arrays["w_spT"] = np.ascontiguousarray(f["a_w_sp_2"][0].transpose(2, 0, 1))
    arrays["v_cols"] = np.ascontiguousarray(np.concatenate([vec[n].reshape(-1, P).T for n in COLS], 1))
    line = np.concatenate([rows[n].reshape(-1) for n in ROWS])
    arrays["v_rows"] = np.ascontiguousarray(np.broadcast_to(line, (P, N_ROWS)))
    arrays["v_lam"] = np.ascontiguousarray(np.broadcast_to(f["b_lambda_2"].reshape(-1), (P, N_LAM)))
    arrays["c_consts"], arrays["c_sel"], arrays["c_late"] = constants()
    return arrays


def kernel(**inputs):
    import numpy as np
    import concourse.bacc as bacc
    from concourse.bass_utils import run_bass_kernel_spmd

    nc = bacc.Bacc("TRN2", target_bir_lowering=False, num_devices=1)
    arrays = arrays_of(inputs)
    I = {n: nc.dram_tensor(n, a.shape, mybir.dt.from_np(a.dtype), kind="ExternalInput").ap() for n, a in arrays.items()}
    out = nc.dram_tensor("out", (1, SEQ, D), F32, kind="ExternalOutput").ap()
    program(nc, I, out)
    return run_bass_kernel_spmd(nc, [arrays], core_ids=[0]).results[0]["out"]
```

```python
from contextlib import ExitStack

import concourse.bass as bass
from concourse import mybir

F32 = mybir.dt.float32
F32R = mybir.dt.float32r
ALU = mybir.AluOpType
ACT = mybir.ActivationFunctionType
AX = mybir.AxisListType

P = 128
SEQ = 256
T = SEQ // P
D = 1024
DC = D // P
EPS = 1e-6
BANK = 512

A_HEADS, A_DIM = 4, 128
A_W = A_HEADS * A_DIM
B_W, B_TAPS = 512, 31
B_PAD = B_TAPS // 2
C_HEADS, C_NOPE, C_ROPE, C_V = 8, 64, 32, 64
C_QK = C_NOPE + C_ROPE
C_QR, C_KVR = 384, 256
N_EXP, E_FF = 16, 1536
CAP = 2 * SEQ // N_EXP

Z_Q = 0
Z_K = Z_Q + A_W
Z_V = Z_K + A_W
Z_O = Z_V + A_W
Z_G = Z_O + A_W
Z_UA = Z_G + 4 * A_HEADS
Z_UG = Z_UA + B_W
Z_CQ = Z_UG + B_W
Z_CKV = Z_CQ + C_QR
Z_GTS = Z_CKV + C_KVR + C_ROPE

D_FF = 2816
LAMBDA_INIT = 0.8 - 0.6 * 0.7408182206817179
NEG = -1e30

G_GROUPS = 8
D_HEADS, D_DIM, D_V = 8, 64, 128

COLS = {}
_at = 0
for _name, _n in (("mix", DC), ("a_norm", A_HEADS), ("conv_w", B_TAPS * 4), ("conv_b", 4),
                  ("ln_g", 4), ("ln_b", 4), ("cq", C_QR // P), ("ckv", C_KVR // P), ("ffn", DC),
                  ("gmlp", DC), ("ffn0", DC), ("ffn1", DC), ("kv", DC), ("bq", DC),
                  ("b_sp", G_GROUPS), ("subln", 1)):
    COLS[_name] = (_at, _n)
    _at += _n
N_COLS = _at
ROWS = {"b_if": (0, 16), "q_g": (16, C_QK), "k_g": (16 + C_QK, C_QK)}
N_ROWS = 16 + 2 * C_QK
N_LAM = 4 * D_DIM
CONSTS = {}
_at = 0
for _name, _n in (("ident", P), ("half", 8), ("upto", P), ("ones", P), ("from", P), ("causal", 2 * P),
                  ("anti", 2 * P), ("cos", T * 16), ("sin", T * 16)):
    CONSTS[_name] = (_at, _n)
    _at += _n
N_CONSTS = _at


class Shared:
    pass


class Stream:

    def __init__(self, ctx, nc, name, ring, bufs):
        self.ring, self.slots, self.bufs = ring, ring.shape[1], bufs
        self.hi = self.lo = None
        self.landed = [ctx.enter_context(nc.semaphore(f"{name}_landed{i}")) for i in range(self.slots)]
        self.hi_ready = ctx.enter_context(nc.semaphore(f"{name}_hi_ready"))
        self.lo_pool = ctx.enter_context(nc.semaphore(f"{name}_lo_pool"))
        self.lo_dve = ctx.enter_context(nc.semaphore(f"{name}_lo_dve"))
        self.used = ctx.enter_context(nc.semaphore(f"{name}_used"))
        self.pieces, self.arrive, self.lows = [], [], []
        self.n_pool = self.n_dve = 0
        self.slot_sum = [0] * self.slots

    def place_halves(self, ctx, nc, name):
        self.hi = ctx.enter_context(nc.sbuf_tensor(f"{name}_whi", [P, self.bufs, 2048], F32R))
        self.lo = ctx.enter_context(nc.sbuf_tensor(f"{name}_wlo", [P, self.bufs, 2048], F32R))

    def add(self, pieces, by_dve=False):
        g = len(self.pieces)
        self.pieces.append(pieces)
        self.slot_sum[g % self.slots] += 16 * len(pieces)
        self.arrive.append(self.slot_sum[g % self.slots])
        if by_dve:
            self.n_dve += 1
            self.lows.append((self.lo_dve, self.n_dve))
        else:
            self.n_pool += 1
            self.lows.append((self.lo_pool, self.n_pool))
        return g

    def size(self, g):
        return sum(nk * n for _, nk, n, _ in self.pieces[g])

    def load(self, sp, g):
        if g >= self.slots:
            sp.wait_ge(*self.lows[g - self.slots])
        for off, nk, n, src in self.pieces[g]:
            dst = self.ring[:, g % self.slots, off:off + nk * n].rearrange("p (k n) -> p k n", n=n)
            sp.dma_start(dst, src).then_inc(self.landed[g % self.slots], 16)

    def split_hi(self, act, g):
        if g >= len(self.pieces):
            return
        n = self.size(g)
        act.wait_ge(self.landed[g % self.slots], self.arrive[g])
        if g >= self.bufs:
            act.wait_ge(self.used, g - self.bufs + 1)
        act.activation(self.hi[:, g % self.bufs, 0:n], self.ring[:, g % self.slots, 0:n],
                       ACT.Copy).then_inc(self.hi_ready, 1)

    def split_lo(self, eng, g):
        if g >= len(self.pieces):
            return
        n = self.size(g)
        eng.wait_ge(self.hi_ready, g + 1)
        eng.tensor_tensor(self.lo[:, g % self.bufs, 0:n], self.ring[:, g % self.slots, 0:n],
                          self.hi[:, g % self.bufs, 0:n].bitcast(F32),
                          ALU.subtract).then_inc(self.lows[g][0], 1)

    def views(self, g, n):
        nk = self.size(g) // n
        return [x[:, g % self.bufs, 0:nk * n].rearrange("p (k n) -> p k n", n=n) for x in (self.hi, self.lo)]


def three_products(pe, out, hi, lo, whi, wlo, start, stop):
    pe.matmul(out, hi, whi, start=start, stop=False)
    pe.matmul(out, hi, wlo, start=False, stop=False)
    return pe.matmul(out, lo, whi, start=False, stop=stop)


def dense_granule(pe, st, g, outs, hi, lo, k0, n, first, last, turned=None, part=None):
    whi, wlo = st.views(g, n)
    nk = whi.shape[1]
    begin, end = {None: (0, nk), 0: (0, nk // 2), 1: (nk // 2, nk)}[part]
    if begin == 0:
        pe.wait_ge(*st.lows[g])
    for k in range(begin, end):
        if turned is not None:
            pe.wait_ge(turned[0], turned[1][k0 + k])
        for t in range(T):
            mm = three_products(pe, outs[t], hi[:, k0 + k, t * P:(t + 1) * P], lo[:, k0 + k, t * P:(t + 1) * P],
                                whi[:, k, :], wlo[:, k, :], first and k == 0, last and k == nk - 1)
    if end == nk:
        mm.then_inc(st.used, 1)



def norm_act(act, m, n):
    for t in range(T):
        act.activation(m.xs[:, t, :], m.x[:, t, :], ACT.Square,
                       accum_out=m.sumsq[:, t:t + 1]).then_inc(m.sumsq_ready, 1)


def norm_pool(pool, m, n):
    pool.wait_ge(m.sumsq_ready, T * (n + 1))
    pool.tensor_scalar(m.meansq[:, :], m.sumsq[:, :], 1.0 / D, EPS, ALU.mult, ALU.add).then_inc(m.meansq_ready, 1)
    pool.wait_ge(m.meansq_ready, n + 1)
    pool.tensor_tensor(m.rstd[:, :], m.meansq[:, :], m.half[:, 0:T], ALU.pow).then_inc(m.rstd_ready, 1)


def turn_tokens(pe, m, src, banks):
    for b in range(DC // 2):
        for cc in range(2):
            for t in range(T):
                c = 2 * b + cc
                mm = pe.transpose(m.ps[:, banks[b], cc * SEQ + t * P:cc * SEQ + (t + 1) * P],
                                  src[:, t, c * P:(c + 1) * P], m.ident)
        mm.then_inc(m.xturn_ps, 1)


def turned_ps(m, banks, c):
    return m.ps[:, banks[c // 2], (c % 2) * SEQ:(c % 2 + 1) * SEQ]


def norm_hi_act(act, m, n, banks, hi, gain, ready, base):
    for c in range(DC):
        act.wait_ge(m.xturn_ps, (DC // 2) * n + c // 2 + 1)
        act.activation(hi[:, c, :], turned_ps(m, banks, c), ACT.Copy, scale=gain[:, c:c + 1]).then_inc(ready, 1)


def norm_lo_dve(dve, m, n, banks, hi, lo, gain, hi_ready, lo_ready, base):
    for c in range(DC):
        dve.wait_ge(hi_ready, base + 2 * (c // 2) + 2)
        dve.scalar_tensor_tensor(lo[:, c, :], turned_ps(m, banks, c), gain[:, c:c + 1],
                                 hi[:, c, :].bitcast(F32), ALU.mult, ALU.subtract).then_inc(lo_ready, 1)


def chunks(w, k0, nk, n0, n):
    return w[k0 * P:(k0 + nk) * P, n0:n0 + n].rearrange("(k p) n -> p k n", p=P)


def col(m, name):
    a, n = COLS[name]
    return m.cols[:, a:a + n]


def row(m, name):
    a, n = ROWS[name]
    return m.rows[:, a:a + n]


def const(m, name):
    a, n = CONSTS[name]
    return m.consts[:, a:a + n]



def mixer(nc, m, I):
    with ExitStack() as ctx:
        def sb(name, shape, dt=F32):
            return ctx.enter_context(nc.sbuf_tensor("sb_" + name, shape, dt))

        def sem(name):
            return ctx.enter_context(nc.semaphore(name))

        ring = sb("mix_ring", [P, 3, 2048])
        st = Stream(ctx, nc, "mix", ring[:, :, :], 2)
        st.place_halves(ctx, nc, "mix")
        ps = m.ps

        blocks = {}

        def dense(name, w, k_chunks, per, n0, n, by_dve=False):
            blocks[name] = [(st.add([(0, per, n, chunks(w, k, per, n0, n))], by_dve), k, per, n)
                            for k in range(0, k_chunks, per)]

        w_in = I["w_in"][0]
        dense("cq", w_in, DC, 4, Z_CQ, C_QR, True)
        dense("ckv", w_in, DC, 4, Z_CKV, C_KVR + C_ROPE, True)
        dense("g", w_in, DC, 8, Z_G, 4 * A_HEADS, True)
        dense("ug", w_in, DC, 4, Z_UG, B_W, True)
        dense("ua", w_in, DC, 4, Z_UA, B_W, True)
        for j in range(2):
            dense(f"uq{j}", I["w_uq"][0], C_QR // P, 3, j * 384, 384)
        for j in range(2):
            dense(f"ukv{j}", I["w_ukv"][0], C_KVR // P, 2, j * 512, 512)
        for name, n0 in (("q", Z_Q), ("k", Z_K), ("v", Z_V), ("o", Z_O)):
            dense(name, w_in, DC, 4, n0, A_W)
        for j in range(6):
            dense(f"gt{j}", w_in, DC, 4, Z_GTS + j * 512, 512)
        for br, w in (("a", I["w_a_out"][0]), ("b", I["w_b_out"][0]), ("c", I["w_c_out"][0])):
            for h in range(2):
                dense(f"y{br}{h}", w, 4, 4, h * 512, 512)
        for h in range(2):
            dense(f"out{h}", I["w_out"][0], DC, 4, h * 512, 512)
        order = list(blocks)
        n_gran = len(st.pieces)

        used_up = [0]

        def early(*shape):
            n = 1
            for d in shape[1:]:
                n *= d
            view = m.ring[:, used_up[0]:used_up[0] + n]
            used_up[0] += n
            dims = " ".join(f"d{i}" for i in range(len(shape) - 1))
            sizes = {f"d{i}": shape[1 + i] for i in range(1, len(shape) - 1)}
            return view.rearrange(f"p ({dims}) -> p {dims}", **sizes)

        m.sel = sb("sel", [8, 8, P])
        xhi, xlo = sb("xhi", [P, DC, SEQ], F32R), sb("xlo", [P, DC, SEQ], F32R)
        gates = sb("gates", [P, T, 2, 2, A_HEADS])
        fabs = sb("fabs", [P, T * 2 * A_HEADS])
        fexp = sb("fexp", [P, T * 2 * A_HEADS])
        logf = sb("logf", [P, T, 2, A_HEADS])
        fcum = sb("fcum", [P, A_HEADS, 2, T])
        ir = sb("ir", [P, T, 2, A_HEADS])
        irow = sb("irow", [2 * A_HEADS, SEQ])
        merged = m.xs
        flat = m.xs[:, :, :].rearrange("p t d -> p (t d)")
        cq = flat[:, 0:T * C_QR].rearrange("p (t n) -> p t n", t=T)
        ckv = flat[:, T * C_QR:T * (C_QR + C_KVR + C_ROPE)].rearrange("p (t n) -> p t n", t=T)
        cstat, crstd = sb("cstat", [P, 4]), sb("crstd", [P, 4])
        csum = sb("csum", [P, 4])
        chi, clo = sb("chi", [P, 5, SEQ], F32R), sb("clo", [P, 5, SEQ], F32R)
        u = sb("u", [P, T, B_W])
        o_gate = early(P, T, A_W)
        qtok, ktok, vtok = early(P, T, A_W), early(P, T, A_W), early(P, T, A_W)
        upad = early(P, 4, SEQ + 2 * B_PAD)
        conv = sb("conv", [P, 4, SEQ])
        scale_q, scale_gt = sb("scale_q", [P, T]), sb("scale_gt", [P, T])
        bst, bmv, brstd = sb("bst", [P, T, 6]), sb("bmv", [P, T, 2]), sb("brstd", [P, T])
        bvar = sb("bvar", [P, T])
        gt = sb("gt", [P, T, 3, D])
        qh, kv = early(P, T, C_HEADS, C_QK), early(P, T, C_HEADS, C_NOPE + C_V)
        kh = early(P, T, C_HEADS, C_QK)
        hss, hrs = sb("hss", [P, 2, T, C_HEADS]), sb("hrs", [P, 2, T, C_HEADS])
        hms, krss = sb("hms", [P, 2, T, C_HEADS]), sb("krss", [P, T])
        yhi = [sb("yahi", [P, 4, SEQ], F32R), xhi, chi]
        ylo = [sb("yalo", [P, 4, SEQ], F32R), xlo, clo]
        qkT = sb("qkT", [P, 2, SEQ])
        decay = sb("decay", [P, 6 * P])
        smat = decay
        amat, amatT = sb("amat", [P, T, SEQ]), sb("amatT", [P, T, SEQ])
        mx, den, mstat = sb("mx", [P, 4]), sb("den", [P, 4]), sb("mstat", [P, 4, 4])
        hst = sb("hst", [P, 3, T])
        hn = early(P, T, A_DIM)
        cT = early(P, 2, SEQ)[0:C_QK]
        pr, prT = early(P, T, SEQ), early(P, T, SEQ)
        cmx, csm = sb("cmx", [P, 2, T]), sb("csm", [P, 2, T])
        ytmp = u
        rope = u[:, :, :].rearrange("p t (i h f) -> p t i h f", i=4, f=16)
        silu = conv
        xscr = smat
        hscr = hn
        gflat = gt[:, :, :, :].rearrange("p t b d -> p (t b d)")
        qsq = gflat[:, 0:T * C_HEADS * C_QK].rearrange("p (t h d) -> p t h d", t=T, h=C_HEADS)
        xsq = gflat[:, 2048:2048 + T * C_HEADS * C_NOPE].rearrange("p (t h d) -> p t h d", t=T, h=C_HEADS)
        parts = [(0, P), (P, 2 * P), (3 * P, 2 * P), (5 * P, P)]

        x_in, const_in, rows_in, scale_ready = sem("x_in"), sem("const_in"), sem("rows_in"), sem("scale_ready")
        xhi_ready, xlo_ready = sem("xhi_ready"), sem("xlo_ready")
        dve_step, act_step, pool_step = sem("mix_dve_step"), sem("mix_act_step"), sem("mix_pool_step")
        z_act, z_dve = sem("z_act"), sem("z_dve")
        gates_ready, fabs_ready, fexp_ready, logl_ready = (sem(s) for s in ("gates_ready", "fabs_ready", "fexp_ready", "logl_ready"))
        logf_ready, fcum_ps, ir_ready, irow_ps, irow_ready = (
            sem(s) for s in ("logf_ready", "fcum_ps", "ir_ready", "irow_ps", "irow_ready"))
        csum_ready, crstd_ready, cnorm_ready, cturn_ps, chi_ready, clo_ready = (
            sem(s) for s in ("csum_ready", "crstd_ready", "cnorm_ready", "cturn_ps", "chi_ready", "clo_ready"))
        pad_ready, u_ready, uturn_ps, upad_ready, conv_step = (
            sem(s) for s in ("pad_ready", "u_ready", "uturn_ps", "upad_ready", "conv_step"))
        ctok_ps, bvar_ready, brstd_ready, bn_ready, bturn_ps, silu_ready, ybhi, yblo = (
            sem(s) for s in ("ctok_ps", "bvar_ready", "brstd_ready", "bn_ready", "bturn_ps", "silu_ready", "ybhi", "yblo"))
        hss_ready, hrs_ready, ckh_ready = (sem(s) for s in ("hss_ready", "hrs_ready", "ckh_ready"))
        qk_ps, qkT_ready, ib_ps, mneg_ready, decay_ready, emt_ready, score_ps, amat_ready, amT_ps, amT_ready, h_ps, hsum_ready, hrstd_ready, hn_ready, hturn_ps, yahi, yalo = (
            sem(s) for s in ("qk_ps", "qkT_ready", "ib_ps", "mneg_ready", "decay_ready", "emt_ready", "score_ps",
                             "amat_ready", "amT_ps", "amT_ready", "h_ps", "hsum_ready", "hrstd_ready", "hn_ready",
                             "hturn_ps", "yahi", "yalo"))
        cqk_ps, cT_ready, cs_ps, cmx_ready, cexp_ready, pr_ready, prT_ps, prT_ready, co_ps, ychi, yclo = (
            sem(s) for s in ("cqk_ps", "cT_ready", "cs_ps", "cmx_ready", "cexp_ready", "pr_ready", "prT_ps",
                             "prT_ready", "co_ps", "ychi", "yclo"))
        y_read, merged_ready, mturn_ps, x1_ready = (sem(s) for s in ("y_read", "merged_ready", "mturn_ps", "x1_ready"))
        m.mixer_sems = range(st.landed[0].num, x1_ready.num + 1)

        steps = []

        def gran(name, *between):
            for i in range(len(blocks[name])):
                steps.append(("gran", (name, i, None)))
                if i == 0:
                    steps.extend(between)
            steps.append(("evac", name))

        def halves(names):
            out = []
            for name in names:
                for i in range(len(blocks[name])):
                    out += [[("gran", (name, i, 0))], [("gran", (name, i, 1))]]
                out[-1].append(("evac", name))
            return out

        taps = [("conv", tap) for tap in range(B_TAPS)]
        gran("cq")
        gran("ckv")
        steps.append(("cnorm", 0))
        gran("g")
        gran("ug", ("gate1", 0))
        steps.append(("cturn", 0))
        gran("ua", ("gate2", 0))
        steps.append(("gate3", 0))
        gran("uq0")
        steps.append(("uturn", 0))
        for name in ("uq1", "ukv0", "ukv1"):
            gran(name)
            steps.append(taps.pop(0))
        steps.append(("chead", 0))
        fill = halves(["q", "k", "v", "o"] + [f"gt{j}" for j in range(6)] + [f"y{br}{h}" for br in "abc" for h in range(2)])
        c_side = [x for h in range(C_HEADS) for x in ([("c1", h)], [("c2", h), ("c2b", h)], [("c3", h)], [("c4", h)])]
        m_side = [x for h in range(A_HEADS) for x in ([("m1", h)], [("m2", h)], [("m3", h)], [("m4", h), ("m4b", h)], [("m5", h)])]
        m_side += [[("b1", 0), ("b2", 0)], [("b3", 0)], [("b4", 0)]]
        C_START, M_START, TAP_START = 9, 13, 6
        for i, half in enumerate(fill):
            need = {"ya": 5 * A_HEADS, "yb": 5 * A_HEADS + 3}.get(half[0][1][0][:2], 0)
            while 23 - len(m_side) < need:
                steps += m_side.pop(0)
            while half[0][1][0][:2] == "yc" and c_side:
                steps += c_side.pop(0)
            steps += half
            c_now = c_side.pop(0) if i >= C_START and c_side else []
            held = m_side and (m_side[0][0][0] == "b1" and taps or m_side[0][0][0] == "b4" and half[0][1][0][0] != "y")
            m_now = m_side.pop(0) if i >= M_START and m_side and not held else []
            steps += c_now[:1] + m_now[:1]
            if i >= TAP_START and taps:
                steps.append(taps.pop(0))
            steps += c_now[1:] + m_now[1:]
        steps.append(("mturn", 0))
        gran("out0", ("mturn", 1))
        gran("out1")

        parity = {name: i % 2 for i, name in enumerate(order)}

        def zbanks(name):
            return [2 * parity[name] + t for t in range(T)]

        def last_gran(name):
            return blocks[name][-1][0]

        by_dve = {"g"} | {f"y{b}{h}" for b in "abc" for h in range(2)} | {"out0", "out1"}
        evac_at, na, nd = {}, 0, 0
        for name in order:
            if name in by_dve:
                nd += 1
                evac_at[name] = (z_dve, nd)
            elif name == "ua":
                evac_at[name] = (u_ready, T)
            else:
                na += 1
                evac_at[name] = (z_act, na)

        SA, SB, SC, SD = 4, 5, 6, 7
        NB4 = [4, 5, 6, 7]
        lookahead = 2

        def cslot(c):
            return ps[:, (SA, SA, SC, SC, SD)[c], (c % 2) * SEQ:(c % 2 + 1) * SEQ]

        gran_steps = [blocks[v[0]][v[1]][0] for s, v in steps if s == "gran" and v[2] != 0]
        assert gran_steps == list(range(n_gran))

        def sq(t):
            return slice(t * P, (t + 1) * P)

        block = ctx.enter_context(nc.Block())

        @block.sync
        def _(sp):
            sp.dma_start(m.x[:, :, :], I["x"][0].rearrange("(t p) d -> p t d", p=P)).then_inc(x_in, 16)
            for g in range(n_gran):
                st.load(sp, g)
                if g == n_gran - 2:
                    sp.wait_ge(yalo, A_HEADS)
                    sp.wait_ge(yclo, C_HEADS)
                    sp.wait_ge(conv_step, 4 * B_TAPS)
                    load_expert(sp, m, I, 0, 0)
            for i in range(1, EARLY):
                load_expert(sp, m, I, 0, i)

        @block.scalar
        def _(act):
            first = P + 8
            act.dma_start(m.consts[:, 0:first], I["c_consts"][:, 0:first]).then_inc(const_in, 16)
            act.dma_start(m.cols[:, :], I["v_cols"]).then_inc(const_in, 16)
            act.dma_start(m.consts[:, first:], I["c_consts"][:, first:]).then_inc(rows_in, 16)
            act.dma_start(m.rows[:, :], I["v_rows"]).then_inc(rows_in, 16)
            act.dma_start(m.sel[:, :, :], I["c_sel"]).then_inc(rows_in, 16)
            act_n = [0]
            st.split_hi(act, 0)
            act.wait_ge(const_in, 32)
            norm_hi_act(act, m, 0, NB4, xhi, col(m, "mix"), xhi_ready, 0)
            for g in range(1, lookahead):
                st.split_hi(act, g)
            norm_act(act, m, 0)
            act.wait_ge(scale_ready, 1)
            act.wait_ge(m.sumsq_ready, T)

            for what, v in steps:
                if what == "gran":
                    if v[2] != 0:
                        st.split_hi(act, blocks[v[0]][v[1]][0] + lookahead)
                elif what == "evac" and v not in by_dve and v != "ua":
                    b = zbanks(v)
                    n = blocks[v][0][3]
                    act.wait_ge(st.used, last_gran(v) + 1)
                    if v in ("cq", "ckv"):
                        i = 0 if v == "cq" else 2
                        w = C_QR if v == "cq" else C_KVR
                        dst = cq if v == "cq" else ckv
                        for t in range(T):
                            act.activation(xscr[:, 0:w], ps[:, b[t], 0:w], ACT.Square, scale=m.rstd[:, t:t + 1],
                                           accum_out=csum[:, i + t:i + t + 1]).then_inc(act_step, 1)
                            act_n[0] += 1
                            act.wait_ge(act_step, act_n[0])
                        for t in range(T):
                            ins = act.activation(dst[:, t, :], ps[:, b[t], 0:n], ACT.Copy, scale=m.rstd[:, t:t + 1])
                            ins.then_inc(csum_ready if t == 0 else z_act, 1)
                    else:
                        if v == "q":
                            dsts, f, s = [qtok[:, t, :] for t in range(T)], ACT.Copy, scale_q
                        elif v == "k":
                            dsts, f, s = [ktok[:, t, :] for t in range(T)], ACT.Copy, m.rstd
                        elif v == "v":
                            dsts, f, s = [vtok[:, t, :] for t in range(T)], ACT.Copy, m.rstd
                        elif v == "ug":
                            dsts, f, s = [u[:, t, :] for t in range(T)], ACT.Sigmoid, m.rstd
                        elif v == "o":
                            dsts, f, s = [o_gate[:, t, :] for t in range(T)], ACT.Sigmoid, m.rstd
                        elif v[0] == "u":
                            j, q = int(v[-1]), v[:2] == "uq"
                            hs = slice(4 * j, 4 * j + 4)
                            dsts, f, s = [(qh if q else kv)[:, t, hs, :].rearrange("p h d -> p (h d)") for t in range(T)], ACT.Copy, None
                        else:
                            j = int(v[2])
                            act.wait_ge(hss_ready, 1)
                            dsts = [gt[:, t, j // 2, (j % 2) * BANK:(j % 2 + 1) * BANK] for t in range(T)]
                            f, s = ACT.Tanh, scale_gt
                        for t in range(T):
                            ins = act.activation(dsts[t], ps[:, b[t], 0:n], f, scale=1.0 if s is None else s[:, t:t + 1])
                        ins.then_inc(z_act, 1)
                elif what == "gate1":
                    act.wait_ge(fabs_ready, 1)
                    act.activation(fexp[:, :], fabs[:, :], ACT.Exp, scale=-1.0).then_inc(fexp_ready, 1)
                    act.wait_ge(fexp_ready, 1)
                    act.activation(fabs[:, :], fexp[:, :], ACT.Ln, bias=1.0).then_inc(logl_ready, 1)
                elif what == "cturn":
                    for c in range(5):
                        act.wait_ge(cturn_ps, 1)
                        gain = (col(m, "cq")[:, c:c + 1] if c < 3 else col(m, "ckv")[:, c - 3:c - 2])
                        act.activation(chi[:, c, :], cslot(c), ACT.Copy, scale=gain).then_inc(chi_ready, 1)
                elif what == "uturn":
                    act.wait_ge(pad_ready, 1)
                    act.wait_ge(uturn_ps, 1)
                    for c in range(4):
                        act.activation(upad[:, c, B_PAD:B_PAD + SEQ],
                                       ps[:, (SC, SD)[c // 2], (c % 2) * SEQ:(c % 2 + 1) * SEQ],
                                       ACT.Copy).then_inc(upad_ready, 1)
                elif what == "m1":
                    act.wait_ge(qk_ps, v + 1)
                    act.activation(qkT[:, :, :].rearrange("p a s -> p (a s)"), ps[:, SA, :], ACT.Copy).then_inc(qkT_ready, 1)
                    act.wait_ge(mneg_ready, v + 1)
                    for j, (a, n) in enumerate(parts):
                        ins = act.activation(decay[:, a:a + n], decay[:, a:a + n], ACT.Exp, bias=mstat[:, 0, j:j + 1])
                    ins.then_inc(decay_ready, 1)
                    act.activation(mstat[:, 2, :], mstat[:, 1, :], ACT.Exp, scale=-1.0).then_inc(emt_ready, 1)
                elif what == "m3":
                    act.wait_ge(amT_ps, v + 1)
                    act.activation(amatT[:, :, :].rearrange("p a s -> p (a s)"), ps[:, SB, :], ACT.Copy).then_inc(amT_ready, 1)
                elif what == "m4":
                    act.wait_ge(h_ps, v + 1)
                    for t in range(T):
                        act.activation(hscr[:, t, :], ps[:, SA, sq(t)], ACT.Square,
                                       accum_out=hst[:, 0, t:t + 1]).then_inc(hsum_ready, 1)
                elif what == "m5":
                    act.wait_ge(hturn_ps, v + 1)
                    act.activation(yhi[0][:, v, :], ps[:, SA, SEQ:2 * SEQ], ACT.Copy,
                                   scale=col(m, "a_norm")[:, v:v + 1]).then_inc(yahi, 1)
                elif what == "c1":
                    act.wait_ge(cqk_ps, v + 1)
                    act.activation(cT[:, :, :].rearrange("p a s -> p (a s)"), ps[0:C_QK, SC, :], ACT.Copy).then_inc(cT_ready, 1)
                elif what == "c2":
                    act.wait_ge(cmx_ready, v + 1)
                    for t in range(T):
                        ins = act.activation(pr[:, t, :], ps[:, SD, t * SEQ:(t + 1) * SEQ], ACT.Exp,
                                             bias=cmx[:, 1, t:t + 1], scale=float(C_QK) ** -0.5,
                                             accum_out=csm[:, 0, t:t + 1])
                    ins.then_inc(cexp_ready, 1)
                elif what == "c3":
                    act.wait_ge(prT_ps, v + 1)
                    act.activation(prT[:, :, :].rearrange("p a s -> p (a s)"), ps[:, SC, :], ACT.Copy).then_inc(prT_ready, 1)
                elif what == "c4":
                    r = slice(64 * (v % 2), 64 * (v % 2) + 64)
                    act.wait_ge(co_ps, v + 1)
                    act.activation(yhi[2][r, v // 2, :], ps[r, SD, 0:SEQ], ACT.Copy).then_inc(ychi, 1)
                elif what == "b4":
                    act.wait_ge(bturn_ps, 1)
                    act.wait_ge(ctok_ps, 1)
                    for c in range(4):
                        act.activation(silu[:, c, :], ps[:, (SA, SB)[c // 2], (c % 2) * SEQ:(c % 2 + 1) * SEQ], ACT.Silu,
                                       bias=col(m, "ln_b")[:, c:c + 1],
                                       scale=col(m, "ln_g")[:, c:c + 1]).then_inc(silu_ready, 1)
                    act.wait_ge(st.used, last_gran("gt5") + 1)
                    for c in range(4):
                        act.wait_ge(silu_ready, c + 1)
                        act.activation(yhi[1][:, c, :], silu[:, c, :], ACT.Copy).then_inc(ybhi, 1)
                elif what == "mturn":
                    for c in range(4 * v, 4 * v + 4):
                        act.wait_ge(mturn_ps, c // 2 + 1)
                        act.activation(xhi[:, c, :], turned_ps(m, [SA, SB, SC, SD], c), ACT.Copy,
                                       scale=0.5).then_inc(xhi_ready, 1)

        @block.tensor
        def _(pe):
            pe.wait_ge(const_in, 32)
            pe.wait_ge(x_in, 16)
            turn_tokens(pe, m, m.x, NB4)
            for what, v in steps:
                if what == "gran":
                    name, i, part = v
                    g, k0, nk, n = blocks[name][i]
                    b = zbanks(name)
                    if i == 0 and part != 1:
                        at = order.index(name)
                        if at >= 2:
                            pe.wait_ge(*evac_at[order[at - 2]])
                    hi, lo, kk = xhi, xlo, k0
                    if name[:2] == "uq":
                        hi, lo = chi, clo
                        pe.wait_ge(clo_ready, 3)
                    elif name[:3] == "ukv":
                        hi, lo, kk = chi, clo, 3
                        pe.wait_ge(clo_ready, 5)
                    elif name[0] == "y":
                        br = "abc".index(name[1])
                        hi, lo = yhi[br], ylo[br]
                        pe.wait_ge((yalo, yblo, yclo)[br], (A_HEADS, 4, C_HEADS)[br])
                    turned = {"cq": (xlo_ready, range(1, DC + 1)), "out0": (xlo_ready, range(DC + 1, 2 * DC + 1))}.get(name)
                    dense_granule(pe, st, g, [ps[:, b[t], 0:n] for t in range(T)], hi, lo, kk, n,
                                  i == 0, i == len(blocks[name]) - 1, turned, part)
                elif what == "gate2":
                    pe.wait_ge(rows_in, 48)
                    pe.wait_ge(logf_ready, 1)
                    for d, tri in ((0, const(m, "upto")), (1, const(m, "from"))):
                        for t in range(T):
                            out = ps[:, SB, (d * T + t) * A_HEADS:(d * T + t + 1) * A_HEADS]
                            other = (t == 1) if d == 0 else (t == 0)
                            mm = pe.matmul(out, tri, logf[:, t, d, :], start=True, stop=not other)
                            if other:
                                mm = pe.matmul(out, const(m, "ones"), logf[:, 1 - t, d, :], start=False, stop=True)
                    mm.then_inc(fcum_ps, 1)
                elif what == "gate3":
                    pe.wait_ge(ir_ready, 1)
                    for t in range(T):
                        mm = pe.transpose(ps[0:2 * A_HEADS, SB, SEQ + t * P:SEQ + (t + 1) * P],
                                          ir[:, t, :, :].rearrange("p d h -> p (d h)"), m.ident)
                    mm.then_inc(irow_ps, 1)
                elif what == "cturn":
                    pe.wait_ge(cnorm_ready, 2 * T)
                    for c in range(5):
                        for t in range(T):
                            src = cq[:, t, c * P:(c + 1) * P] if c < 3 else ckv[:, t, (c - 3) * P:(c - 2) * P]
                            mm = pe.transpose(cslot(c)[:, t * P:(t + 1) * P], src, m.ident)
                    mm.then_inc(cturn_ps, 1)
                elif what == "uturn":
                    pe.wait_ge(u_ready, T)
                    pe.wait_ge(clo_ready, 5)
                    for c in range(4):
                        for t in range(T):
                            mm = pe.transpose(ps[:, (SC, SD)[c // 2], (c % 2) * SEQ + t * P:(c % 2) * SEQ + (t + 1) * P],
                                              u[:, t, c * P:(c + 1) * P], m.ident)
                    mm.then_inc(uturn_ps, 1)
                elif what == "m1":
                    if v == 0:
                        pe.wait_ge(*evac_at["q"])
                        pe.wait_ge(*evac_at["k"])
                        pe.wait_ge(irow_ready, 1)
                        pe.wait_ge(clo_ready, 5)
                    else:
                        pe.wait_ge(yalo, v)
                    for a, src in ((0, qtok), (1, ktok)):
                        for t in range(T):
                            mm = pe.transpose(ps[:, SA, a * SEQ + t * P:a * SEQ + (t + 1) * P],
                                              src[:, t, v * P:(v + 1) * P], m.ident)
                    mm.then_inc(qk_ps, 1)
                    if v >= 1:
                        pe.wait_ge(amT_ready, v)
                    for d in range(2):
                        mm = pe.matmul(ps[:, SB, d * SEQ:(d + 1) * SEQ], m.sel[:, d * A_HEADS + v, :], irow[:, :],
                                       start=True, stop=True)
                    mm.then_inc(ib_ps, 1)
                elif what == "m2":
                    pe.wait_ge(qkT_ready, v + 1)
                    for t in range(T):
                        mm = pe.matmul(ps[:, SA, t * SEQ:(t + 1) * SEQ], qkT[:, 0, sq(t)], qkT[:, 1, :],
                                       start=True, stop=True)
                    mm.then_inc(score_ps, 1)
                elif what == "m3":
                    pe.wait_ge(amat_ready, v + 1)
                    for s in range(T):
                        for t in range(T):
                            mm = pe.transpose(ps[:, SB, s * SEQ + t * P:s * SEQ + (t + 1) * P], amat[:, t, sq(s)], m.ident)
                    mm.then_inc(amT_ps, 1)
                elif what == "m4":
                    if v == 0:
                        pe.wait_ge(*evac_at["v"])
                    pe.wait_ge(amT_ready, v + 1)
                    for t in range(T):
                        for s in range(T):
                            mm = pe.matmul(ps[:, SA, sq(t)], amatT[:, s, sq(t)], vtok[:, s, v * P:(v + 1) * P],
                                           start=s == 0, stop=s == T - 1)
                    mm.then_inc(h_ps, 1)
                elif what == "m5":
                    pe.wait_ge(hn_ready, T * (v + 1))
                    for t in range(T):
                        mm = pe.transpose(ps[:, SA, SEQ + t * P:SEQ + (t + 1) * P], hn[:, t, :], m.ident)
                    mm.then_inc(hturn_ps, 1)
                elif what == "c1":
                    if v == 0:
                        pe.wait_ge(ckh_ready, 2)
                        pe.wait_ge(upad_ready, 4)
                    else:
                        pe.wait_ge(prT_ready, v)
                    for a, src in ((0, qh), (1, kh)):
                        for t in range(T):
                            mm = pe.transpose(ps[0:C_QK, SC, a * SEQ + t * P:a * SEQ + (t + 1) * P], src[:, t, v, :], m.ident)
                    mm.then_inc(cqk_ps, 1)
                elif what == "c2":
                    pe.wait_ge(cT_ready, v + 1)
                    if v >= 1:
                        pe.wait_ge(yclo, v)
                    for t in range(T):
                        mm = pe.matmul(ps[:, SD, t * SEQ:(t + 1) * SEQ], cT[:, 0, sq(t)], cT[:, 1, :], start=True, stop=True)
                    mm.then_inc(cs_ps, 1)
                elif what == "c3":
                    pe.wait_ge(pr_ready, v + 1)
                    for s in range(T):
                        for t in range(T):
                            mm = pe.transpose(ps[:, SC, s * SEQ + t * P:s * SEQ + (t + 1) * P], pr[:, t, sq(s)], m.ident)
                    mm.then_inc(prT_ps, 1)
                elif what == "c4":
                    pe.wait_ge(prT_ready, v + 1)
                    r = slice(64 * (v % 2), 64 * (v % 2) + 64)
                    for s in range(T):
                        mm = pe.matmul(ps[r, SD, 0:SEQ], kv[:, s, v, C_NOPE:], prT[:, s, :], start=s == 0, stop=s == T - 1)
                    mm.then_inc(co_ps, 1)
                elif what == "b1":
                    pe.wait_ge(conv_step, 4 * B_TAPS)
                    pe.wait_ge(yalo, A_HEADS)
                    pe.wait_ge(amT_ready, A_HEADS)
                    for t in range(T):
                        for c in range(4):
                            mm = pe.transpose(ps[:, (SA, SB)[t], c * P:(c + 1) * P], conv[:, c, sq(t)], m.ident)
                    mm.then_inc(ctok_ps, 1)
                elif what == "b4":
                    pe.wait_ge(bn_ready, T)
                    for c in range(4):
                        for t in range(T):
                            mm = pe.transpose(ps[:, (SA, SB)[c // 2], (c % 2) * SEQ + t * P:(c % 2) * SEQ + (t + 1) * P],
                                              u[:, t, c * P:(c + 1) * P], m.ident)
                    mm.then_inc(bturn_ps, 1)
                elif what == "mturn":
                    pe.wait_ge(merged_ready, v + 1)
                    pe.wait_ge(yclo, C_HEADS)
                    pe.wait_ge(silu_ready, 4)
                    banks = [SA, SB, SC, SD]
                    for b in (2 * v, 2 * v + 1):
                        for cc in range(2):
                            for t in range(T):
                                c = 2 * b + cc
                                mm = pe.transpose(ps[:, banks[b], cc * SEQ + t * P:cc * SEQ + (t + 1) * P],
                                                  merged[:, t, c * P:(c + 1) * P], m.ident)
                        mm.then_inc(mturn_ps, 1)

        @block.vector
        def _(dve):
            n_step = [0]

            def link(ins):
                n_step[0] += 1
                ins.then_inc(dve_step, 1)
                dve.wait_ge(dve_step, n_step[0])

            dve.memset(upad[:, :, 0:B_PAD], 0.0)
            dve.memset(upad[:, :, B_PAD + SEQ:], 0.0).then_inc(pad_ready, 1)
            st.split_lo(dve, 0)
            dve.wait_ge(const_in, 32)
            norm_lo_dve(dve, m, 0, NB4, xhi, xlo, col(m, "mix"), xhi_ready, xlo_ready, 0)

            for g in range(1, lookahead):
                st.split_lo(dve, g)
            dve.wait_ge(m.rstd_ready, 1)
            dve.wait_ge(rows_in, 48)

            for what, v in steps:
                if what == "gran":
                    g = blocks[v[0]][v[1]][0] + lookahead
                    if v[2] != 0 and g < n_gran and st.lows[g][0] is st.lo_dve:
                        st.split_lo(dve, g)
                elif what == "evac" and v[0] == "u" and v[1] in "qk":
                    dve.wait_ge(*evac_at[v])
                    hs, q = slice(4 * int(v[-1]), 4 * int(v[-1]) + 4), v[:2] == "uq"
                    for t in range(T):
                        src = qh[:, t, hs, :] if q else kv[:, t, hs, 0:C_NOPE]
                        ins = dve.tensor_tensor((qsq if q else xsq)[:, t, hs, :], src, src, ALU.mult)
                    link(ins)
                    for t in range(T):
                        ins = dve.tensor_reduce(hss[:, 0 if q else 1, t, hs], (qsq if q else xsq)[:, t, hs, :], AX.X, ALU.add)
                    link(ins)
                elif what == "evac" and (v in by_dve or v == "ua"):
                    b = zbanks(v)
                    dve.wait_ge(st.used, last_gran(v) + 1)
                    if v == "g":
                        for t in range(T):
                            ins = dve.scalar_tensor_tensor(gates[:, t, :, :, :].rearrange("p d i h -> p (d i h)"),
                                                           ps[:, b[t], 0:16], m.rstd[:, t:t + 1], row(m, "b_if"), ALU.mult, ALU.add)
                            ins.then_inc(gates_ready if t == 0 else z_dve, 1)
                    elif v == "ua":
                        dve.wait_ge(*evac_at["ug"])
                        for t in range(T):
                            ins = dve.scalar_tensor_tensor(u[:, t, :], ps[:, b[t], :], m.rstd[:, t:t + 1], u[:, t, :], ALU.mult, ALU.mult)
                            ins.then_inc(u_ready, 1)
                    elif v[0] == "y":
                        br, h = "abc".index(v[1]), int(v[2])
                        for t in range(T):
                            dst = merged[:, t, h * BANK:(h + 1) * BANK]
                            g_t = gt[:, t, br, h * BANK:(h + 1) * BANK]
                            if br == 0:
                                dve.wait_ge(*evac_at["gt5"])
                                ins = dve.scalar_tensor_tensor(dst, g_t, 1.0, ps[:, b[t], :], ALU.add, ALU.mult)
                                if t == 0:
                                    link(ins)
                                else:
                                    ins.then_inc(z_dve, 1)
                                    dve.wait_ge(*evac_at[v])
                            else:
                                ins = dve.scalar_tensor_tensor(ytmp[:, t, :], g_t, 1.0, ps[:, b[t], :], ALU.add, ALU.mult)
                                if t == 0:
                                    link(ins)
                                else:
                                    ins.then_inc(z_dve, 1)
                                    dve.wait_ge(*evac_at[v])
                                ins = dve.tensor_tensor(dst, dst, ytmp[:, t, :], ALU.add)
                                if br == 2 and t == T - 1:
                                    ins.then_inc(merged_ready, 1)
                                else:
                                    link(ins)
                    else:
                        h = int(v[3])
                        for t in range(T):
                            ins = dve.tensor_tensor(m.x[:, t, h * BANK:(h + 1) * BANK], ps[:, b[t], :],
                                                    m.x[:, t, h * BANK:(h + 1) * BANK], ALU.add)
                        ins.then_inc(z_dve, 1)
                elif what == "gate1":
                    dve.wait_ge(*evac_at["g"])
                    dve.wait_ge(gates_ready, 1)
                    f = gates[:, :, :, 1, :].rearrange("p t d h -> p (t d) h")
                    l3 = fabs[:, :].rearrange("p (a h) -> p a h", h=A_HEADS)
                    dve.scalar_tensor_tensor(l3, f, -1.0, f, ALU.mult, ALU.max).then_inc(fabs_ready, 1)
                    dve.wait_ge(logl_ready, 1)
                    dve.scalar_tensor_tensor(logf[:, :, :, :].rearrange("p t d h -> p (t d) h"), f, 0.0, l3,
                                             ALU.min, ALU.subtract).then_inc(logf_ready, 1)
                elif what == "gate2":
                    dve.wait_ge(fcum_ps, 1)
                    fps = ps[:, SB, 0:2 * T * A_HEADS].rearrange("p (d t h) -> p d t h", d=2, t=T)
                    link(dve.tensor_copy(fcum[:, :, :, :].rearrange("p h d t -> p d t h"), fps))
                    for d in range(2):
                        ins = dve.tensor_tensor(ir[:, :, d, :], gates[:, :, d, 0, :], fps[:, d, :, :], ALU.subtract)
                        if d == 0:
                            link(ins)
                    ins.then_inc(ir_ready, 1)
                elif what == "gate3":
                    dve.wait_ge(irow_ps, 1)
                    dve.tensor_copy(irow[:, :], ps[0:2 * A_HEADS, SB, SEQ:2 * SEQ]).then_inc(irow_ready, 1)
                elif what == "cnorm":
                    dve.wait_ge(crstd_ready, 1)
                    dve.wait_ge(*evac_at["ckv"])
                    for i in range(4):
                        a = cq[:, i % 2, :] if i < 2 else ckv[:, i % 2, 0:C_KVR]
                        dve.tensor_scalar(a, a, crstd[:, i:i + 1], None, ALU.mult).then_inc(cnorm_ready, 1)
                elif what == "cturn":
                    for c in range(5):
                        dve.wait_ge(chi_ready, min(5, 2 * (c // 2) + 2))
                        gain = (col(m, "cq")[:, c:c + 1] if c < 3 else col(m, "ckv")[:, c - 3:c - 2])
                        dve.scalar_tensor_tensor(clo[:, c, :], cslot(c), gain, chi[:, c, :].bitcast(F32),
                                                 ALU.mult, ALU.subtract).then_inc(clo_ready, 1)
                elif what == "conv":
                    w0, _ = COLS["conv_w"]
                    for c in range(4):
                        if v == 0:
                            dve.wait_ge(upad_ready, c + 1)
                            ins = dve.tensor_scalar(conv[:, c, :], upad[:, c, 0:SEQ], m.cols[:, w0 + c:w0 + c + 1],
                                                    col(m, "conv_b")[:, c:c + 1], ALU.mult, ALU.add)
                        else:
                            dve.wait_ge(conv_step, 4 * (v - 1) + c + 1)
                            w = w0 + v * 4 + c
                            ins = dve.scalar_tensor_tensor(conv[:, c, :], upad[:, c, v:v + SEQ], m.cols[:, w:w + 1],
                                                           conv[:, c, :], ALU.mult, ALU.add)
                        ins.then_inc(conv_step, 1)
                elif what == "chead":
                    dve.wait_ge(*evac_at["ukv1"])
                    q4, k4, kv4 = qh[:, :, :, :], kh[:, :, :, :], kv[:, :, :, :]

                    def cs(name):
                        return const(m, name).rearrange("p (t a f) -> p t a f", t=T, a=1)

                    for t in range(T):
                        ins = dve.tensor_tensor_reduce(decay[:, t * C_ROPE:(t + 1) * C_ROPE], ckv[:, t, C_KVR:], ckv[:, t, C_KVR:], 1.0, 0.0,
                                                       ALU.mult, ALU.add, krss[:, t:t + 1])
                    link(ins)
                    for t in range(T):
                        ins = dve.tensor_scalar(hss[:, 1, t, :], hss[:, 1, t, :], krss[:, t:t + 1], None, ALU.add)
                    ins.then_inc(hss_ready, 1)
                    dve.wait_ge(hrs_ready, 1)
                    for t in range(T):
                        hb = [hrs[:, a, t, :].unsqueeze(2) for a in range(2)]
                        link(dve.tensor_tensor(q4[:, t], q4[:, t], hb[0].to_broadcast([P, C_HEADS, C_QK]), ALU.mult))
                        link(dve.tensor_tensor(q4[:, t], q4[:, t],
                                               row(m, "q_g").unsqueeze(1).to_broadcast([P, C_HEADS, C_QK]), ALU.mult))
                        link(dve.tensor_tensor(k4[:, t, :, 0:C_NOPE], kv4[:, t, :, 0:C_NOPE],
                                               hb[1].to_broadcast([P, C_HEADS, C_NOPE]), ALU.mult))
                        link(dve.tensor_tensor(k4[:, t, :, C_NOPE:],
                                               ckv[:, t, C_KVR:].unsqueeze(1).to_broadcast([P, C_HEADS, C_ROPE]),
                                               hb[1].to_broadcast([P, C_HEADS, C_ROPE]), ALU.mult))
                        link(dve.tensor_tensor(k4[:, t], k4[:, t],
                                               row(m, "k_g").unsqueeze(1).to_broadcast([P, C_HEADS, C_QK]), ALU.mult))
                    for a in (q4, k4):
                        for t in range(T):
                            r1, r2 = a[:, t, :, C_NOPE:C_NOPE + 16], a[:, t, :, C_NOPE + 16:]
                            c_t = cs("cos")[:, t].to_broadcast([P, C_HEADS, 16])
                            s_t = cs("sin")[:, t].to_broadcast([P, C_HEADS, 16])
                            rp = [rope[:, t, i, :, :] for i in range(4)]
                            dve.tensor_tensor(rp[0], r1, c_t, ALU.mult)
                            dve.tensor_tensor(rp[1], r2, s_t, ALU.mult)
                            dve.tensor_tensor(rp[2], r2, c_t, ALU.mult)
                            link(dve.tensor_tensor(rp[3], r1, s_t, ALU.mult))
                            dve.tensor_tensor(r1, rp[0], rp[1], ALU.subtract)
                            ins = dve.tensor_tensor(r2, rp[2], rp[3], ALU.add)
                            if t < T - 1:
                                link(ins)
                        ins.then_inc(ckh_ready, 1)
                        dve.wait_ge(ckh_ready, 1 if a is q4 else 2)
                elif what == "m1":
                    dve.wait_ge(ib_ps, v + 1)
                    if v >= 1:
                        dve.wait_ge(emt_ready, v)
                    for j, (a, n) in enumerate(parts):
                        d, t = j // 2, j % 2
                        src = ps[:, SB, d * SEQ:d * SEQ + SEQ]
                        msk = const(m, ("causal", "anti")[d])
                        if n == P:
                            src, msk = (src[:, 0:P], msk[:, P:]) if d == 0 else (src[:, P:], msk[:, 0:P])
                        ins = dve.tensor_tensor_reduce(decay[:, a:a + n], src, msk, 1.0, 0.0, ALU.add, ALU.max, mx[:, j:j + 1])
                    link(ins)
                    link(dve.tensor_tensor(mstat[:, 1, :], mx[:, :], fcum[:, v, :, :].rearrange("p d t -> p (d t)"), ALU.add))
                    dve.tensor_scalar(mstat[:, 0, :], mx[:, :], -1.0, None, ALU.mult).then_inc(mneg_ready, 1)
                elif what == "m2":
                    dve.wait_ge(score_ps, v + 1)
                    dve.wait_ge(emt_ready, v + 1)
                    for j, (a, n) in enumerate(parts):
                        d, t = j // 2, j % 2
                        src = ps[:, SA, t * SEQ:(t + 1) * SEQ]
                        if n == P:
                            src = src[:, 0:P] if d == 0 else src[:, P:]
                        ins = dve.tensor_tensor_reduce(smat[:, a:a + n], src, decay[:, a:a + n], 1.0, 0.0,
                                                       ALU.mult, ALU.add, den[:, j:j + 1])
                    link(ins)
                    link(dve.scalar_tensor_tensor(den[:, :], den[:, :], -1.0, den[:, :], ALU.mult, ALU.max))
                    link(dve.tensor_tensor(den[:, :], den[:, :], mstat[:, 2, :], ALU.max))
                    link(dve.reciprocal(mstat[:, 3, :], den[:, :]))
                    f0, f1, b0, b1 = parts
                    rd = [mstat[:, 3, j:j + 1] for j in range(4)]
                    dve.tensor_scalar(amat[:, 1, :], smat[:, f1[0]:f1[0] + f1[1]], rd[1], None, ALU.mult)
                    link(dve.tensor_scalar(amat[:, 0, :], smat[:, b0[0]:b0[0] + b0[1]], rd[2], None, ALU.mult))
                    dve.scalar_tensor_tensor(amat[:, 0, 0:P], smat[:, f0[0]:f0[0] + P], rd[0], amat[:, 0, 0:P],
                                             ALU.mult, ALU.add)
                    dve.scalar_tensor_tensor(amat[:, 1, P:], smat[:, b1[0]:b1[0] + P], rd[3], amat[:, 1, P:],
                                             ALU.mult, ALU.add).then_inc(amat_ready, 1)
                    dve.wait_ge(amat_ready, v + 1)
                elif what == "m4b":
                    dve.wait_ge(hrstd_ready, v + 1)
                    if v == 0:
                        dve.wait_ge(*evac_at["o"])
                    for t in range(T):
                        dve.scalar_tensor_tensor(hn[:, t, :], ps[:, SA, sq(t)], hst[:, 2, t:t + 1],
                                                 o_gate[:, t, v * P:(v + 1) * P], ALU.mult, ALU.mult).then_inc(hn_ready, 1)
                elif what == "m5":
                    dve.wait_ge(yahi, v + 1)
                    dve.scalar_tensor_tensor(ylo[0][:, v, :], ps[:, SA, SEQ:2 * SEQ], col(m, "a_norm")[:, v:v + 1],
                                             yhi[0][:, v, :].bitcast(F32), ALU.mult, ALU.subtract).then_inc(yalo, 1)
                elif what == "c2":
                    dve.wait_ge(cs_ps, v + 1)
                    link(dve.tensor_reduce(cmx[:, 0, :], ps[:, SD, :].rearrange("p (t s) -> p t s", t=T), AX.X, ALU.max))
                    dve.tensor_scalar(cmx[:, 1, :], cmx[:, 0, :], -float(C_QK) ** -0.5, None, ALU.mult).then_inc(cmx_ready, 1)
                elif what == "c2b":
                    dve.wait_ge(cexp_ready, v + 1)
                    link(dve.reciprocal(csm[:, 1, :], csm[:, 0, :]))
                    for t in range(T):
                        ins = dve.tensor_scalar(pr[:, t, :], pr[:, t, :], csm[:, 1, t:t + 1], None, ALU.mult)
                    ins.then_inc(pr_ready, 1)
                elif what == "c4":
                    r = slice(64 * (v % 2), 64 * (v % 2) + 64)
                    dve.wait_ge(ychi, v + 1)
                    dve.tensor_tensor(ylo[2][r, v // 2, :], ps[r, SD, 0:SEQ], yhi[2][r, v // 2, :].bitcast(F32),
                                      ALU.subtract).then_inc(yclo, 1)
                elif what == "b2":
                    dve.wait_ge(ctok_ps, 1)
                    for t in range(T):
                        link(dve.bn_stats(bst[:, t, :], ps[:, (SA, SB)[t], :]))
                        ins = dve.bn_aggr(bmv[:, t, :], bst[:, t, :])
                        if t == 0:
                            link(ins)
                    ins.then_inc(bvar_ready, 1)
                    dve.wait_ge(bvar_ready, 1)
                elif what == "b3":
                    dve.wait_ge(brstd_ready, 1)
                    for t in range(T):
                        dve.tensor_scalar(u[:, t, :], ps[:, (SA, SB)[t], :], bmv[:, t, 0:1], brstd[:, t:t + 1],
                                          ALU.subtract, ALU.mult).then_inc(bn_ready, 1)
                elif what == "b4":
                    for c in range(4):
                        dve.wait_ge(ybhi, c + 1)
                        dve.tensor_tensor(ylo[1][:, c, :], silu[:, c, :], yhi[1][:, c, :].bitcast(F32),
                                          ALU.subtract).then_inc(yblo, 1)
                elif what == "mturn":
                    for c in range(4 * v, 4 * v + 4):
                        dve.wait_ge(xhi_ready, DC + 2 * (c // 2) + 2)
                        dve.scalar_tensor_tensor(xlo[:, c, :], turned_ps(m, [SA, SB, SC, SD], c), 0.5,
                                                 xhi[:, c, :].bitcast(F32), ALU.mult, ALU.subtract).then_inc(xlo_ready, 1)

        @block.gpsimd
        def _(pool):
            n_step = [0]

            def link(ins):
                n_step[0] += 1
                ins.then_inc(pool_step, 1)
                pool.wait_ge(pool_step, n_step[0])

            pool.wait_ge(const_in, 32)
            norm_pool(pool, m, 0)
            pool.wait_ge(m.rstd_ready, 1)
            pool.tensor_scalar(scale_q[:, :], m.rstd[:, :], float(A_DIM) ** -0.5, None, ALU.mult)
            pool.tensor_scalar(scale_gt[:, :], m.rstd[:, :], 0.5, None, ALU.mult).then_inc(scale_ready, 1)
            for what, v in steps:
                if what == "gran":
                    g = blocks[v[0]][v[1]][0] + lookahead
                    if v[2] != 0 and g < n_gran and st.lows[g][0] is st.lo_pool:
                        st.split_lo(pool, g)
                elif what == "cnorm":
                    pool.wait_ge(csum_ready, 2)
                    pool.tensor_scalar(cstat[:, 0:2], csum[:, 0:2], 1.0 / C_QR, EPS, ALU.mult, ALU.add)
                    link(pool.tensor_scalar(cstat[:, 2:4], csum[:, 2:4], 1.0 / C_KVR, EPS, ALU.mult, ALU.add))
                    pool.tensor_tensor(crstd[:, :], cstat[:, :], m.half[:, 0:4], ALU.pow).then_inc(crstd_ready, 1)
                elif what == "chead":
                    pool.wait_ge(hss_ready, 1)
                    h2, ms2, rs2 = (a[:, :, :, :].rearrange("p a t h -> p (a t h)") for a in (hss, hms, hrs))
                    link(pool.tensor_scalar(ms2, h2, 1.0 / C_QK, EPS, ALU.mult, ALU.add))
                    pool.tensor_tensor(rs2, ms2, m.half[:, 0:1].to_broadcast([P, 2 * T * C_HEADS]), ALU.pow).then_inc(hrs_ready, 1)
                elif what == "m4":
                    pool.wait_ge(hsum_ready, T * (v + 1))
                    link(pool.tensor_scalar(hst[:, 1, :], hst[:, 0, :], 1.0 / A_DIM, EPS, ALU.mult, ALU.add))
                    pool.tensor_tensor(hst[:, 2, :], hst[:, 1, :], m.half[:, 0:T], ALU.pow).then_inc(hrstd_ready, 1)
                elif what == "b2":
                    pool.wait_ge(bvar_ready, 1)
                    link(pool.tensor_scalar(bvar[:, :], bmv[:, :, 1], EPS, None, ALU.add))
                    pool.tensor_tensor(brstd[:, :], bvar[:, :], m.half[:, 0:T], ALU.pow).then_inc(brstd_ready, 1)



FJ = E_FF // (P // CAP)
FB = FJ // P
E_COLS = 256
GK = 2
NS = 12
EARLY = 4


def expert_place(m, i):
    n = E_FF if i < 8 else E_COLS
    ring = m.ring[:, i * GK * E_FF:(i + 1) * GK * E_FF] if i < EARLY else m.e_ring[:, i - EARLY, :]
    return ring.rearrange("p (k n) -> p k n", n=n)


def load_expert(sp, m, I, e, i):
    if i < 8:
        w = I["w_e_gate"] if i < 4 else I["w_e_up"]
        r = (i % 4) * GK * P
        src = w[0, e, r:r + GK * P, :]
    else:
        src = I["w_e_down"][0, e, :, (i - 8) * E_COLS:(i - 7) * E_COLS]
    sp.dma_start(expert_place(m, i), src.rearrange("(k p) n -> p k n", p=P)).then_inc(m.e_landed[i], 16)


def experts(nc, m, I, st):
    with ExitStack() as ctx:
        def sb(name, shape, dt=F32):
            return ctx.enter_context(nc.sbuf_tensor("sb_" + name, shape, dt))

        def sem(name):
            return ctx.enter_context(nc.semaphore(name))

        ps = m.ps
        J = P // CAP
        NC = E_COLS
        ACC = (0, 1, 2, 3)
        GATE, UP, DOWN = 4, 5, (6, 7)
        NBANKS = [4, 5, 6, 7]
        LOGIT, AFF, SLOT = 5, 6, 7

        m.e_ring = sb("e_ring", [P, NS - EARLY, GK * E_FF])
        xgT = sb("xgT", [P, DC, N_EXP * CAP])
        xnT = xgT[:, :, 0:SEQ]
        wr = sb("wr", [P, DC, N_EXP])
        late = m.rows[:, 0:CAP]
        smx, ssum = sb("smx", [P, 2, T]), sb("ssum", [P, 2, T])
        aff = sb("aff", [P, T, N_EXP])
        affT, work, above, equal = (m.xs[0:N_EXP, 1, i * SEQ:(i + 1) * SEQ] for i in range(4))
        one = const(m, "ones")[0:N_EXP, 0:1].to_broadcast([N_EXP, SEQ])
        top8, cnt = sb("top8", [N_EXP, 8]), sb("cnt", [N_EXP, 2])
        hot = sb("hot", [P, T, N_EXP, CAP], F32R)
        hotg = m.xs[:, 0, :].rearrange("p (t e c) -> p t e c", t=T, e=N_EXP)
        xshi, xslo = sb("xshi", [P, T, D], F32R), sb("xslo", [P, T, D], F32R)
        at = CONSTS["causal"][0]
        xgs = m.consts[:, at:at + DC * CAP].rearrange("p (k c) -> p k c", k=DC)
        hotgs = sb("hotgs", [P, T, J, CAP])
        at = CONSTS["anti"][0]
        gs = m.consts[:, at:at + SEQ]
        sg, hT = sb("sg", [P, FJ]), sb("hT", [P, FB, P])
        hs = sg
        ysb = m.xs[:, 1, :]

        wr_in, late_in = sem("wr_in"), sem("late_in")
        landed = m.e_landed
        xnT_act, logits_ps, smx_ready, exp_ready, aff_ready, affT_ps, slot_ready, slot_ps, hot_ready, hotg_ready = (
            sem(s) for s in ("xnT_act", "logits_ps", "smx_ready", "exp_ready", "aff_ready", "affT_ps", "slot_ready",
                             "slot_ps", "hot_ready", "hotg_ready"))
        dve_step = sem("e_dve_step")
        xshi_ready, xslo_ready = sem("xshi_ready"), sem("xslo_ready")
        gather_ps, xg_act, xg_dve = sem("gather_ps"), sem("xg_act"), sem("xg_dve")
        used, xgs_ready, g_ps, gs_ready, sg_ready, h_ready, hT_ps, hT_ready, y_act, y_dve, scattered = (
            sem(s) for s in ("e_used", "xgs_ready", "g_ps", "gs_ready", "sg_ready", "h_ready", "hT_ps", "hT_ready",
                             "y_act", "y_dve", "scattered"))

        def place(i):
            return expert_place(m, i)

        block = ctx.enter_context(nc.Block())

        @block.sync
        def _(sp):
            sp.dma_start(wr[:, :, :], I["w_router"][0].rearrange("(k p) n -> p k n", p=P)).then_inc(wr_in, 16)
            sp.dma_start(late[:, :], I["c_late"][:, 3 * P:]).then_inc(late_in, 16)
            for i in range(EARLY, NS):
                load_expert(sp, m, I, 0, i)
            sp.sem_clear(m.mixer_sems)
            with sp.Fori(1, N_EXP) as e:
                for i in range(NS):
                    sp.wait_ge(used, e * NS + (i + 1 - NS))
                    load_expert(sp, m, I, e, i)
            sp.wait_ge(used, (N_EXP - 1) * NS + EARLY)
            for g in range(st.slots):
                st.load(sp, g)

        @block.scalar
        def _(act):
            gain = col(m, "ffn")
            for c in range(DC):
                act.wait_ge(m.xturn_ps, 4 + c // 2 + 1)
                act.activation(xnT[:, c, :], turned_ps(m, NBANKS, c), ACT.Copy, scale=gain[:, c:c + 1]).then_inc(xnT_act, 1)
            norm_act(act, m, 1)
            act.wait_ge(smx_ready, 1)
            for t in range(T):
                ins = act.activation(aff[:, t, :], ps[:, LOGIT, t * N_EXP:(t + 1) * N_EXP], ACT.Exp,
                                     bias=smx[:, 1, t:t + 1], scale=m.rstd[:, t:t + 1], accum_out=ssum[:, 0, t:t + 1])
            ins.then_inc(exp_ready, 1)
            for t in range(T):
                act.activation(xshi[:, t, :], m.x[:, t, :], ACT.Copy, scale=m.rstd[:, t:t + 1]).then_inc(xshi_ready, 1)
            for c in range(0, DC, 2):
                act.wait_ge(gather_ps, c + 1)
                act.activation(xgT[:, c, :], ps[:, 4 + c % 4, :], ACT.Copy, scale=gain[:, c:c + 1]).then_inc(xg_act, 1)
            with act.Fori(0, N_EXP) as e:
                act.wait_ge(g_ps, e + 1)
                for t in range(T):
                    ins = act.activation(gs[:, t * P:(t + 1) * P], ps[:, GATE + t, FJ:FJ + P], ACT.Copy)
                ins.then_inc(gs_ready, 1)
                act.wait_ge(used, e * NS + 4)
                act.activation(sg[:, :], ps[:, GATE, 0:FJ], ACT.Silu).then_inc(sg_ready, 1)
                act.wait_ge(used, e * NS + 10)
                act.activation(ysb[:, 0:BANK], ps[:, DOWN[0], :], ACT.Copy).then_inc(y_act, 1)
            act.wait_ge(scattered, N_EXP)
            for h in range(2):
                act.activation(m.x[:, 0, h * BANK:(h + 1) * BANK], ps[:, ACC[h], :], ACT.Copy)

        @block.tensor
        def _(pe):
            turn_tokens(pe, m, m.x, NBANKS)
            pe.wait_ge(wr_in, 16)
            pe.wait_ge(xnT_act, DC)
            for t in range(T):
                for c in range(DC):
                    mm = pe.matmul(ps[:, LOGIT, t * N_EXP:(t + 1) * N_EXP], xnT[:, c, t * P:(t + 1) * P], wr[:, c, :],
                                   start=c == 0, stop=c == DC - 1)
            mm.then_inc(logits_ps, 1)
            for t in range(T):
                for h in range(2):
                    pe.matmul(ps[:, ACC[2 * t + h], :], m.ident, m.x[:, t, h * BANK:(h + 1) * BANK], start=True, stop=True)
            pe.wait_ge(aff_ready, T)
            for t in range(T):
                mm = pe.transpose(ps[0:N_EXP, AFF, t * P:(t + 1) * P], aff[:, t, :], m.ident)
            mm.then_inc(affT_ps, 1)
            pe.wait_ge(slot_ready, 1)
            for t in range(T):
                mm = pe.transpose(ps[:, SLOT, t * N_EXP:(t + 1) * N_EXP], affT[:, t * P:(t + 1) * P], m.ident[0:N_EXP, 0:N_EXP])
            mm.then_inc(slot_ps, 1)
            pe.wait_ge(xslo_ready, T)
            pe.wait_ge(hot_ready, T)
            for c in range(DC):
                if c >= 4:
                    pe.wait_ge((xg_act, xg_dve)[c % 2], (c - 4) // 2 + 1)
                for t in range(T):
                    for part in (xshi, xslo):
                        mm = pe.matmul(ps[:, 4 + c % 4, :], part[:, t, c * P:(c + 1) * P],
                                       hot[:, t, :, :].rearrange("p e c -> p (e c)"),
                                       start=t == 0 and part is xshi, stop=t == T - 1 and part is xslo)
                mm.then_inc(gather_ps, 1)
            pe.wait_ge(xg_act, DC // 2)
            pe.wait_ge(xg_dve, DC // 2)
            with pe.Fori(0, N_EXP) as e:
                pe.wait_ge(xgs_ready, e * 2 + 2)
                for t in range(T):
                    mm = pe.transpose(ps[:, GATE + t, FJ:FJ + P], hotgs[:, t, :, :].rearrange("p j c -> p (j c)"), m.ident)
                mm.then_inc(g_ps, 1)
                pe.wait_ge(gs_ready, e + 1)
                for i in range(8):
                    pe.wait_ge(landed[i], e * 16 + 16)
                    for q in range(GK):
                        k = (i % 4) * GK + q
                        for j in range(J):
                            mm = pe.matmul(ps[j * CAP:(j + 1) * CAP, GATE if i < 4 else UP, 0:FJ], xgs[:, k, :],
                                           place(i)[:, q, j * FJ:(j + 1) * FJ], start=k == 0, stop=k == DC - 1)
                    mm.then_inc(used, 1)
                pe.wait_ge(h_ready, e + 1)
                for b in range(FB):
                    mm = pe.transpose(ps[:, GATE, b * P:(b + 1) * P], hs[:, b * P:(b + 1) * P], m.ident)
                mm.then_inc(hT_ps, 1)
                pe.wait_ge(hT_ready, e + 1)
                for i in range(4):
                    pe.wait_ge(landed[8 + i], e * 16 + 16)
                    for b in range(FB):
                        for j in range(J):
                            mm = pe.matmul(ps[j * CAP:(j + 1) * CAP, DOWN[i // 2], (i % 2) * NC:(i % 2 + 1) * NC],
                                           hT[:, b, j * CAP:(j + 1) * CAP], place(8 + i)[:, j * FB + b, :],
                                           start=b == 0, stop=b == FB - 1)
                    mm.then_inc(used, 1)
                pe.wait_ge(y_act, e + 1)
                pe.wait_ge(y_dve, e + 1)
                for t in range(T):
                    for h in range(2):
                        mm = pe.matmul(ps[:, ACC[2 * t + h], :], gs[:, t * P:(t + 1) * P], ysb[:, h * BANK:(h + 1) * BANK],
                                       start=False, stop=True, skip_group_check=True)
                mm.then_inc(scattered, 1)

        @block.vector
        def _(dve):
            n_step = [0]

            def link(ins):
                n_step[0] += 1
                ins.then_inc(dve_step, 1)
                dve.wait_ge(dve_step, n_step[0])

            gain = col(m, "ffn")
            dve.wait_ge(logits_ps, 1)
            link(dve.tensor_reduce(smx[:, 0, :], ps[:, LOGIT, 0:T * N_EXP].rearrange("p (t e) -> p t e", t=T), AX.X, ALU.max))
            dve.wait_ge(m.rstd_ready, 2)
            dve.scalar_tensor_tensor(smx[:, 1, :], smx[:, 0, :], -1.0, m.rstd[:, :], ALU.mult, ALU.mult).then_inc(smx_ready, 1)
            dve.wait_ge(exp_ready, 1)
            link(dve.reciprocal(ssum[:, 1, :], ssum[:, 0, :]))
            for t in range(T):
                dve.tensor_scalar(aff[:, t, :], aff[:, t, :], ssum[:, 1, t:t + 1], None, ALU.mult).then_inc(aff_ready, 1)
            for t in range(T):
                dve.wait_ge(xshi_ready, t + 1)
                dve.scalar_tensor_tensor(xslo[:, t, :], m.x[:, t, :], m.rstd[:, t:t + 1], xshi[:, t, :].bitcast(F32),
                                         ALU.mult, ALU.subtract).then_inc(xslo_ready, 1)
            dve.wait_ge(affT_ps, 1)
            link(dve.tensor_copy(affT[:, :], ps[0:N_EXP, AFF, 0:SEQ]))
            src = affT
            for r in range(CAP // 8):
                link(dve.max(top8[:, :], src[:, :]))
                if r < CAP // 8 - 1:
                    link(dve.match_replace(work[:, :], top8[:, :], src[:, :], -1.0))
                    src = work
            link(dve.tensor_scalar(above[:, :], affT[:, :], top8[:, 7:8], None, ALU.is_gt, ALU.add, accum_out=cnt[:, 0:1]))
            link(dve.tensor_scalar(equal[:, :], affT[:, :], top8[:, 7:8], None, ALU.is_equal))
            link(dve.tensor_scalar(cnt[:, 1:2], cnt[:, 0:1], -1.0, float(CAP), ALU.mult, ALU.add))
            link(dve.tensor_tensor_scan(work[:, :], one, equal[:, :], 0.0, ALU.mult, ALU.add))
            link(dve.scalar_tensor_tensor(equal[:, :], work[:, :], cnt[:, 1:2], equal[:, :], ALU.is_le, ALU.mult))
            link(dve.tensor_tensor(above[:, :], above[:, :], equal[:, :], ALU.add))
            link(dve.tensor_tensor_scan(work[:, :], one, above[:, :], 0.0, ALU.mult, ALU.add))
            dve.tensor_tensor(affT[:, :], work[:, :], above[:, :], ALU.mult).then_inc(slot_ready, 1)
            dve.wait_ge(slot_ps, 1)
            dve.wait_ge(late_in, 16)
            for t in range(T):
                slots = ps[:, SLOT, t * N_EXP:(t + 1) * N_EXP].unsqueeze(2).to_broadcast([P, N_EXP, CAP])
                dve.tensor_tensor(hot[:, t, :, :], slots, late[:, :].unsqueeze(1).to_broadcast([P, N_EXP, CAP]),
                                  ALU.is_equal).then_inc(hot_ready, 1)
            dve.wait_ge(hot_ready, T)
            for t in range(T):
                dve.tensor_tensor(hotg[:, t, :, :], hot[:, t, :, :].bitcast(F32), aff[:, t, :].unsqueeze(2).to_broadcast([P, N_EXP, CAP]),
                                  ALU.mult).then_inc(hotg_ready, 1)
            for c in range(1, DC, 2):
                dve.wait_ge(gather_ps, c + 1)
                dve.tensor_scalar(xgT[:, c, :], ps[:, 4 + c % 4, :], gain[:, c:c + 1], None, ALU.mult).then_inc(xg_dve, 1)
            with dve.Fori(0, N_EXP) as e:
                dve.wait_ge(sg_ready, e + 1)
                dve.wait_ge(used, e * NS + 8)
                dve.tensor_tensor(hs[:, :], ps[:, UP, 0:FJ], sg[:, :], ALU.mult).then_inc(h_ready, 1)
                dve.wait_ge(hT_ps, e + 1)
                dve.tensor_copy(hT[:, :, :].rearrange("p b c -> p (b c)"), ps[:, GATE, 0:FJ]).then_inc(hT_ready, 1)
                dve.wait_ge(used, e * NS + 12)
                dve.tensor_copy(ysb[:, BANK:], ps[:, DOWN[1], :]).then_inc(y_dve, 1)
            dve.wait_ge(scattered, N_EXP)
            for h in range(2):
                dve.tensor_copy(m.x[:, 1, h * BANK:(h + 1) * BANK], ps[:, ACC[2 + h], :])

        @block.gpsimd
        def _(pool):
            norm_pool(pool, m, 1)

            def take(e):
                pool.tensor_copy(xgs[:, :, :], xgT[:, :, bass.ds(e * CAP, CAP)]).then_inc(xgs_ready, 1)
                pool.tensor_copy(hotgs[:, :, :, :],
                                 hotg[:, :, bass.ds(e, 1), :].to_broadcast([P, T, J, CAP])).then_inc(xgs_ready, 1)

            pool.wait_ge(hotg_ready, T)
            pool.wait_ge(xg_act, DC // 2)
            pool.wait_ge(xg_dve, DC // 2)
            take(0)
            with pool.Fori(0, N_EXP - 1) as e:
                pool.wait_ge(used, e * NS + 8)
                take(e + 1)



FW = 256
FN = D_FF // FW
FC = FW // P


def second_stream(m, ctx, nc, I):
    st = Stream(ctx, nc, "net", m.ring[:, :].rearrange("p (s n) -> p s n", n=2048), 3)
    at = {}

    def dense(name, w, n0, by_dve=False):
        at[name] = [st.add([(0, 4, BANK, chunks(w, k, 4, n0, BANK))], by_dve) for k in (0, 4)]

    def ffn(l):
        gu, down = I["ffn_w_gu_2"][l], I["ffn_w_down_2"][l]
        at[f"ffn{l}"] = len(st.pieces)

        def gate_up(b):
            for k in (0, 4):
                st.add([(0, 4, FW, chunks(gu, k, 4, b * FW, FW)), (4 * FW, 4, FW, chunks(gu, k, 4, D_FF + b * FW, FW))])

        for b in range(FN):
            gate_up(b)
            if b >= 1:
                st.add([(0, FC, D, chunks(down, (b - 1) * FC, FC, 0, D))], by_dve=True)
        st.add([(0, FC, D, chunks(down, (FN - 1) * FC, FC, 0, D))], by_dve=True)

    for name, n0 in (("v0", D), ("v1", D + BANK), ("u0", 0), ("u1", BANK)):
        dense(name, I["a_w_in_2"][0], n0, by_dve=name == "v0")
    for h in range(2):
        dense(f"go{h}", I["a_w_out_2"][0], h * BANK)
    ffn(0)
    for h in range(2):
        for name, w, n0 in (("q", I["b_w_q_2"][0], 0), ("k", I["kv_w_2"], 0), ("w", I["kv_w_2"], D)):
            dense(f"{name}{h}", w, n0 + h * BANK, by_dve=h == 1 and name != "q")
    at["o0"], at["o1"] = [], []
    for k in (0, 4):
        for h in range(2):
            at[f"o{h}"].append(st.add([(0, 4, BANK, chunks(I["b_w_o_2"][0], k, 4, h * BANK, BANK))], by_dve=True))
    ffn(1)
    return st, at


def add_to_x(dve, m, st, at, name, banks, h, done=None):
    dve.wait_ge(st.used, at[name][-1] + 1)
    for t in range(T):
        dst = m.x[:, t, h * BANK:(h + 1) * BANK]
        ins = dve.tensor_tensor(dst, m.ps[:, banks[t], :], dst, ALU.add)
    if done is not None:
        ins.then_inc(done, 1)


def gmlp(nc, m, I, st, at, use):
    with ExitStack() as ctx:
        def sb(name, shape, dt=F32):
            return ctx.enter_context(nc.sbuf_tensor("sb_" + name, shape, dt))

        def sem(name):
            return ctx.enter_context(nc.semaphore(name))

        ps = m.ps
        ut, vt = sb("g_u", [P, T, D]), sb("g_v", [P, T, D])
        wsp, gain = sb("wsp", [P, G_GROUPS, P]), sb("g_gain", [P, D])
        bst, bmv, bvar, brs = sb("g_bst", [P, T, 2, 6]), sb("g_bmv", [P, T, 2]), sb("g_bvar", [P, T]), sb("g_brs", [P, T])
        tmp = sb("g_tmp", [P, 2, T, P])
        wsp_in, gain_in, wsp_ready = sem("wsp_in"), sem("gain_in"), sem("wsp_ready")
        z_act, var_ready, rs_ready, v_ready, sp_ps, mix_ready, mixT_ps, mhi, mlo, out_read = (
            sem(s) for s in ("g_z_act", "g_var_ready", "g_rs_ready", "g_v_ready", "sp_ps", "g_mix_ready", "g_mixT_ps",
                             "g_mhi", "g_mlo", "g_out_read"))
        dve_step = sem("g_dve_step")
        xhi_ready, xlo_ready = sem("g_xhi_ready"), sem("g_xlo_ready")
        order = ["v0", "v1", "u0", "u1"]
        first = at["v0"][0]
        last = at["go1"][-1]
        look = 2
        NB = [4, 5, 6, 7]
        block = ctx.enter_context(nc.Block())

        def zb(i):
            return [2 * (i % 2) + t for t in range(T)]

        @block.sync
        def _(sp):
            sp.dma_start(wsp[:, :, :], I["w_spT"]).then_inc(wsp_in, 16)
            sp.dma_start(gain[:, :], I["a_v_norm_2"][0].partition_broadcast(P)).then_inc(gain_in, 16)
            for g in range(first + st.slots, last + 1 + st.slots):
                st.load(sp, g)

        @block.scalar
        def _(act):
            st.split_hi(act, first)
            norm_hi_act(act, m, use, NB, m.xhi, col(m, "gmlp"), xhi_ready, 0)
            st.split_hi(act, first + 1)
            norm_act(act, m, use)
            for i, name in enumerate(order):
                for g in at[name]:
                    st.split_hi(act, g + look)
                if i == 0:
                    act.wait_ge(m.rstd_ready, use + 1)
                act.wait_ge(st.used, at[name][-1] + 1)
                for t in range(T):
                    dst = (vt, ut)[i // 2][:, t, (i % 2) * BANK:(i % 2 + 1) * BANK]
                    act.activation(dst, ps[:, zb(i)[t], :], ACT.Gelu_apprx_tanh, scale=m.rstd[:, t:t + 1]).then_inc(z_act, 1)
            for c in range(DC):
                act.wait_ge(mixT_ps, c // 2 + 1)
                act.activation(m.xhi[:, c, :], turned_ps(m, [0, 1, 2, 3], c), ACT.Copy).then_inc(mhi, 1)
            for name in ("go0", "go1"):
                for g in at[name]:
                    st.split_hi(act, g + look)

        @block.gpsimd
        def _(pool):
            pool.wait_ge(wsp_in, 16)
            pool.tensor_tensor(wsp[:, :, :], wsp[:, :, :],
                               const(m, "upto").unsqueeze(1).to_broadcast([P, G_GROUPS, P]), ALU.mult).then_inc(wsp_ready, 1)
            norm_pool(pool, m, use)
            for i, name in enumerate(order + ["go0", "go1"]):
                for g in at[name]:
                    st.split_lo(pool, g + look)
                if name == "v1":
                    pool.wait_ge(var_ready, 1)
                    pool.tensor_scalar(bvar[:, :], bmv[:, :, 1], EPS, None, ALU.add).then_inc(rs_ready, 1)
                    pool.wait_ge(rs_ready, 1)
                    pool.tensor_tensor(brs[:, :], bvar[:, :], m.half[:, 0:T], ALU.pow).then_inc(rs_ready, 1)

        @block.tensor
        def _(pe):
            turn_tokens(pe, m, m.x, NB)
            for i, name in enumerate(order):
                if i >= 2:
                    pe.wait_ge(z_act, T * (i - 1))
                for j, g in enumerate(at[name]):
                    dense_granule(pe, st, g, [ps[:, b, :] for b in zb(i)], m.xhi, m.xlo, 4 * j, BANK, j == 0, j == 1,
                                  (xlo_ready, range(1, DC + 1)) if i == 0 else None)
            pe.wait_ge(v_ready, T)
            pe.wait_ge(wsp_ready, 1)
            for q in range(G_GROUPS):
                mm = pe.matmul(ps[:, 4 + q // 2, (q % 2) * SEQ:(q % 2 + 1) * SEQ], wsp[:, q, :],
                               vt[:, :, q * P:(q + 1) * P], start=True, stop=True)
                if q % 2:
                    mm.then_inc(sp_ps, 1)
            pe.wait_ge(z_act, 4 * T)
            for b in range(4):
                pe.wait_ge(mix_ready, 2 * b + 2)
                for cc in range(2):
                    for t in range(T):
                        c = 2 * b + cc
                        mm = pe.transpose(ps[:, b, cc * SEQ + t * P:cc * SEQ + (t + 1) * P], ut[:, t, c * P:(c + 1) * P], m.ident)
                mm.then_inc(mixT_ps, 1)
            for h in range(2):
                for j, g in enumerate(at[f"go{h}"]):
                    dense_granule(pe, st, g, [ps[:, 4 + 2 * h + t, :] for t in range(T)], m.xhi, m.xlo, 4 * j, BANK,
                                  j == 0, j == 1, (mlo, range(1, DC + 1)) if h == 0 else None)

        @block.vector
        def _(dve):
            n_step = [0]

            def link(ins):
                n_step[0] += 1
                ins.then_inc(dve_step, 1)
                dve.wait_ge(dve_step, n_step[0])

            st.split_lo(dve, first)
            norm_lo_dve(dve, m, use, NB, m.xhi, m.xlo, col(m, "gmlp"), xhi_ready, xlo_ready, 0)
            st.split_lo(dve, first + 1)
            for i in range(2):
                dve.wait_ge(z_act, T * (i + 1))
                for t in range(T):
                    ins = dve.bn_stats(bst[:, t, i, :], vt[:, t, i * BANK:(i + 1) * BANK])
            link(ins)
            for t in range(T):
                ins = dve.bn_aggr(bmv[:, t, :], bst[:, t, :, :].rearrange("p i s -> p (i s)"))
            ins.then_inc(var_ready, 1)
            dve.wait_ge(rs_ready, 2)
            for t in range(T):
                dve.tensor_scalar(vt[:, t, :], vt[:, t, :], bmv[:, t, 0:1], brs[:, t:t + 1], ALU.subtract,
                                  ALU.mult).then_inc(v_ready, 1)
            dve.wait_ge(gain_in, 16)
            dve.wait_ge(z_act, 4 * T)
            for q in range(G_GROUPS):
                dve.wait_ge(sp_ps, q // 2 + 1)
                sl = slice(q * P, (q + 1) * P)
                link(dve.tensor_tensor(tmp[:, q % 2, :, :],
                                       ps[:, 4 + q // 2, (q % 2) * SEQ:(q % 2 + 1) * SEQ].rearrange("p (t d) -> p t d", t=T),
                                       gain[:, sl].unsqueeze(1).to_broadcast([P, T, P]), ALU.mult))
                dve.scalar_tensor_tensor(ut[:, :, sl], tmp[:, q % 2, :, :], col(m, "b_sp")[:, q:q + 1], ut[:, :, sl],
                                         ALU.add, ALU.mult).then_inc(mix_ready, 1)
            dve.wait_ge(mix_ready, G_GROUPS)
            for c in range(DC):
                dve.wait_ge(mhi, 2 * (c // 2) + 2)
                dve.tensor_tensor(m.xlo[:, c, :], turned_ps(m, [0, 1, 2, 3], c), m.xhi[:, c, :].bitcast(F32),
                                  ALU.subtract).then_inc(mlo, 1)
            for h in range(2):
                add_to_x(dve, m, st, at, f"go{h}", [4 + 2 * h + t for t in range(T)], h)


def swiglu(nc, m, I, st, at, l, use):
    with ExitStack() as ctx:
        def sb(name, shape, dt=F32):
            return ctx.enter_context(nc.sbuf_tensor(f"sb_f{l}_" + name, shape, dt))

        def sem(name):
            return ctx.enter_context(nc.semaphore(f"f{l}_" + name))

        ps = m.ps
        sg, ft = sb("sg", [P, T, FW]), sb("ft", [P, T, FW])
        ahi, alo = sb("ahi", [P, FC, SEQ], F32R), sb("alo", [P, FC, SEQ], F32R)
        xhi_ready, xlo_ready, silu_ready, ft_ready, turn_ps, ahi_ready, alo_ready, sums_ready = (
            sem(s) for s in ("xhi_ready", "xlo_ready", "silu_ready", "ft_ready", "turn_ps", "ahi_ready", "alo_ready", "sums_ready"))
        g0 = at[f"ffn{l}"]
        n_gran = 3 * FN
        gain = col(m, f"ffn{l}")
        ACC, GU, TURN = (0, 1, 2, 3), (4, 5), 6
        NB = list(ACC)
        ROUND, BLOCKS = 6, 2
        TURNS = (FN - 3) // BLOCKS
        look = 2

        def shift(it, n):
            return 0 if isinstance(it, int) and it == 0 else it * n

        def w_hi(act, i, it):
            g = g0 + i
            n = st.size(g)
            act.wait_ge(st.landed[g % st.slots], shift(it, 16 * len(st.pieces[g])) + st.arrive[g])
            act.wait_ge(st.used, shift(it, ROUND) + (g - st.bufs + 1))
            act.activation(st.hi[:, g % st.bufs, 0:n], st.ring[:, g % st.slots, 0:n], ACT.Copy).then_inc(st.hi_ready, 1)

        def is_down(i):
            return i >= 2 and (i - 2) % 3 == 2 or i == n_gran - 1

        def w_lo(eng, i, it):
            g = g0 + i
            n = st.size(g)
            eng.wait_ge(st.hi_ready, shift(it, ROUND) + (g + 1))
            eng.tensor_tensor(st.lo[:, g % st.bufs, 0:n], st.ring[:, g % st.slots, 0:n],
                              st.hi[:, g % st.bufs, 0:n].bitcast(F32), ALU.subtract).then_inc(st.lows[g][0], 1)

        def lo_done(eng, i, it):
            s, n = st.lows[g0 + i]
            eng.wait_ge(s, shift(it, 2 if is_down(i) else 4) + n)

        def gu_index(b):
            return 0 if b == 0 else 2 + 3 * (b - 1)

        def down_index(b):
            return 4 + 3 * b if b < FN - 1 else n_gran - 1

        block = ctx.enter_context(nc.Block())

        @block.sync
        def _(sp):
            def load(i, it):
                g = g0 + i
                lo_done(sp, i - st.slots, it)
                for off, nk, n, src in pieces(i, it):
                    dst = st.ring[:, g % st.slots, off:off + nk * n].rearrange("p (k n) -> p k n", n=n)
                    sp.dma_start(dst, src).then_inc(st.landed[g % st.slots], 16)

            def pieces(i, it):
                if is_down(i):
                    b = (i - 2) // 3
                    src = I["ffn_w_down_2"][l, bass.ds(it * (BLOCKS * FW) + b * FW, FW), :].rearrange("(k p) n -> p k n", p=P)
                    return [(0, FC, D, src)]
                b, k = 1 + (i - 2) // 3, 4 * ((i - 2) % 3)
                rows = I["ffn_w_gu_2"][l, k * P:(k + 4) * P, :]
                return [(a * 4 * FW, 4, FW, rows[:, bass.ds(it * (BLOCKS * FW) + (a * D_FF + b * FW), FW)]
                         .rearrange("(k p) n -> p k n", p=P)) for a in range(2)]

            for i in range(st.slots, 2 + ROUND):
                st.load(sp, g0 + i)
            with sp.Fori(0, TURNS - 1) as it:
                for r in range(ROUND):
                    load(2 + ROUND + r, it)
            for i in range(2 + ROUND * TURNS, n_gran):
                st.load(sp, g0 + i)
            for g in range(g0 + n_gran, min(g0 + n_gran + st.slots, len(st.pieces))):
                st.load(sp, g)

        @block.scalar
        def _(act):
            norm_hi_act(act, m, use, NB, m.xhi, gain, xhi_ready, 0)
            norm_act(act, m, use)

            def part(b, it):
                i = gu_index(b)
                for r in range(3 if b else 2):
                    if i + r + look < n_gran:
                        w_hi(act, i + r + look, it)
                    else:
                        st.split_hi(act, g0 + n_gran)
                    if r == 1:
                        act.wait_ge(st.used, shift(it, ROUND) + (g0 + i + 2))
                        for t in range(T):
                            act.activation(sg[:, t, :], ps[:, GU[t], 0:FW], ACT.Silu, scale=m.rstd[:, t:t + 1]).then_inc(silu_ready, 1)
                act.wait_ge(turn_ps, shift(it, BLOCKS) + (b + 1))
                act.activation(ahi[:, :, :].rearrange("p c s -> p (c s)"), ps[:, TURN, :], ACT.Copy).then_inc(ahi_ready, 1)

            act.wait_ge(m.rstd_ready, use + 1)
            part(0, 0)
            with act.Fori(0, TURNS) as it:
                for b in range(1, 1 + BLOCKS):
                    part(b, it)
            for b in range(FN - 2, FN):
                part(b, 0)
            st.split_hi(act, g0 + n_gran + 1)
            act.wait_ge(st.used, g0 + n_gran)
            for h in range(2):
                act.activation(m.x[:, 0, h * BANK:(h + 1) * BANK], ps[:, ACC[h], :], ACT.Copy)

        @block.gpsimd
        def _(pool):
            norm_pool(pool, m, use)
            for i in range(look, 2 + look):
                w_lo(pool, i, 0)
            with pool.Fori(0, TURNS) as it:
                for r in range(ROUND):
                    if not is_down(2 + look + r):
                        w_lo(pool, 2 + look + r, it)
            for i in range(2 + look + ROUND * TURNS, n_gran):
                if not is_down(i):
                    w_lo(pool, i, 0)
            for g in range(g0 + n_gran, g0 + n_gran + look):
                st.split_lo(pool, g)

        @block.tensor
        def _(pe):
            turn_tokens(pe, m, m.x, NB)

            def gate_up(b, it):
                for j in range(2):
                    i = gu_index(b) + j
                    lo_done(pe, i, it)
                    whi, wlo = [x[:, (g0 + i) % st.bufs, :].rearrange("p (a k n) -> p k a n", a=2, n=FW) for x in (st.hi, st.lo)]
                    for k in range(4):
                        c = 4 * j + k
                        if b == 0:
                            pe.wait_ge(xlo_ready, c + 1)
                        for t in range(T):
                            mm = three_products(pe, ps[:, GU[t], :], m.xhi[:, c, t * P:(t + 1) * P], m.xlo[:, c, t * P:(t + 1) * P],
                                                whi[:, k, :, :], wlo[:, k, :, :], c == 0, c == DC - 1)
                    mm.then_inc(st.used, 1)

            def down(b, it):
                i = down_index(b)
                lo_done(pe, i, it)
                pe.wait_ge(alo_ready, shift(it, BLOCKS) + (b + 1))
                whi, wlo = [x[:, (g0 + i) % st.bufs, :].rearrange("p (k n) -> p k n", n=D) for x in (st.hi, st.lo)]
                for k in range(FC):
                    for t in range(T):
                        for h in range(2):
                            hs = slice(h * BANK, (h + 1) * BANK)
                            at_, al_ = ahi[:, k, t * P:(t + 1) * P], alo[:, k, t * P:(t + 1) * P]
                            out = ps[:, ACC[2 * t + h], :]
                            for a, w in ((at_, whi), (at_, wlo), (al_, whi)):
                                mm = pe.matmul(out, a, w[:, k, hs], start=False, stop=True, skip_group_check=True)
                mm.then_inc(st.used, 1)

            def turn(b, it):
                pe.wait_ge(ft_ready, shift(it, T * BLOCKS) + T * (b + 1))
                for c in range(FC):
                    for t in range(T):
                        mm = pe.transpose(ps[:, TURN, c * SEQ + t * P:c * SEQ + (t + 1) * P], ft[:, t, c * P:(c + 1) * P], m.ident)
                mm.then_inc(turn_ps, 1)

            gate_up(0, 0)
            for t in range(T):
                for h in range(2):
                    pe.matmul(ps[:, ACC[2 * t + h], :], m.ident, m.x[:, t, h * BANK:(h + 1) * BANK], start=True, stop=True)
            turn(0, 0)
            with pe.Fori(0, TURNS) as it:
                for b in range(1, 1 + BLOCKS):
                    gate_up(b, it)
                    down(b - 1, it)
                    turn(b, it)
            for b in range(FN - 2, FN):
                gate_up(b, 0)
                down(b - 1, 0)
                turn(b, 0)
            down(FN - 1, 0)

        @block.vector
        def _(dve):
            norm_lo_dve(dve, m, use, NB, m.xhi, m.xlo, gain, xhi_ready, xlo_ready, 0)

            def part(b, it):
                i = gu_index(b)
                for r in range(3 if b else 2):
                    if i + r + look < n_gran and is_down(i + r + look):
                        w_lo(dve, i + r + look, it)
                for t in range(T):
                    dve.wait_ge(silu_ready, shift(it, T * BLOCKS) + (T * b + t + 1))
                    dve.scalar_tensor_tensor(ft[:, t, :], ps[:, GU[t], FW:], m.rstd[:, t:t + 1], sg[:, t, :], ALU.mult,
                                             ALU.mult).then_inc(ft_ready, 1)
                dve.wait_ge(ahi_ready, shift(it, BLOCKS) + (b + 1))
                dve.tensor_tensor(alo[:, :, :].rearrange("p c s -> p (c s)"), ps[:, TURN, :],
                                  ahi[:, :, :].rearrange("p c s -> p (c s)").bitcast(F32), ALU.subtract).then_inc(alo_ready, 1)

            dve.wait_ge(m.rstd_ready, use + 1)
            part(0, 0)
            with dve.Fori(0, TURNS) as it:
                for b in range(1, 1 + BLOCKS):
                    part(b, it)
            for b in range(FN - 2, FN):
                part(b, 0)
            dve.wait_ge(st.used, g0 + n_gran)
            for h in range(2):
                dve.tensor_copy(m.x[:, 1, h * BANK:(h + 1) * BANK], ps[:, ACC[2 + h], :])


def diff_attention(nc, m, I, st, at, use):
    with ExitStack() as ctx:
        def sb(name, shape, dt=F32):
            return ctx.enter_context(nc.sbuf_tensor("sb_" + name, shape, dt))

        def sem(name):
            return ctx.enter_context(nc.semaphore(name))

        ps = m.ps
        khi, klo = sb("d_khi", [P, DC, SEQ], F32R), sb("d_klo", [P, DC, SEQ], F32R)
        yhi, ylo = sb("d_yhi", [P, DC, SEQ], F32R), sb("d_ylo", [P, DC, SEQ], F32R)
        qt, kt, vt = sb("d_q", [P, T, D]), sb("d_k", [P, T, D]), sb("d_v", [P, T, D])
        dist, lam_in_ = sb("dist", [P, 3 * P]), sb("lam_in", [P, N_LAM])
        lam, lamw = sb("lam", [P, 8]), sb("lamw", [P, 2 * D_DIM])
        sub = sb("sub", [P, 1])
        qkT = sb("d_qkT", [P, 2, SEQ])
        bias = sb("d_bias", [P, 2, 3 * P])
        e = sb("d_e", [P, 2, 3 * P])
        eT = sb("d_eT", [P, 3 * P])
        mx, sm = sb("d_mx", [P, 2, 4]), sb("d_sm", [P, 2, 4])
        ost, on = sb("d_ost", [P, 3, T]), sb("d_on", [P, T, D_V])
        xhi_ready, xlo_ready, z_act, dist_in, lam_in, dve_step, pool_step = (
            sem(s) for s in ("d_xhi_ready", "d_xlo_ready", "d_z_act", "d_dist_in", "d_lam_in", "d_dve_step", "d_pool_step"))
        lsum_ready, lexp_ready, lam_ready = sem("lsum_ready"), sem("lexp_ready"), sem("lam_ready")
        bias_ready, qk_ps, qkT_ready, s_ps, mx_ready, e_ready, a_ready, aT_ps, aT_ready, o_ps, osum_ready, ors_ready, on_ready, oT_ps, ohi, olo = (
            sem(s) for s in ("bias_ready", "d_qk_ps", "d_qkT_ready", "s_ps", "d_mx_ready", "e_ready", "a_ready", "aT_ps",
                             "aT_ready", "o_ps", "osum_ready", "ors_ready", "on_ready", "oT_ps", "ohi", "olo"))
        order = ["q0", "k0", "w0", "q1", "k1", "w1"]
        fill = [[("q1", 0, None), ("q1", 1, None)]]
        fill += [[(name, j, 0), (name, j, 1)] for name, j in (("k1", 0), ("k1", 1), ("w1", 0), ("w1", 1), ("o0", 0), ("o1", 0))]
        fill += [[None, ("o0", 1, 0)], [None, ("o1", 1, 0)]]
        tail = (("o0", 1, 1), ("o1", 1, 1))
        first, last = at["q0"][0], at["o1"][-1]
        look = 2
        NB = [4, 5, 6, 7]
        QK, S, AO = 4, (5, 6), 7
        SCALE = float(D_DIM) ** -0.5
        slopes = [2.0 ** (-8.0 * (h + 1) / D_HEADS) for h in range(D_HEADS)]
        spans = [slice(0, P), slice(P, 3 * P)]
        block = ctx.enter_context(nc.Block())

        def zb(name):
            i = order.index(name) if name in order else int(name[1])
            return [2 * (i % 2) + t for t in range(T)]

        def z_done(name):
            return T * (order.index(name) + 1)

        def ended(s, n):
            f = fill[s][n]
            return [at[f[0]][f[1]]] if f is not None and f[2] != 0 else []

        @block.sync
        def _(sp):
            sp.dma_start(dist[:, :], I["c_late"][:, 0:3 * P]).then_inc(dist_in, 16)
            sp.dma_start(lam_in_[:, :], I["v_lam"]).then_inc(lam_in, 16)
            for g in range(first + st.slots, last + 1 + st.slots):
                st.load(sp, g)

        @block.scalar
        def _(act):
            def evac(name):
                act.wait_ge(st.used, at[name][-1] + 1)
                for t in range(T):
                    dst = {"q": qt, "k": kt, "w": vt}[name[0]][:, t, int(name[1]) * BANK:(int(name[1]) + 1) * BANK]
                    act.activation(dst, ps[:, zb(name)[t], :], ACT.Copy, scale=m.rstd[:, t:t + 1]).then_inc(z_act, 1)

            for b in range(4):
                act.wait_ge(m.xturn_ps, 4 * use + b + 1)
                for hi, name in ((m.xhi, "bq"), (khi, "kv")):
                    for c in (2 * b, 2 * b + 1):
                        act.activation(hi[:, c, :], turned_ps(m, NB, c), ACT.Copy,
                                       scale=col(m, name)[:, c:c + 1]).then_inc(xhi_ready, 1)
            norm_act(act, m, use)
            act.wait_ge(lsum_ready, 1)
            act.activation(lam[:, 2:4], lam[:, 0:2], ACT.Exp).then_inc(lexp_ready, 1)
            act.wait_ge(m.rstd_ready, use + 1)
            for name in order[:3]:
                for g in at[name]:
                    st.split_hi(act, g + look)
                evac(name)
            for s in range(D_HEADS + 1):
                if s >= 1 and fill[s - 1][1][0] in order and fill[s - 1][1][1] == 1:
                    evac(fill[s - 1][1][0])
                if s < D_HEADS:
                    act.wait_ge(qk_ps, s + 1)
                    if s >= 1:
                        act.wait_ge(s_ps, s)
                    act.activation(qkT[:, :, :].rearrange("p a s -> p (a s)"), ps[:, QK, :], ACT.Copy).then_inc(qkT_ready, 1)
                if s >= 1:
                    act.wait_ge(aT_ps, s)
                    act.activation(eT[:, :], ps[:, AO, 0:3 * P], ACT.Copy).then_inc(aT_ready, 1)
                for g in ended(s, 0):
                    st.split_hi(act, g + look)
                if s >= 1:
                    act.wait_ge(o_ps, s)
                    for t in range(T):
                        act.activation(on[:, t, :], ps[:, AO, t * P:(t + 1) * P], ACT.Square,
                                       accum_out=ost[:, 0, t:t + 1]).then_inc(osum_ready, 1)
                if s < D_HEADS:
                    act.wait_ge(mx_ready, s + 1)
                    for i in range(2):
                        for t in range(T):
                            act.activation(e[:, i, spans[t]], e[:, i, spans[t]], ACT.Exp, bias=mx[:, 1, 2 * i + t:2 * i + t + 1],
                                           scale=SCALE, accum_out=sm[:, 0, 2 * i + t:2 * i + t + 1]).then_inc(e_ready, 1)
                if s >= 1:
                    act.wait_ge(oT_ps, s)
                    act.activation(yhi[:, s - 1, :], ps[:, AO, SEQ:], ACT.Copy, scale=sub[:, 0:1]).then_inc(ohi, 1)
                for g in ended(s, 1):
                    st.split_hi(act, g + look)
            for name, j, _ in tail:
                st.split_hi(act, at[name][j] + look)

        @block.gpsimd
        def _(pool):
            n_step = [0]

            def link(ins):
                n_step[0] += 1
                ins.then_inc(pool_step, 1)
                pool.wait_ge(pool_step, n_step[0])

            def bias_of(h):
                if h >= 2:
                    pool.wait_ge(mx_ready, h - 1)
                pool.tensor_scalar(bias[:, h % 2, :], dist[:, :], slopes[h] / SCALE, None, ALU.mult).then_inc(bias_ready, 1)

            norm_pool(pool, m, use)
            for name in order[:3]:
                for g in at[name]:
                    st.split_lo(pool, g + look)
            pool.wait_ge(dist_in, 16)
            bias_of(0)
            bias_of(1)
            for s in range(1, D_HEADS + 1):
                pool.wait_ge(osum_ready, T * s)
                link(pool.tensor_scalar(ost[:, 1, :], ost[:, 0, :], 1.0 / D_V, EPS, ALU.mult, ALU.add))
                pool.tensor_tensor(ost[:, 2, :], ost[:, 1, :], m.half[:, 0:T], ALU.pow).then_inc(ors_ready, 1)
                if s + 1 < D_HEADS:
                    bias_of(s + 1)
            for name, j, _ in tail:
                st.split_lo(pool, at[name][j] + look)

        @block.tensor
        def _(pe):
            def granule(name, j, part=None):
                if j == 0 and name[0] == "o":
                    pe.wait_ge(z_act, z_done(("k1", "w1")[int(name[1])]))
                elif j == 0 and order.index(name) >= 2:
                    pe.wait_ge(z_act, z_done(order[order.index(name) - 2]))
                if name[0] == "o":
                    pe.wait_ge(olo, 4 * j + (2 if part == 0 else 4))
                hi, lo = {"q": (m.xhi, m.xlo), "o": (yhi, ylo)}.get(name[0], (khi, klo))
                turned = {"q0": (xlo_ready, [4 * (c // 2) + c % 2 + 1 for c in range(DC)]),
                          "k0": (xlo_ready, [4 * (c // 2) + c % 2 + 3 for c in range(DC)])}.get(name)
                dense_granule(pe, st, at[name][j], [ps[:, b, :] for b in zb(name)], hi, lo, 4 * j, BANK, j == 0, j == 1, turned, part)

            turn_tokens(pe, m, m.x, NB)
            for name in order[:3]:
                for j in range(2):
                    granule(name, j)
            pe.wait_ge(xlo_ready, 2 * DC)
            for s in range(D_HEADS + 1):
                if s < D_HEADS:
                    pe.wait_ge(z_act, z_done("k1" if s >= 4 else "k0"))
                    if s >= 1:
                        pe.wait_ge(qkT_ready, s)
                    for a, src in ((0, qt), (1, kt)):
                        for t in range(T):
                            mm = pe.transpose(ps[:, QK, a * SEQ + t * P:a * SEQ + (t + 1) * P], src[:, t, s * P:(s + 1) * P], m.ident)
                    mm.then_inc(qk_ps, 1)
                if s >= 1:
                    pe.wait_ge(a_ready, s)
                    if s >= 2:
                        pe.wait_ge(olo, s - 1)
                    for n in range(3):
                        mm = pe.transpose(ps[:, AO, n * P:(n + 1) * P], e[:, 0, n * P:(n + 1) * P], m.ident)
                    mm.then_inc(aT_ps, 1)
                if fill[s][0] is not None:
                    granule(*fill[s][0])
                if s < D_HEADS:
                    pe.wait_ge(qkT_ready, s + 1)
                    for i in range(2):
                        r = slice(i * D_DIM, (i + 1) * D_DIM)
                        for t in range(T):
                            mm = pe.matmul(ps[:, S[i], spans[t]], qkT[r, 0, t * P:(t + 1) * P], qkT[r, 1, 0:(t + 1) * P],
                                           start=True, stop=True)
                    mm.then_inc(s_ps, 1)
                if s >= 1:
                    h = s - 1
                    pe.wait_ge(aT_ready, s)
                    pe.wait_ge(z_act, z_done("w1" if h >= 4 else "w0"))
                    v = [vt[:, k, h * P:(h + 1) * P] for k in range(T)]
                    pe.matmul(ps[:, AO, 0:P], eT[:, 0:P], v[0], start=True, stop=True)
                    pe.matmul(ps[:, AO, P:2 * P], eT[:, P:2 * P], v[0], start=True, stop=False)
                    pe.matmul(ps[:, AO, P:2 * P], eT[:, 2 * P:], v[1], start=False, stop=True).then_inc(o_ps, 1)
                granule(*fill[s][1])
                if s >= 1:
                    pe.wait_ge(on_ready, T * s)
                    for t in range(T):
                        mm = pe.transpose(ps[:, AO, SEQ + t * P:SEQ + (t + 1) * P], on[:, t, :], m.ident)
                    mm.then_inc(oT_ps, 1)
            for f in tail:
                granule(*f)

        @block.vector
        def _(dve):
            n_step = [0]

            def link(ins):
                n_step[0] += 1
                ins.then_inc(dve_step, 1)
                dve.wait_ge(dve_step, n_step[0])

            dve.wait_ge(lam_in, 16)
            for i in range(2):
                a = lam_in_[:, 2 * i * D_DIM:(2 * i + 1) * D_DIM]
                b = lam_in_[:, (2 * i + 1) * D_DIM:(2 * i + 2) * D_DIM]
                ins = dve.tensor_tensor_reduce(lamw[:, i * D_DIM:(i + 1) * D_DIM], a, b, 1.0, 0.0, ALU.mult, ALU.add, lam[:, i:i + 1])
            ins.then_inc(lsum_ready, 1)
            for b in range(4):
                dve.wait_ge(xhi_ready, 4 * b + 4)
                for hi, lo, name in ((m.xhi, m.xlo, "bq"), (khi, klo, "kv")):
                    for c in (2 * b, 2 * b + 1):
                        dve.scalar_tensor_tensor(lo[:, c, :], turned_ps(m, NB, c), col(m, name)[:, c:c + 1],
                                                 hi[:, c, :].bitcast(F32), ALU.mult, ALU.subtract).then_inc(xlo_ready, 1)
            dve.wait_ge(lexp_ready, 1)
            link(dve.tensor_tensor(lam[:, 4:5], lam[:, 3:4], lam[:, 2:3], ALU.subtract))
            link(dve.tensor_scalar(lam[:, 5:6], lam[:, 4:5], -LAMBDA_INIT, None, ALU.add))
            dve.tensor_scalar(sub[:, :], col(m, "subln"), 1.0 - LAMBDA_INIT, None, ALU.mult).then_inc(lam_ready, 1)
            dve.wait_ge(lam_ready, 1)
            for s in range(D_HEADS + 1):
                if s < D_HEADS:
                    dve.wait_ge(s_ps, s + 1)
                    dve.wait_ge(bias_ready, s + 1)
                    if s >= 1:
                        dve.wait_ge(aT_ps, s)
                    for i in range(2):
                        for t in range(T):
                            ins = dve.tensor_tensor_reduce(e[:, i, spans[t]], ps[:, S[i], spans[t]], bias[:, s % 2, spans[t]], 1.0,
                                                           -3e38, ALU.add, ALU.max, mx[:, 0, 2 * i + t:2 * i + t + 1])
                    link(ins)
                    dve.tensor_scalar(mx[:, 1, :], mx[:, 0, :], -SCALE, None, ALU.mult).then_inc(mx_ready, 1)
                if s >= 1:
                    dve.wait_ge(ors_ready, s)
                    for t in range(T):
                        dve.tensor_scalar(on[:, t, :], ps[:, AO, t * P:(t + 1) * P], ost[:, 2, t:t + 1], None,
                                          ALU.mult).then_inc(on_ready, 1)
                if s < D_HEADS:
                    dve.wait_ge(e_ready, 4 * (s + 1))
                    link(dve.reciprocal(sm[:, 1, :], sm[:, 0, :]))
                    link(dve.tensor_scalar(sm[:, 1, 2:4], sm[:, 1, 2:4], lam[:, 5:6], None, ALU.mult))
                    for t in range(T):
                        ins = dve.tensor_scalar(e[:, 0, spans[t]], e[:, 0, spans[t]], sm[:, 1, t:t + 1], None, ALU.mult)
                    link(ins)
                    for t in range(T):
                        ins = dve.scalar_tensor_tensor(e[:, 0, spans[t]], e[:, 1, spans[t]], sm[:, 1, 2 + t:3 + t], e[:, 0, spans[t]],
                                                       ALU.mult, ALU.add)
                    ins.then_inc(a_ready, 1)
                if s >= 1:
                    dve.wait_ge(ohi, s)
                    dve.scalar_tensor_tensor(ylo[:, s - 1, :], ps[:, AO, SEQ:], sub[:, 0:1], yhi[:, s - 1, :].bitcast(F32),
                                             ALU.mult, ALU.subtract).then_inc(olo, 1)
                for g in ended(s, 0) + ended(s, 1):
                    st.split_lo(dve, g + look)
            for h in range(2):
                add_to_x(dve, m, st, at, f"o{h}", zb(f"o{h}"), h)


def final_norm(nc, m, I, out, use):
    with ExitStack() as ctx:
        gain = ctx.enter_context(nc.sbuf_tensor("sb_final_gain", [P, D], F32))
        gain_in, y_ready = ctx.enter_context(nc.semaphore("final_gain_in")), ctx.enter_context(nc.semaphore("y_ready"))
        block = ctx.enter_context(nc.Block())
        dram = out[0].rearrange("(t p) d -> p t d", p=P)

        @block.sync
        def _(sp):
            sp.dma_start(gain[:, :], I["final_norm_2"].partition_broadcast(P)).then_inc(gain_in, 16)
            for t in range(T):
                sp.wait_ge(y_ready, t + 1)
                sp.dma_start(dram[:, t, :], m.xs[:, t, :]).then_inc(m.out_done, 16)
            sp.wait_ge(m.out_done, 16 * T)

        @block.scalar
        def _(act):
            norm_act(act, m, use)

        @block.gpsimd
        def _(pool):
            norm_pool(pool, m, use)

        @block.vector
        def _(dve):
            dve.wait_ge(m.rstd_ready, use + 1)
            dve.wait_ge(gain_in, 16)
            for t in range(T):
                dve.scalar_tensor_tensor(m.xs[:, t, :], m.x[:, t, :], m.rstd[:, t:t + 1], gain[:, :], ALU.mult,
                                         ALU.mult).then_inc(y_ready, 1)



def program(nc, I, out):
    m = Shared()
    with ExitStack() as ctx:
        def sb(name, shape, dt=F32):
            return ctx.enter_context(nc.sbuf_tensor("sb_" + name, shape, dt))

        def sem(name):
            return ctx.enter_context(nc.semaphore(name))

        m.ps = ctx.enter_context(nc.psum_tensor("ps", [P, 8, BANK], F32))
        m.x, m.xs = sb("x", [P, T, D]), sb("xs", [P, T, D])
        m.sumsq, m.meansq, m.rstd = sb("sumsq", [P, T]), sb("meansq", [P, T]), sb("rstd", [P, T])
        m.consts, m.cols, m.rows = sb("consts", [P, N_CONSTS]), sb("cols", [P, N_COLS]), sb("rows", [P, N_ROWS])
        m.ident, m.half = const(m, "ident"), const(m, "half")
        m.sumsq_ready, m.meansq_ready, m.rstd_ready = sem("sumsq_ready"), sem("meansq_ready"), sem("rstd_ready")
        m.xturn_ps, m.out_done = sem("xturn_ps"), sem("out_done")
        m.ring = sb("ring", [P, EARLY * GK * E_FF])
        m.e_landed = [sem(f"e_landed{i}") for i in range(NS)]
        st, at = second_stream(m, ctx, nc, I)
        mixer(nc, m, I)
        experts(nc, m, I, st)
        m.xhi, m.xlo = sb("xhi2", [P, DC, SEQ], F32R), sb("xlo2", [P, DC, SEQ], F32R)
        st.place_halves(ctx, nc, "net")
        gmlp(nc, m, I, st, at, 2)
        swiglu(nc, m, I, st, at, 0, 3)
        diff_attention(nc, m, I, st, at, 4)
        swiglu(nc, m, I, st, at, 1, 5)
        final_norm(nc, m, I, out, 6)


_INS = ["x", "w_in", "w_a_out", "w_b_out", "w_uq", "w_ukv", "w_c_out", "w_out", "w_router", "w_e_gate", "w_e_up",
        "w_e_down", "a_w_in_2", "a_v_norm_2", "a_w_out_2", "ffn_w_gu_2", "ffn_w_down_2", "kv_w_2",
        "b_w_q_2", "b_w_o_2", "final_norm_2"]


def constants():
    import numpy as np

    i = np.arange(P)
    a, b = i[:, None], i[None, :]
    z = np.zeros((P, P))
    ang = (np.arange(SEQ, dtype=np.float32)[:, None]
           * (np.float32(10000.0) ** (-np.arange(0, C_ROPE, 2, dtype=np.float32) / C_ROPE))[None, :])
    turn = lambda y: y.reshape(T, P, 16).transpose(1, 0, 2).reshape(P, T * 16)
    c = {
        "ident": a == b, "upto": a <= b, "from": a >= b, "ones": z + 1,
        "causal": np.concatenate([z, np.where(b <= a, 0, NEG)], 1),
        "anti": np.concatenate([np.where(b >= a, 0, NEG), z], 1),
        "cos": turn(np.cos(ang)), "sin": turn(np.sin(ang)),
        "half": z[:, :8] - 0.5,
    }
    dist = np.concatenate([np.where(b <= a, b - a, NEG), b - a - P, np.where(b <= a, b - a, NEG)], 1)
    late = np.concatenate([dist, z[:, :CAP] + np.arange(1, CAP + 1)], 1)
    sel = np.zeros((8, 8, P), np.float32)
    sel[np.arange(8), np.arange(8)] = 1
    return np.concatenate([c[n] for n in CONSTS], 1).astype(np.float32), sel, late.astype(np.float32)


def arrays_of(inputs):
    import numpy as np

    f = {k: np.asarray(v) for k, v in inputs.items()}
    vec = {"mix": f["mix_norm_g"], "a_norm": f["a_norm_g"], "conv_w": f["conv_w"], "conv_b": f["conv_b"],
           "ln_g": f["conv_ln_g"], "ln_b": f["conv_ln_b"], "cq": f["cq_norm_g"], "ckv": f["ckv_norm_g"],
           "ffn": f["ffn_norm_g"], "gmlp": f["a_norm_2"], "ffn0": f["ffn_norm_2"][0], "ffn1": f["ffn_norm_2"][1],
           "kv": f["kv_norm_2"], "bq": f["b_norm_2"], "b_sp": f["a_b_sp_2"], "subln": f["b_subln_2"]}
    rows = {"b_if": f["b_if"], "q_g": f["q_norm_g"], "k_g": f["k_norm_g"]}
    arrays = {n: np.ascontiguousarray(f[n]) for n in _INS}
    arrays["w_spT"] = np.ascontiguousarray(f["a_w_sp_2"][0].transpose(2, 0, 1))
    arrays["v_cols"] = np.ascontiguousarray(np.concatenate([vec[n].reshape(-1, P).T for n in COLS], 1))
    line = np.concatenate([rows[n].reshape(-1) for n in ROWS])
    arrays["v_rows"] = np.ascontiguousarray(np.broadcast_to(line, (P, N_ROWS)))
    arrays["v_lam"] = np.ascontiguousarray(np.broadcast_to(f["b_lambda_2"].reshape(-1), (P, N_LAM)))
    arrays["c_consts"], arrays["c_sel"], arrays["c_late"] = constants()
    return arrays


def kernel(**inputs):
    import numpy as np
    import concourse.bacc as bacc
    from concourse.bass_utils import run_bass_kernel_spmd

    nc = bacc.Bacc("TRN2", target_bir_lowering=False, num_devices=1)
    arrays = arrays_of(inputs)
    I = {n: nc.dram_tensor(n, a.shape, mybir.dt.from_np(a.dtype), kind="ExternalInput").ap() for n, a in arrays.items()}
    out = nc.dram_tensor("out", (1, SEQ, D), F32, kind="ExternalOutput").ap()
    program(nc, I, out)
    return run_bass_kernel_spmd(nc, [arrays], core_ids=[0]).results[0]["out"]
```

```python
from contextlib import ExitStack

import concourse.bass as bass
from concourse import mybir

F32 = mybir.dt.float32
F32R = mybir.dt.float32r
ALU = mybir.AluOpType
ACT = mybir.ActivationFunctionType
AX = mybir.AxisListType

P = 128
SEQ = 256
T = SEQ // P
D = 1024
DC = D // P
EPS = 1e-6
BANK = 512

A_HEADS, A_DIM = 4, 128
A_W = A_HEADS * A_DIM
B_W, B_TAPS = 512, 31
B_PAD = B_TAPS // 2
C_HEADS, C_NOPE, C_ROPE, C_V = 8, 64, 32, 64
C_QK = C_NOPE + C_ROPE
C_QR, C_KVR = 384, 256
N_EXP, E_FF = 16, 1536
CAP = 2 * SEQ // N_EXP

Z_Q = 0
Z_K = Z_Q + A_W
Z_V = Z_K + A_W
Z_O = Z_V + A_W
Z_G = Z_O + A_W
Z_UA = Z_G + 4 * A_HEADS
Z_UG = Z_UA + B_W
Z_CQ = Z_UG + B_W
Z_CKV = Z_CQ + C_QR
Z_GTS = Z_CKV + C_KVR + C_ROPE

D_FF = 2816
LAMBDA_INIT = 0.8 - 0.6 * 0.7408182206817179
NEG = -1e30

G_GROUPS = 8
D_HEADS, D_DIM, D_V = 8, 64, 128

COLS = {}
_at = 0
for _name, _n in (("mix", DC), ("a_norm", A_HEADS), ("conv_w", B_TAPS * 4), ("conv_b", 4),
                  ("ln_g", 4), ("ln_b", 4), ("cq", C_QR // P), ("ckv", C_KVR // P), ("ffn", DC),
                  ("gmlp", DC), ("ffn0", DC), ("ffn1", DC), ("kv", DC), ("bq", DC),
                  ("b_sp", G_GROUPS), ("subln", 1)):
    COLS[_name] = (_at, _n)
    _at += _n
N_COLS = _at
ROWS = {"b_if": (0, 16), "q_g": (16, C_QK), "k_g": (16 + C_QK, C_QK)}
N_ROWS = 16 + 2 * C_QK
N_LAM = 4 * D_DIM
CONSTS = {}
_at = 0
for _name, _n in (("ident", P), ("half", 8), ("upto", P), ("ones", P), ("from", P), ("causal", 2 * P),
                  ("anti", 2 * P), ("cos", T * 16), ("sin", T * 16)):
    CONSTS[_name] = (_at, _n)
    _at += _n
N_CONSTS = _at


class Shared:
    pass


class Stream:

    def __init__(self, ctx, nc, name, ring, hi_bufs, lo_bufs):
        self.ring, self.slots, self.hi_bufs, self.lo_bufs = ring, ring.shape[1], hi_bufs, lo_bufs
        self.hi = self.lo = None
        self.landed = [ctx.enter_context(nc.semaphore(f"{name}_landed{i}")) for i in range(self.slots)]
        self.hi_ready = ctx.enter_context(nc.semaphore(f"{name}_hi_ready"))
        self.lo_pool = ctx.enter_context(nc.semaphore(f"{name}_lo_pool"))
        self.lo_dve = ctx.enter_context(nc.semaphore(f"{name}_lo_dve"))
        self.used = ctx.enter_context(nc.semaphore(f"{name}_used"))
        self.pieces, self.arrive, self.lows = [], [], []
        self.n_pool = self.n_dve = 0
        self.slot_sum = [0] * self.slots

    def place_halves(self, ctx, nc, name):
        self.hi = ctx.enter_context(nc.sbuf_tensor(f"{name}_whi", [P, self.hi_bufs, 2048], F32R))
        self.lo = ctx.enter_context(nc.sbuf_tensor(f"{name}_wlo", [P, self.lo_bufs, 2048], F32R))

    def add(self, pieces, by_dve=False):
        g = len(self.pieces)
        self.pieces.append(pieces)
        self.slot_sum[g % self.slots] += 16 * len(pieces)
        self.arrive.append(self.slot_sum[g % self.slots])
        if by_dve:
            self.n_dve += 1
            self.lows.append((self.lo_dve, self.n_dve))
        else:
            self.n_pool += 1
            self.lows.append((self.lo_pool, self.n_pool))
        return g

    def size(self, g):
        return sum(nk * n for _, nk, n, _ in self.pieces[g])

    def load(self, sp, g):
        if g >= self.slots:
            sp.wait_ge(*self.lows[g - self.slots])
        for off, nk, n, src in self.pieces[g]:
            dst = self.ring[:, g % self.slots, off:off + nk * n].rearrange("p (k n) -> p k n", n=n)
            sp.dma_start(dst, src).then_inc(self.landed[g % self.slots], 16)

    def split_hi(self, act, g):
        if g >= len(self.pieces):
            return
        n = self.size(g)
        act.wait_ge(self.landed[g % self.slots], self.arrive[g])
        if g >= self.hi_bufs:
            act.wait_ge(self.used, g - self.hi_bufs + 1)
        act.activation(self.hi[:, g % self.hi_bufs, 0:n], self.ring[:, g % self.slots, 0:n],
                       ACT.Copy).then_inc(self.hi_ready, 1)

    def split_lo(self, eng, g):
        if g >= len(self.pieces):
            return
        n = self.size(g)
        eng.wait_ge(self.hi_ready, g + 1)
        if g >= self.lo_bufs and self.lo_bufs < self.hi_bufs:
            eng.wait_ge(self.used, g - self.lo_bufs + 1)
        eng.tensor_tensor(self.lo[:, g % self.lo_bufs, 0:n], self.ring[:, g % self.slots, 0:n],
                          self.hi[:, g % self.hi_bufs, 0:n].bitcast(F32),
                          ALU.subtract).then_inc(self.lows[g][0], 1)

    def views(self, g, n):
        nk = self.size(g) // n
        return [x[:, g % bufs, 0:nk * n].rearrange("p (k n) -> p k n", n=n)
                for x, bufs in ((self.hi, self.hi_bufs), (self.lo, self.lo_bufs))]


def three_products(pe, out, hi, lo, whi, wlo, start, stop):
    pe.matmul(out, hi, whi, start=start, stop=False)
    pe.matmul(out, hi, wlo, start=False, stop=False)
    return pe.matmul(out, lo, whi, start=False, stop=stop)


def dense_granule(pe, st, g, outs, hi, lo, k0, n, first, last, turned=None, part=None):
    whi, wlo = st.views(g, n)
    nk = whi.shape[1]
    begin, end = part or (0, nk)
    if begin == 0:
        pe.wait_ge(*st.lows[g])
    for k in range(begin, end):
        if turned is not None:
            pe.wait_ge(turned[0], turned[1][k0 + k])
        for t in range(T):
            mm = three_products(pe, outs[t], hi[:, k0 + k, t * P:(t + 1) * P], lo[:, k0 + k, t * P:(t + 1) * P],
                                whi[:, k, :], wlo[:, k, :], first and k == 0, last and k == nk - 1)
    if end == nk:
        mm.then_inc(st.used, 1)



def norm_act(act, m, n, tiles=range(T)):
    for t in tiles:
        act.activation(m.xs[:, t, :], m.x[:, t, :], ACT.Square,
                       accum_out=m.sumsq[:, t:t + 1]).then_inc(m.sumsq_ready, 1)


def norm_pool(pool, m, n):
    pool.wait_ge(m.sumsq_ready, T * (n + 1))
    pool.tensor_scalar(m.meansq[:, :], m.sumsq[:, :], 1.0 / D, EPS, ALU.mult, ALU.add).then_inc(m.meansq_ready, 1)
    pool.wait_ge(m.meansq_ready, n + 1)
    pool.tensor_tensor(m.rstd[:, :], m.meansq[:, :], m.half[:, 0:T], ALU.pow).then_inc(m.rstd_ready, 1)


def norm_pool_tile(pool, m, n, t):
    pool.wait_ge(m.sumsq_ready, T * n + t + 1)
    pool.tensor_scalar(m.meansq[:, t:t + 1], m.sumsq[:, t:t + 1], 1.0 / D, EPS, ALU.mult, ALU.add).then_inc(m.meansq_ready, 1)
    pool.wait_ge(m.meansq_ready, n + t + 1)
    pool.tensor_tensor(m.rstd[:, t:t + 1], m.meansq[:, t:t + 1], m.half[:, 0:1], ALU.pow).then_inc(m.rstd_ready, 1)


def turn_tokens(pe, m, src, banks):
    for b in range(DC // 2):
        for cc in range(2):
            for t in range(T):
                c = 2 * b + cc
                mm = pe.transpose(m.ps[:, banks[b], cc * SEQ + t * P:cc * SEQ + (t + 1) * P],
                                  src[:, t, c * P:(c + 1) * P], m.ident)
        mm.then_inc(m.xturn_ps, 1)


def turned_ps(m, banks, c):
    return m.ps[:, banks[c // 2], (c % 2) * SEQ:(c % 2 + 1) * SEQ]


def norm_hi_act(act, m, n, banks, hi, gain, ready, base):
    for c in range(DC):
        act.wait_ge(m.xturn_ps, (DC // 2) * n + c // 2 + 1)
        act.activation(hi[:, c, :], turned_ps(m, banks, c), ACT.Copy, scale=gain[:, c:c + 1]).then_inc(ready, 1)


def norm_lo_dve(dve, m, n, banks, hi, lo, gain, hi_ready, lo_ready, base):
    for c in range(DC):
        dve.wait_ge(hi_ready, base + 2 * (c // 2) + 2)
        dve.scalar_tensor_tensor(lo[:, c, :], turned_ps(m, banks, c), gain[:, c:c + 1],
                                 hi[:, c, :].bitcast(F32), ALU.mult, ALU.subtract).then_inc(lo_ready, 1)


def chunks(w, k0, nk, n0, n):
    return w[k0 * P:(k0 + nk) * P, n0:n0 + n].rearrange("(k p) n -> p k n", p=P)


def col(m, name):
    a, n = COLS[name]
    return m.cols[:, a:a + n]


def row(m, name):
    a, n = ROWS[name]
    return m.rows[:, a:a + n]


def const(m, name):
    a, n = CONSTS[name]
    return m.consts[:, a:a + n]



def mixer(nc, m, I):
    with ExitStack() as ctx:
        def sb(name, shape, dt=F32):
            return ctx.enter_context(nc.sbuf_tensor("sb_" + name, shape, dt))

        def sem(name):
            return ctx.enter_context(nc.semaphore(name))

        ring = sb("mix_ring", [P, 3, 2048])
        st = Stream(ctx, nc, "mix", ring[:, :, :], 3, 2)
        st.place_halves(ctx, nc, "mix")
        ps = m.ps

        blocks = {}

        ALL, FIRST = (0, 4), (0,)

        def dense(name, w, k_chunks, per, n0, n, by_dve=()):
            blocks[name] = [(st.add([(0, per, n, chunks(w, k, per, n0, n))], k in by_dve), k, per, n)
                            for k in range(0, k_chunks, per)]

        w_in = I["w_in"][0]
        dense("cq", w_in, DC, 4, Z_CQ, C_QR, ALL)
        dense("ckv", w_in, DC, 4, Z_CKV, C_KVR + C_ROPE, ALL)
        dense("g", w_in, DC, 8, Z_G, 4 * A_HEADS, ALL)
        dense("ug", w_in, DC, 4, Z_UG, B_W, ALL)
        dense("ua", w_in, DC, 4, Z_UA, B_W, ALL)
        dense("uq0", I["w_uq"][0], C_QR // P, 3, 0, 384)
        dense("uq1", I["w_uq"][0], C_QR // P, 3, 384, 384)
        dense("ukv0", I["w_ukv"][0], C_KVR // P, 2, 0, 512)
        dense("q", w_in, DC, 4, Z_Q, A_W, FIRST)
        dense("ukv1", I["w_ukv"][0], C_KVR // P, 2, 512, 512)
        dense("k", w_in, DC, 4, Z_K, A_W)
        dense("v", w_in, DC, 4, Z_V, A_W)
        dense("o", w_in, DC, 4, Z_O, A_W)
        for j in range(6):
            dense(f"gt{j}", w_in, DC, 4, Z_GTS + j * 512, 512)
        for br, w in (("a", I["w_a_out"][0]), ("b", I["w_b_out"][0]), ("c", I["w_c_out"][0])):
            for h in range(2):
                dense(f"y{br}{h}", w, 4, 4, h * 512, 512)
        for h in range(2):
            dense(f"out{h}", I["w_out"][0], DC, 4, h * 512, 512)
        order = list(blocks)
        n_gran = len(st.pieces)

        used_up = [0]

        def early(*shape):
            n = 1
            for d in shape[1:]:
                n *= d
            view = m.ring[:, used_up[0]:used_up[0] + n]
            used_up[0] += n
            dims = " ".join(f"d{i}" for i in range(len(shape) - 1))
            sizes = {f"d{i}": shape[1 + i] for i in range(1, len(shape) - 1)}
            return view.rearrange(f"p ({dims}) -> p {dims}", **sizes)

        m.sel = sb("sel", [8, 8, P])
        xhi, xlo = sb("xhi", [P, DC, SEQ], F32R), sb("xlo", [P, DC, SEQ], F32R)
        gates = early(P, T, 2, 2, A_HEADS)
        fabs = early(P, T * 2 * A_HEADS)
        fexp = early(P, T * 2 * A_HEADS)
        logf = early(P, T, 2, A_HEADS)
        fcum = sb("fcum", [P, A_HEADS, 2, T])
        ir = sb("ir", [P, T, 2, A_HEADS])
        irow = sb("irow", [2 * A_HEADS, SEQ])
        flat = m.xs[:, :, :].rearrange("p t d -> p (t d)")
        cq = flat[:, 0:T * C_QR].rearrange("p (t n) -> p t n", t=T)
        ckv = flat[:, T * C_QR:T * (C_QR + C_KVR + C_ROPE)].rearrange("p (t n) -> p t n", t=T)
        cstat, crstd = sb("cstat", [P, 4]), sb("crstd", [P, 4])
        csum = sb("csum", [P, 4])
        chi, clo = sb("chi", [P, 5, SEQ], F32R), sb("clo", [P, 5, SEQ], F32R)
        u = sb("u", [P, T, B_W])
        o_gate = early(P, T, A_W)
        qtok, ktok, vtok = early(P, T, A_W), early(P, T, A_W), early(P, T, A_W)
        upad = early(P, 4, SEQ + 2 * B_PAD)
        conv = sb("conv", [P, 4, SEQ])
        scale_q, scale_gt = sb("scale_q", [P, T]), sb("scale_gt", [P, T])
        bst, bmv, brstd = sb("bst", [P, T, 6]), sb("bmv", [P, T, 2]), sb("brstd", [P, T])
        bvar = sb("bvar", [P, T])
        gt = sb("gt", [P, T, 2, D])
        gate = [gt[:, :, 0, :], gt[:, :, 1, :], m.xs]
        merged = gate[0]
        qh, kv = early(P, T, C_HEADS, C_QK), early(P, T, C_HEADS, C_NOPE + C_V)
        kh = early(P, T, C_HEADS, C_QK)
        hss, hrs = sb("hss", [P, 2, T, C_HEADS]), sb("hrs", [P, 2, T, C_HEADS])
        hms, krss = sb("hms", [P, 2, T, C_HEADS]), sb("krss", [P, T])
        yhi = [sb("yahi", [P, 4, SEQ], F32R), xhi, chi]
        ylo = [sb("yalo", [P, 4, SEQ], F32R), xlo, clo]
        qkT = sb("qkT", [P, 2, SEQ])
        decay = sb("decay", [P, 6 * P])
        smat = decay
        amat, amatT = sb("amat", [P, T, SEQ]), sb("amatT", [P, T, SEQ])
        mx, den, mstat = sb("mx", [P, 4]), sb("den", [P, 4]), sb("mstat", [P, 4, 4])
        hst = sb("hst", [P, 3, T])
        hn = early(P, T, A_DIM)
        cT = early(P, 2, SEQ)[0:C_QK]
        pr, prT = early(P, T, SEQ), early(P, T, SEQ)
        cmx, csm = sb("cmx", [P, 2, T]), sb("csm", [P, 2, T])
        ytmp = u
        rope = u[:, :, :].rearrange("p t (i h f) -> p t i h f", i=4, f=16)
        silu = conv
        xscr = smat
        hscr = hn
        gflat = gt[:, :, :, :].rearrange("p t b d -> p (t b d)")
        qsq = gflat[:, 0:T * C_HEADS * C_QK].rearrange("p (t h d) -> p t h d", t=T, h=C_HEADS)
        xsq = gflat[:, 2048:2048 + T * C_HEADS * C_NOPE].rearrange("p (t h d) -> p t h d", t=T, h=C_HEADS)
        parts = [(0, P), (P, 2 * P), (3 * P, 2 * P), (5 * P, P)]

        x_in, const_in, rows_in, scale_ready = sem("x_in"), sem("const_in"), sem("rows_in"), sem("scale_ready")
        xhi_ready, xlo_ready = sem("xhi_ready"), sem("xlo_ready")
        dve_step, act_step, pool_step = sem("mix_dve_step"), sem("mix_act_step"), sem("mix_pool_step")
        z_act, z_dve = sem("z_act"), sem("z_dve")
        gates_ready, fabs_ready, fexp_ready, logl_ready = (sem(s) for s in ("gates_ready", "fabs_ready", "fexp_ready", "logl_ready"))
        logf_ready, fcum_ps, ir_ready, irow_ps, irow_ready = (
            sem(s) for s in ("logf_ready", "fcum_ps", "ir_ready", "irow_ps", "irow_ready"))
        csum_ready, crstd_ready, cnorm_ready, cturn_ps, chi_ready, clo_ready = (
            sem(s) for s in ("csum_ready", "crstd_ready", "cnorm_ready", "cturn_ps", "chi_ready", "clo_ready"))
        pad_ready, u_ready, uturn_ps, upad_ready, conv_step = (
            sem(s) for s in ("pad_ready", "u_ready", "uturn_ps", "upad_ready", "conv_step"))
        ctok_ps, bvar_ready, brstd_ready, bn_ready, bturn_ps, silu_ready, ybhi, yblo = (
            sem(s) for s in ("ctok_ps", "bvar_ready", "brstd_ready", "bn_ready", "bturn_ps", "silu_ready", "ybhi", "yblo"))
        hss_ready, hrs_ready, ckh_ready = (sem(s) for s in ("hss_ready", "hrs_ready", "ckh_ready"))
        qk_ps, qkT_ready, ib_ps, mneg_ready, decay_ready, emt_ready, score_ps, amat_ready, amT_ps, amT_ready, h_ps, hsum_ready, hrstd_ready, hn_ready, hturn_ps, yahi, yalo = (
            sem(s) for s in ("qk_ps", "qkT_ready", "ib_ps", "mneg_ready", "decay_ready", "emt_ready", "score_ps",
                             "amat_ready", "amT_ps", "amT_ready", "h_ps", "hsum_ready", "hrstd_ready", "hn_ready",
                             "hturn_ps", "yahi", "yalo"))
        cqk_ps, cT_ready, cs_ps, cmx_ready, cexp_ready, pr_ready, prT_ps, prT_ready, co_ps, ychi, yclo = (
            sem(s) for s in ("cqk_ps", "cT_ready", "cs_ps", "cmx_ready", "cexp_ready", "pr_ready", "prT_ps",
                             "prT_ready", "co_ps", "ychi", "yclo"))
        y_read, merged_ready, mturn_ps, x1_ready = (sem(s) for s in ("y_read", "merged_ready", "mturn_ps", "x1_ready"))
        m.mixer_sems = range(st.landed[0].num, x1_ready.num + 1)

        steps = []

        lookahead = 2

        def split_after(name, i):
            if blocks[name][i][0] + lookahead < n_gran:
                steps.append(("split", blocks[name][i][0] + lookahead))

        def gran(name, *between):
            for i in range(len(blocks[name])):
                steps.append(("gran", (name, i, None)))
                split_after(name, i)
                if i == 0:
                    steps.extend(between)
            steps.append(("evac", name))

        def halves(names):
            out = []
            for name in names:
                for i in range(len(blocks[name])):
                    out += [[("gran", (name, i, (0, 2)))], [("gran", (name, i, (2, 4)))]]
                out[-1].append(("evac", name))
            return out

        taps = [("conv", tap) for tap in range(B_TAPS)]
        gran("cq")
        gran("ckv")
        steps.append(("cnorm", 0))
        gran("g")
        gran("ug", ("gate1", 0))
        steps.append(("cturn", 0))
        gran("ua", ("gate2", 0))
        steps.append(("gate3", 0))
        gran("uq0")
        steps.append(("uturn", 0))
        for name in ('uq1', 'ukv0', 'q', 'ukv1'):
            gran(name)
            steps.append(taps.pop(0))
        steps.append(("chead", 0))
        fill = halves(['k', 'v', 'o'] + [f"gt{j}" for j in range(6)] + [f"y{br}{h}" for br in "abc" for h in range(2)])
        c_side = [x for h in range(C_HEADS) for x in ([("c1", h)], [("c2", h), ("c2b", h)], [("c3", h)], [("c4", h)])]
        m_side = [x for h in range(A_HEADS) for x in ([("m1", h)], [("m2", h)], [("m3", h)], [("m4", h), ("m4b", h)], [("m5", h)])]
        m_side += [[("b1", 0), ("b2", 0)], [("b3", 0)], [("b4", 0)]]
        C_START, M_START, TAP_START = 9, 9, 5
        for i, half in enumerate(fill):
            need = {"ya": 5 * A_HEADS, "yb": 5 * A_HEADS + 3}.get(half[0][1][0][:2], 0)
            while 23 - len(m_side) < need:
                steps += m_side.pop(0)
            while half[0][1][0][:2] == "yc" and c_side:
                steps += c_side.pop(0)
            ends = half[0][1] if half[0][1][2] == (2, 4) else None
            if i == len(fill) - 1:
                steps.append(("mturn", 0))
            steps += half
            c_now = c_side.pop(0) if i >= C_START and c_side else []
            held = m_side and (m_side[0][0][0] == "b1" and taps or m_side[0][0][0] == "b4" and half[0][1][0][0] != "y")
            m_now = m_side.pop(0) if i >= M_START and m_side and not held else []
            steps += c_now[:1] + m_now[:1] + c_now[1:]
            if ends is not None:
                split_after(ends[0], ends[1])
            if i >= TAP_START and taps:
                steps.append(taps.pop(0))
            steps += m_now[1:]
        gran("out0", ("mturn", 1))
        gran("out1")

        parity = {name: i % 2 for i, name in enumerate(order)}

        def zbanks(name):
            return [2 * parity[name] + t for t in range(T)]

        def last_gran(name):
            return blocks[name][-1][0]

        by_dve = {"g"} | {f"y{b}{h}" for b in "abc" for h in range(2)} | {"out0", "out1"}
        evac_at, na, nd = {}, 0, 0
        for name in order:
            if name in by_dve:
                nd += 1
                evac_at[name] = (z_dve, nd)
            elif name == "ua":
                evac_at[name] = (u_ready, T)
            else:
                na += 1
                evac_at[name] = (z_act, na)

        SA, SB, SC, SD = 4, 5, 6, 7
        NB4 = [4, 5, 6, 7]

        def cslot(c):
            return ps[:, (SA, SA, SC, SC, SD)[c], (c % 2) * SEQ:(c % 2 + 1) * SEQ]

        gran_steps = [blocks[v[0]][v[1]][0] for s, v in steps if s == "gran" and (v[2] is None or v[2][0] == 0)]
        assert gran_steps == list(range(n_gran))

        def sq(t):
            return slice(t * P, (t + 1) * P)

        block = ctx.enter_context(nc.Block())

        @block.sync
        def _(sp):
            sp.dma_start(m.x[:, :, :], I["x"][0].rearrange("(t p) d -> p t d", p=P)).then_inc(x_in, 16)
            for g in range(n_gran):
                st.load(sp, g)
                if g == n_gran - 2:
                    sp.wait_ge(yalo, A_HEADS)
                    sp.wait_ge(yclo, C_HEADS)
                    sp.wait_ge(conv_step, 4 * B_TAPS)
                    load_expert(sp, m, I, 0, 0)
            for i in range(1, EARLY):
                load_expert(sp, m, I, 0, i)

        @block.scalar
        def _(act):
            first = P + 8
            act.dma_start(m.consts[:, 0:first], I["c_consts"][:, 0:first]).then_inc(const_in, 16)
            act.dma_start(m.cols[:, :], I["v_cols"]).then_inc(const_in, 16)
            act.dma_start(m.consts[:, first:], I["c_consts"][:, first:]).then_inc(rows_in, 16)
            act.dma_start(m.rows[:, :], I["v_rows"]).then_inc(rows_in, 16)
            act.dma_start(m.sel[:, :, :], I["c_sel"]).then_inc(rows_in, 16)
            act.dma_start(m.wr[:, :, :], I["w_router"][0].rearrange("(k p) n -> p k n", p=P)).then_inc(m.wr_in, 16)
            act_n = [0]
            st.split_hi(act, 0)
            act.wait_ge(const_in, 32)
            norm_hi_act(act, m, 0, NB4, xhi, col(m, "mix"), xhi_ready, 0)
            for g in range(1, lookahead):
                st.split_hi(act, g)
            norm_act(act, m, 0)
            act.wait_ge(scale_ready, 1)
            act.wait_ge(m.sumsq_ready, T)

            for what, v in steps:
                if what == "split":
                    st.split_hi(act, v)
                elif what == "evac" and v not in by_dve and v != "ua":
                    b = zbanks(v)
                    n = blocks[v][0][3]
                    act.wait_ge(st.used, last_gran(v) + 1)
                    if v in ("cq", "ckv"):
                        i = 0 if v == "cq" else 2
                        w = C_QR if v == "cq" else C_KVR
                        dst = cq if v == "cq" else ckv
                        for t in range(T):
                            act.activation(xscr[:, 0:w], ps[:, b[t], 0:w], ACT.Square, scale=m.rstd[:, t:t + 1],
                                           accum_out=csum[:, i + t:i + t + 1]).then_inc(act_step, 1)
                            act_n[0] += 1
                            act.wait_ge(act_step, act_n[0])
                        for t in range(T):
                            ins = act.activation(dst[:, t, :], ps[:, b[t], 0:n], ACT.Copy, scale=m.rstd[:, t:t + 1])
                            ins.then_inc(csum_ready if t == 0 else z_act, 1)
                    else:
                        if v == "q":
                            dsts, f, s = [qtok[:, t, :] for t in range(T)], ACT.Copy, scale_q
                        elif v == "k":
                            dsts, f, s = [ktok[:, t, :] for t in range(T)], ACT.Copy, m.rstd
                        elif v == "v":
                            dsts, f, s = [vtok[:, t, :] for t in range(T)], ACT.Copy, m.rstd
                        elif v == "ug":
                            dsts, f, s = [u[:, t, :] for t in range(T)], ACT.Sigmoid, m.rstd
                        elif v == "o":
                            dsts, f, s = [o_gate[:, t, :] for t in range(T)], ACT.Sigmoid, m.rstd
                        elif v[0] == "u":
                            j, q = int(v[-1]), v[:2] == "uq"
                            hs = slice(4 * j, 4 * j + 4)
                            dsts, f, s = [(qh if q else kv)[:, t, hs, :].rearrange("p h d -> p (h d)") for t in range(T)], ACT.Copy, None
                        else:
                            j = int(v[2])
                            act.wait_ge(hss_ready, 1)
                            if j == 4:
                                act.wait_ge(ckh_ready, 2)
                            dsts = [gate[j // 2][:, t, (j % 2) * BANK:(j % 2 + 1) * BANK] for t in range(T)]
                            f, s = ACT.Tanh, scale_gt
                        for t in range(T):
                            ins = act.activation(dsts[t], ps[:, b[t], 0:n], f, scale=1.0 if s is None else s[:, t:t + 1])
                        ins.then_inc(z_act, 1)
                elif what == "gate1":
                    act.wait_ge(fabs_ready, 1)
                    act.activation(fexp[:, :], fabs[:, :], ACT.Exp, scale=-1.0).then_inc(fexp_ready, 1)
                    act.wait_ge(fexp_ready, 1)
                    act.activation(fabs[:, :], fexp[:, :], ACT.Ln, bias=1.0).then_inc(logl_ready, 1)
                elif what == "cturn":
                    for c in range(5):
                        act.wait_ge(cturn_ps, 1)
                        gain = (col(m, "cq")[:, c:c + 1] if c < 3 else col(m, "ckv")[:, c - 3:c - 2])
                        act.activation(chi[:, c, :], cslot(c), ACT.Copy, scale=gain).then_inc(chi_ready, 1)
                elif what == "uturn":
                    act.wait_ge(pad_ready, 1)
                    act.wait_ge(uturn_ps, 1)
                    for c in range(4):
                        act.activation(upad[:, c, B_PAD:B_PAD + SEQ],
                                       ps[:, (SC, SD)[c // 2], (c % 2) * SEQ:(c % 2 + 1) * SEQ],
                                       ACT.Copy).then_inc(upad_ready, 1)
                elif what == "m1":
                    act.wait_ge(qk_ps, v + 1)
                    act.activation(qkT[:, :, :].rearrange("p a s -> p (a s)"), ps[:, SA, :], ACT.Copy).then_inc(qkT_ready, 1)
                    act.wait_ge(mneg_ready, v + 1)
                    for j, (a, n) in enumerate(parts):
                        ins = act.activation(decay[:, a:a + n], decay[:, a:a + n], ACT.Exp, bias=mstat[:, 0, j:j + 1])
                    ins.then_inc(decay_ready, 1)
                    act.activation(mstat[:, 2, :], mstat[:, 1, :], ACT.Exp, scale=-1.0).then_inc(emt_ready, 1)
                elif what == "m3":
                    act.wait_ge(amT_ps, v + 1)
                    act.activation(amatT[:, :, :].rearrange("p a s -> p (a s)"), ps[:, SB, :], ACT.Copy).then_inc(amT_ready, 1)
                elif what == "m4":
                    act.wait_ge(h_ps, v + 1)
                    for t in range(T):
                        act.activation(hscr[:, t, :], ps[:, SA, sq(t)], ACT.Square,
                                       accum_out=hst[:, 0, t:t + 1]).then_inc(hsum_ready, 1)
                elif what == "m5":
                    act.wait_ge(hturn_ps, v + 1)
                    act.activation(yhi[0][:, v, :], ps[:, SA, SEQ:2 * SEQ], ACT.Copy,
                                   scale=col(m, "a_norm")[:, v:v + 1]).then_inc(yahi, 1)
                elif what == "c1":
                    act.wait_ge(cqk_ps, v + 1)
                    act.activation(cT[:, :, :].rearrange("p a s -> p (a s)"), ps[0:C_QK, SC, :], ACT.Copy).then_inc(cT_ready, 1)
                elif what == "c2":
                    act.wait_ge(cmx_ready, v + 1)
                    for t in range(T):
                        ins = act.activation(pr[:, t, :], ps[:, SD, t * SEQ:(t + 1) * SEQ], ACT.Exp,
                                             bias=cmx[:, 1, t:t + 1], scale=float(C_QK) ** -0.5,
                                             accum_out=csm[:, 0, t:t + 1])
                    ins.then_inc(cexp_ready, 1)
                elif what == "c3":
                    act.wait_ge(prT_ps, v + 1)
                    act.activation(prT[:, :, :].rearrange("p a s -> p (a s)"), ps[:, SC, :], ACT.Copy).then_inc(prT_ready, 1)
                elif what == "c4":
                    r = slice(64 * (v % 2), 64 * (v % 2) + 64)
                    act.wait_ge(co_ps, v + 1)
                    act.activation(yhi[2][r, v // 2, :], ps[r, SD, 0:SEQ], ACT.Copy).then_inc(ychi, 1)
                elif what == "b4":
                    act.wait_ge(bturn_ps, 1)
                    act.wait_ge(ctok_ps, 1)
                    for c in range(4):
                        act.activation(silu[:, c, :], ps[:, (SA, SB)[c // 2], (c % 2) * SEQ:(c % 2 + 1) * SEQ], ACT.Silu,
                                       bias=col(m, "ln_b")[:, c:c + 1],
                                       scale=col(m, "ln_g")[:, c:c + 1]).then_inc(silu_ready, 1)
                    act.wait_ge(st.used, last_gran("gt5") + 1)
                    for c in range(4):
                        act.wait_ge(silu_ready, c + 1)
                        act.activation(yhi[1][:, c, :], silu[:, c, :], ACT.Copy).then_inc(ybhi, 1)
                elif what == "mturn":
                    for c in range(4 * v, 4 * v + 4):
                        act.wait_ge(mturn_ps, c // 2 + 1)
                        act.activation(xhi[:, c, :], turned_ps(m, [SA, SB, SC, SD], c), ACT.Copy,
                                       scale=0.5).then_inc(xhi_ready, 1)

        @block.tensor
        def _(pe):
            pe.wait_ge(const_in, 32)
            pe.wait_ge(x_in, 16)
            turn_tokens(pe, m, m.x, NB4)
            for what, v in steps:
                if what == "gran":
                    name, i, part = v
                    g, k0, nk, n = blocks[name][i]
                    b = zbanks(name)
                    if i == 0 and part != (2, 4):
                        at = order.index(name)
                        if at >= 2:
                            pe.wait_ge(*evac_at[order[at - 2]])
                    hi, lo, kk = xhi, xlo, k0
                    if name[:2] == "uq":
                        hi, lo = chi, clo
                        pe.wait_ge(clo_ready, 3)
                    elif name[:3] == "ukv":
                        hi, lo, kk = chi, clo, 3
                        pe.wait_ge(clo_ready, 5)
                    elif name[0] == "y":
                        br = "abc".index(name[1])
                        hi, lo = yhi[br], ylo[br]
                        pe.wait_ge((yalo, yblo, yclo)[br], (A_HEADS, 4, C_HEADS)[br])
                    turned = {"cq": (xlo_ready, range(1, DC + 1)), "out0": (xlo_ready, range(DC + 1, 2 * DC + 1))}.get(name)
                    dense_granule(pe, st, g, [ps[:, b[t], 0:n] for t in range(T)], hi, lo, kk, n,
                                  i == 0, i == len(blocks[name]) - 1, turned, part)
                elif what == "gate2":
                    pe.wait_ge(rows_in, 48)
                    pe.wait_ge(logf_ready, 1)
                    for d, tri in ((0, const(m, "upto")), (1, const(m, "from"))):
                        for t in range(T):
                            out = ps[:, SB, (d * T + t) * A_HEADS:(d * T + t + 1) * A_HEADS]
                            other = (t == 1) if d == 0 else (t == 0)
                            mm = pe.matmul(out, tri, logf[:, t, d, :], start=True, stop=not other)
                            if other:
                                mm = pe.matmul(out, const(m, "ones"), logf[:, 1 - t, d, :], start=False, stop=True)
                    mm.then_inc(fcum_ps, 1)
                elif what == "gate3":
                    pe.wait_ge(ir_ready, 1)
                    for t in range(T):
                        mm = pe.transpose(ps[0:2 * A_HEADS, SB, SEQ + t * P:SEQ + (t + 1) * P],
                                          ir[:, t, :, :].rearrange("p d h -> p (d h)"), m.ident)
                    mm.then_inc(irow_ps, 1)
                elif what == "cturn":
                    pe.wait_ge(cnorm_ready, 2 * T)
                    for c in range(5):
                        for t in range(T):
                            src = cq[:, t, c * P:(c + 1) * P] if c < 3 else ckv[:, t, (c - 3) * P:(c - 2) * P]
                            mm = pe.transpose(cslot(c)[:, t * P:(t + 1) * P], src, m.ident)
                    mm.then_inc(cturn_ps, 1)
                elif what == "uturn":
                    pe.wait_ge(u_ready, T)
                    pe.wait_ge(clo_ready, 5)
                    for c in range(4):
                        for t in range(T):
                            mm = pe.transpose(ps[:, (SC, SD)[c // 2], (c % 2) * SEQ + t * P:(c % 2) * SEQ + (t + 1) * P],
                                              u[:, t, c * P:(c + 1) * P], m.ident)
                    mm.then_inc(uturn_ps, 1)
                elif what == "m1":
                    if v == 0:
                        pe.wait_ge(*evac_at["q"])
                        pe.wait_ge(*evac_at["k"])
                        pe.wait_ge(irow_ready, 1)
                        pe.wait_ge(clo_ready, 5)
                    else:
                        pe.wait_ge(yalo, v)
                    for a, src in ((0, qtok), (1, ktok)):
                        for t in range(T):
                            mm = pe.transpose(ps[:, SA, a * SEQ + t * P:a * SEQ + (t + 1) * P],
                                              src[:, t, v * P:(v + 1) * P], m.ident)
                    mm.then_inc(qk_ps, 1)
                    if v >= 1:
                        pe.wait_ge(amT_ready, v)
                    for d in range(2):
                        mm = pe.matmul(ps[:, SB, d * SEQ:(d + 1) * SEQ], m.sel[:, d * A_HEADS + v, :], irow[:, :],
                                       start=True, stop=True)
                    mm.then_inc(ib_ps, 1)
                elif what == "m2":
                    pe.wait_ge(qkT_ready, v + 1)
                    for t in range(T):
                        mm = pe.matmul(ps[:, SA, t * SEQ:(t + 1) * SEQ], qkT[:, 0, sq(t)], qkT[:, 1, :],
                                       start=True, stop=True)
                    mm.then_inc(score_ps, 1)
                elif what == "m3":
                    pe.wait_ge(amat_ready, v + 1)
                    for s in range(T):
                        for t in range(T):
                            mm = pe.transpose(ps[:, SB, s * SEQ + t * P:s * SEQ + (t + 1) * P], amat[:, t, sq(s)], m.ident)
                    mm.then_inc(amT_ps, 1)
                elif what == "m4":
                    if v == 0:
                        pe.wait_ge(*evac_at["v"])
                    pe.wait_ge(amT_ready, v + 1)
                    for t in range(T):
                        for s in range(T):
                            mm = pe.matmul(ps[:, SA, sq(t)], amatT[:, s, sq(t)], vtok[:, s, v * P:(v + 1) * P],
                                           start=s == 0, stop=s == T - 1)
                    mm.then_inc(h_ps, 1)
                elif what == "m5":
                    pe.wait_ge(hn_ready, T * (v + 1))
                    for t in range(T):
                        mm = pe.transpose(ps[:, SA, SEQ + t * P:SEQ + (t + 1) * P], hn[:, t, :], m.ident)
                    mm.then_inc(hturn_ps, 1)
                elif what == "c1":
                    if v == 0:
                        pe.wait_ge(ckh_ready, 2)
                        pe.wait_ge(upad_ready, 4)
                    else:
                        pe.wait_ge(prT_ready, v)
                    for a, src in ((0, qh), (1, kh)):
                        for t in range(T):
                            mm = pe.transpose(ps[0:C_QK, SC, a * SEQ + t * P:a * SEQ + (t + 1) * P], src[:, t, v, :], m.ident)
                    mm.then_inc(cqk_ps, 1)
                elif what == "c2":
                    pe.wait_ge(cT_ready, v + 1)
                    if v >= 1:
                        pe.wait_ge(yclo, v)
                    for t in range(T):
                        mm = pe.matmul(ps[:, SD, t * SEQ:(t + 1) * SEQ], cT[:, 0, sq(t)], cT[:, 1, :], start=True, stop=True)
                    mm.then_inc(cs_ps, 1)
                elif what == "c3":
                    pe.wait_ge(pr_ready, v + 1)
                    for s in range(T):
                        for t in range(T):
                            mm = pe.transpose(ps[:, SC, s * SEQ + t * P:s * SEQ + (t + 1) * P], pr[:, t, sq(s)], m.ident)
                    mm.then_inc(prT_ps, 1)
                elif what == "c4":
                    pe.wait_ge(prT_ready, v + 1)
                    r = slice(64 * (v % 2), 64 * (v % 2) + 64)
                    for s in range(T):
                        mm = pe.matmul(ps[r, SD, 0:SEQ], kv[:, s, v, C_NOPE:], prT[:, s, :], start=s == 0, stop=s == T - 1)
                    mm.then_inc(co_ps, 1)
                elif what == "b1":
                    pe.wait_ge(conv_step, 4 * B_TAPS)
                    pe.wait_ge(yalo, A_HEADS)
                    pe.wait_ge(amT_ready, A_HEADS)
                    for t in range(T):
                        for c in range(4):
                            mm = pe.transpose(ps[:, (SA, SB)[t], c * P:(c + 1) * P], conv[:, c, sq(t)], m.ident)
                    mm.then_inc(ctok_ps, 1)
                elif what == "b4":
                    pe.wait_ge(bn_ready, T)
                    for c in range(4):
                        for t in range(T):
                            mm = pe.transpose(ps[:, (SA, SB)[c // 2], (c % 2) * SEQ + t * P:(c % 2) * SEQ + (t + 1) * P],
                                              u[:, t, c * P:(c + 1) * P], m.ident)
                    mm.then_inc(bturn_ps, 1)
                elif what == "mturn":
                    pe.wait_ge(merged_ready, v + 1)
                    pe.wait_ge(yclo, C_HEADS)
                    pe.wait_ge(silu_ready, 4)
                    banks = [SA, SB, SC, SD]
                    for b in (2 * v, 2 * v + 1):
                        for cc in range(2):
                            for t in range(T):
                                c = 2 * b + cc
                                mm = pe.transpose(ps[:, banks[b], cc * SEQ + t * P:cc * SEQ + (t + 1) * P],
                                                  merged[:, t, c * P:(c + 1) * P], m.ident)
                        mm.then_inc(mturn_ps, 1)

        @block.vector
        def _(dve):
            n_step = [0]

            def link(ins):
                n_step[0] += 1
                ins.then_inc(dve_step, 1)
                dve.wait_ge(dve_step, n_step[0])

            dve.memset(upad[:, :, 0:B_PAD], 0.0)
            dve.memset(upad[:, :, B_PAD + SEQ:], 0.0).then_inc(pad_ready, 1)
            st.split_lo(dve, 0)
            dve.wait_ge(const_in, 32)
            norm_lo_dve(dve, m, 0, NB4, xhi, xlo, col(m, "mix"), xhi_ready, xlo_ready, 0)

            for g in range(1, lookahead):
                st.split_lo(dve, g)
            dve.wait_ge(m.rstd_ready, 1)
            dve.wait_ge(rows_in, 48)

            for what, v in steps:
                if what == "split":
                    if st.lows[v][0] is st.lo_dve:
                        st.split_lo(dve, v)
                elif what == "evac" and v[0] == "u" and v[1] in "qk":
                    dve.wait_ge(*evac_at[v])
                    hs, q = slice(4 * int(v[-1]), 4 * int(v[-1]) + 4), v[:2] == "uq"
                    for t in range(T):
                        src = qh[:, t, hs, :] if q else kv[:, t, hs, 0:C_NOPE]
                        ins = dve.tensor_tensor((qsq if q else xsq)[:, t, hs, :], src, src, ALU.mult)
                    link(ins)
                    for t in range(T):
                        ins = dve.tensor_reduce(hss[:, 0 if q else 1, t, hs], (qsq if q else xsq)[:, t, hs, :], AX.X, ALU.add)
                    link(ins)
                elif what == "evac" and (v in by_dve or v == "ua"):
                    b = zbanks(v)
                    dve.wait_ge(st.used, last_gran(v) + 1)
                    if v == "g":
                        for t in range(T):
                            ins = dve.scalar_tensor_tensor(gates[:, t, :, :, :].rearrange("p d i h -> p (d i h)"),
                                                           ps[:, b[t], 0:16], m.rstd[:, t:t + 1], row(m, "b_if"), ALU.mult, ALU.add)
                            ins.then_inc(gates_ready if t == 0 else z_dve, 1)
                    elif v == "ua":
                        dve.wait_ge(*evac_at["ug"])
                        for t in range(T):
                            ins = dve.scalar_tensor_tensor(u[:, t, :], ps[:, b[t], :], m.rstd[:, t:t + 1], u[:, t, :], ALU.mult, ALU.mult)
                            ins.then_inc(u_ready, 1)
                    elif v[0] == "y":
                        br, h = "abc".index(v[1]), int(v[2])
                        if br == 0:
                            dve.wait_ge(*evac_at["gt5"])
                        for t in range(T):
                            dst = merged[:, t, h * BANK:(h + 1) * BANK] if br == 0 else ytmp[:, t, :]
                            ins = dve.scalar_tensor_tensor(dst, gate[br][:, t, h * BANK:(h + 1) * BANK], 1.0, ps[:, b[t], :],
                                                           ALU.add, ALU.mult)
                        ins.then_inc(z_dve, 1)
                        dve.wait_ge(*evac_at[v])
                        if br > 0:
                            for t in range(T):
                                dst = merged[:, t, h * BANK:(h + 1) * BANK]
                                ins = dve.tensor_tensor(dst, dst, ytmp[:, t, :], ALU.add)
                            if br == 2:
                                ins.then_inc(merged_ready, 1)
                                dve.wait_ge(merged_ready, h + 1)
                            else:
                                link(ins)
                    else:
                        h = int(v[3])
                        for t in range(T):
                            ins = dve.tensor_tensor(m.x[:, t, h * BANK:(h + 1) * BANK], ps[:, b[t], :],
                                                    m.x[:, t, h * BANK:(h + 1) * BANK], ALU.add)
                        ins.then_inc(z_dve, 1)
                elif what == "gate1":
                    dve.wait_ge(*evac_at["g"])
                    dve.wait_ge(gates_ready, 1)
                    f = gates[:, :, :, 1, :].rearrange("p t d h -> p (t d) h")
                    l3 = fabs[:, :].rearrange("p (a h) -> p a h", h=A_HEADS)
                    dve.scalar_tensor_tensor(l3, f, -1.0, f, ALU.mult, ALU.max).then_inc(fabs_ready, 1)
                    dve.wait_ge(logl_ready, 1)
                    dve.scalar_tensor_tensor(logf[:, :, :, :].rearrange("p t d h -> p (t d) h"), f, 0.0, l3,
                                             ALU.min, ALU.subtract).then_inc(logf_ready, 1)
                elif what == "gate2":
                    dve.wait_ge(fcum_ps, 1)
                    fps = ps[:, SB, 0:2 * T * A_HEADS].rearrange("p (d t h) -> p d t h", d=2, t=T)
                    link(dve.tensor_copy(fcum[:, :, :, :].rearrange("p h d t -> p d t h"), fps))
                    for d in range(2):
                        ins = dve.tensor_tensor(ir[:, :, d, :], gates[:, :, d, 0, :], fps[:, d, :, :], ALU.subtract)
                        if d == 0:
                            link(ins)
                    ins.then_inc(ir_ready, 1)
                elif what == "gate3":
                    dve.wait_ge(irow_ps, 1)
                    dve.tensor_copy(irow[:, :], ps[0:2 * A_HEADS, SB, SEQ:2 * SEQ]).then_inc(irow_ready, 1)
                elif what == "cnorm":
                    dve.wait_ge(crstd_ready, 1)
                    dve.wait_ge(*evac_at["ckv"])
                    for i in range(4):
                        a = cq[:, i % 2, :] if i < 2 else ckv[:, i % 2, 0:C_KVR]
                        dve.tensor_scalar(a, a, crstd[:, i:i + 1], None, ALU.mult).then_inc(cnorm_ready, 1)
                elif what == "cturn":
                    for c in range(5):
                        dve.wait_ge(chi_ready, min(5, 2 * (c // 2) + 2))
                        gain = (col(m, "cq")[:, c:c + 1] if c < 3 else col(m, "ckv")[:, c - 3:c - 2])
                        dve.scalar_tensor_tensor(clo[:, c, :], cslot(c), gain, chi[:, c, :].bitcast(F32),
                                                 ALU.mult, ALU.subtract).then_inc(clo_ready, 1)
                elif what == "conv":
                    w0, _ = COLS["conv_w"]
                    for c in range(4):
                        if v == 0:
                            dve.wait_ge(upad_ready, c + 1)
                            ins = dve.tensor_scalar(conv[:, c, :], upad[:, c, 0:SEQ], m.cols[:, w0 + c:w0 + c + 1],
                                                    col(m, "conv_b")[:, c:c + 1], ALU.mult, ALU.add)
                        else:
                            dve.wait_ge(conv_step, 4 * (v - 1) + c + 1)
                            w = w0 + v * 4 + c
                            ins = dve.scalar_tensor_tensor(conv[:, c, :], upad[:, c, v:v + SEQ], m.cols[:, w:w + 1],
                                                           conv[:, c, :], ALU.mult, ALU.add)
                        ins.then_inc(conv_step, 1)
                elif what == "chead":
                    dve.wait_ge(*evac_at["ukv1"])
                    q4, k4, kv4 = qh[:, :, :, :], kh[:, :, :, :], kv[:, :, :, :]

                    def cs(name):
                        return const(m, name).rearrange("p (t a f) -> p t a f", t=T, a=1)

                    for t in range(T):
                        ins = dve.tensor_tensor_reduce(decay[:, t * C_ROPE:(t + 1) * C_ROPE], ckv[:, t, C_KVR:], ckv[:, t, C_KVR:], 1.0, 0.0,
                                                       ALU.mult, ALU.add, krss[:, t:t + 1])
                    link(ins)
                    for t in range(T):
                        ins = dve.tensor_scalar(hss[:, 1, t, :], hss[:, 1, t, :], krss[:, t:t + 1], None, ALU.add)
                    ins.then_inc(hss_ready, 1)
                    dve.wait_ge(hrs_ready, 1)
                    for t in range(T):
                        hb = [hrs[:, a, t, :].unsqueeze(2) for a in range(2)]
                        link(dve.tensor_tensor(q4[:, t], q4[:, t], hb[0].to_broadcast([P, C_HEADS, C_QK]), ALU.mult))
                        link(dve.tensor_tensor(q4[:, t], q4[:, t],
                                               row(m, "q_g").unsqueeze(1).to_broadcast([P, C_HEADS, C_QK]), ALU.mult))
                        link(dve.tensor_tensor(k4[:, t, :, 0:C_NOPE], kv4[:, t, :, 0:C_NOPE],
                                               hb[1].to_broadcast([P, C_HEADS, C_NOPE]), ALU.mult))
                        link(dve.tensor_tensor(k4[:, t, :, C_NOPE:],
                                               ckv[:, t, C_KVR:].unsqueeze(1).to_broadcast([P, C_HEADS, C_ROPE]),
                                               hb[1].to_broadcast([P, C_HEADS, C_ROPE]), ALU.mult))
                        link(dve.tensor_tensor(k4[:, t], k4[:, t],
                                               row(m, "k_g").unsqueeze(1).to_broadcast([P, C_HEADS, C_QK]), ALU.mult))
                    for a in (q4, k4):
                        for t in range(T):
                            r1, r2 = a[:, t, :, C_NOPE:C_NOPE + 16], a[:, t, :, C_NOPE + 16:]
                            c_t = cs("cos")[:, t].to_broadcast([P, C_HEADS, 16])
                            s_t = cs("sin")[:, t].to_broadcast([P, C_HEADS, 16])
                            rp = [rope[:, t, i, :, :] for i in range(4)]
                            dve.tensor_tensor(rp[0], r1, c_t, ALU.mult)
                            dve.tensor_tensor(rp[1], r2, s_t, ALU.mult)
                            dve.tensor_tensor(rp[2], r2, c_t, ALU.mult)
                            link(dve.tensor_tensor(rp[3], r1, s_t, ALU.mult))
                            dve.tensor_tensor(r1, rp[0], rp[1], ALU.subtract)
                            ins = dve.tensor_tensor(r2, rp[2], rp[3], ALU.add)
                            if t < T - 1:
                                link(ins)
                        ins.then_inc(ckh_ready, 1)
                        dve.wait_ge(ckh_ready, 1 if a is q4 else 2)
                elif what == "m1":
                    dve.wait_ge(ib_ps, v + 1)
                    if v >= 1:
                        dve.wait_ge(emt_ready, v)
                    for j, (a, n) in enumerate(parts):
                        d, t = j // 2, j % 2
                        src = ps[:, SB, d * SEQ:d * SEQ + SEQ]
                        msk = const(m, ("causal", "anti")[d])
                        if n == P:
                            src, msk = (src[:, 0:P], msk[:, P:]) if d == 0 else (src[:, P:], msk[:, 0:P])
                        ins = dve.tensor_tensor_reduce(decay[:, a:a + n], src, msk, 1.0, 0.0, ALU.add, ALU.max, mx[:, j:j + 1])
                    link(ins)
                    link(dve.tensor_tensor(mstat[:, 1, :], mx[:, :], fcum[:, v, :, :].rearrange("p d t -> p (d t)"), ALU.add))
                    dve.tensor_scalar(mstat[:, 0, :], mx[:, :], -1.0, None, ALU.mult).then_inc(mneg_ready, 1)
                elif what == "m2":
                    dve.wait_ge(score_ps, v + 1)
                    dve.wait_ge(emt_ready, v + 1)
                    for j, (a, n) in enumerate(parts):
                        d, t = j // 2, j % 2
                        src = ps[:, SA, t * SEQ:(t + 1) * SEQ]
                        if n == P:
                            src = src[:, 0:P] if d == 0 else src[:, P:]
                        ins = dve.tensor_tensor_reduce(smat[:, a:a + n], src, decay[:, a:a + n], 1.0, 0.0,
                                                       ALU.mult, ALU.add, den[:, j:j + 1])
                    link(ins)
                    link(dve.scalar_tensor_tensor(den[:, :], den[:, :], -1.0, den[:, :], ALU.mult, ALU.max))
                    link(dve.tensor_tensor(den[:, :], den[:, :], mstat[:, 2, :], ALU.max))
                    link(dve.reciprocal(mstat[:, 3, :], den[:, :]))
                    f0, f1, b0, b1 = parts
                    rd = [mstat[:, 3, j:j + 1] for j in range(4)]
                    dve.tensor_scalar(amat[:, 1, :], smat[:, f1[0]:f1[0] + f1[1]], rd[1], None, ALU.mult)
                    link(dve.tensor_scalar(amat[:, 0, :], smat[:, b0[0]:b0[0] + b0[1]], rd[2], None, ALU.mult))
                    dve.scalar_tensor_tensor(amat[:, 0, 0:P], smat[:, f0[0]:f0[0] + P], rd[0], amat[:, 0, 0:P],
                                             ALU.mult, ALU.add)
                    dve.scalar_tensor_tensor(amat[:, 1, P:], smat[:, b1[0]:b1[0] + P], rd[3], amat[:, 1, P:],
                                             ALU.mult, ALU.add).then_inc(amat_ready, 1)
                    dve.wait_ge(amat_ready, v + 1)
                elif what == "m4b":
                    dve.wait_ge(hrstd_ready, v + 1)
                    if v == 0:
                        dve.wait_ge(*evac_at["o"])
                    for t in range(T):
                        dve.scalar_tensor_tensor(hn[:, t, :], ps[:, SA, sq(t)], hst[:, 2, t:t + 1],
                                                 o_gate[:, t, v * P:(v + 1) * P], ALU.mult, ALU.mult).then_inc(hn_ready, 1)
                elif what == "m5":
                    dve.wait_ge(yahi, v + 1)
                    dve.scalar_tensor_tensor(ylo[0][:, v, :], ps[:, SA, SEQ:2 * SEQ], col(m, "a_norm")[:, v:v + 1],
                                             yhi[0][:, v, :].bitcast(F32), ALU.mult, ALU.subtract).then_inc(yalo, 1)
                elif what == "c2":
                    dve.wait_ge(cs_ps, v + 1)
                    link(dve.tensor_reduce(cmx[:, 0, :], ps[:, SD, :].rearrange("p (t s) -> p t s", t=T), AX.X, ALU.max))
                    dve.tensor_scalar(cmx[:, 1, :], cmx[:, 0, :], -float(C_QK) ** -0.5, None, ALU.mult).then_inc(cmx_ready, 1)
                elif what == "c2b":
                    dve.wait_ge(cexp_ready, v + 1)
                    link(dve.reciprocal(csm[:, 1, :], csm[:, 0, :]))
                    for t in range(T):
                        ins = dve.tensor_scalar(pr[:, t, :], pr[:, t, :], csm[:, 1, t:t + 1], None, ALU.mult)
                    ins.then_inc(pr_ready, 1)
                elif what == "c4":
                    r = slice(64 * (v % 2), 64 * (v % 2) + 64)
                    dve.wait_ge(ychi, v + 1)
                    dve.tensor_tensor(ylo[2][r, v // 2, :], ps[r, SD, 0:SEQ], yhi[2][r, v // 2, :].bitcast(F32),
                                      ALU.subtract).then_inc(yclo, 1)
                elif what == "b2":
                    dve.wait_ge(ctok_ps, 1)
                    for t in range(T):
                        link(dve.bn_stats(bst[:, t, :], ps[:, (SA, SB)[t], :]))
                        ins = dve.bn_aggr(bmv[:, t, :], bst[:, t, :])
                        if t == 0:
                            link(ins)
                    ins.then_inc(bvar_ready, 1)
                    dve.wait_ge(bvar_ready, 1)
                elif what == "b3":
                    dve.wait_ge(brstd_ready, 1)
                    for t in range(T):
                        dve.tensor_scalar(u[:, t, :], ps[:, (SA, SB)[t], :], bmv[:, t, 0:1], brstd[:, t:t + 1],
                                          ALU.subtract, ALU.mult).then_inc(bn_ready, 1)
                elif what == "b4":
                    for c in range(4):
                        dve.wait_ge(ybhi, c + 1)
                        dve.tensor_tensor(ylo[1][:, c, :], silu[:, c, :], yhi[1][:, c, :].bitcast(F32),
                                          ALU.subtract).then_inc(yblo, 1)
                elif what == "mturn":
                    for c in range(4 * v, 4 * v + 4):
                        dve.wait_ge(xhi_ready, DC + 2 * (c // 2) + 2)
                        dve.scalar_tensor_tensor(xlo[:, c, :], turned_ps(m, [SA, SB, SC, SD], c), 0.5,
                                                 xhi[:, c, :].bitcast(F32), ALU.mult, ALU.subtract).then_inc(xlo_ready, 1)

        @block.gpsimd
        def _(pool):
            n_step = [0]

            def link(ins):
                n_step[0] += 1
                ins.then_inc(pool_step, 1)
                pool.wait_ge(pool_step, n_step[0])

            pool.wait_ge(const_in, 32)
            norm_pool(pool, m, 0)
            pool.wait_ge(m.rstd_ready, 1)
            pool.tensor_scalar(scale_q[:, :], m.rstd[:, :], float(A_DIM) ** -0.5, None, ALU.mult)
            pool.tensor_scalar(scale_gt[:, :], m.rstd[:, :], 0.5, None, ALU.mult).then_inc(scale_ready, 1)
            for what, v in steps:
                if what == "split":
                    if st.lows[v][0] is st.lo_pool:
                        st.split_lo(pool, v)
                elif what == "cnorm":
                    pool.wait_ge(csum_ready, 2)
                    pool.tensor_scalar(cstat[:, 0:2], csum[:, 0:2], 1.0 / C_QR, EPS, ALU.mult, ALU.add)
                    link(pool.tensor_scalar(cstat[:, 2:4], csum[:, 2:4], 1.0 / C_KVR, EPS, ALU.mult, ALU.add))
                    pool.tensor_tensor(crstd[:, :], cstat[:, :], m.half[:, 0:4], ALU.pow).then_inc(crstd_ready, 1)
                elif what == "chead":
                    pool.wait_ge(hss_ready, 1)
                    h2, ms2, rs2 = (a[:, :, :, :].rearrange("p a t h -> p (a t h)") for a in (hss, hms, hrs))
                    link(pool.tensor_scalar(ms2, h2, 1.0 / C_QK, EPS, ALU.mult, ALU.add))
                    pool.tensor_tensor(rs2, ms2, m.half[:, 0:1].to_broadcast([P, 2 * T * C_HEADS]), ALU.pow).then_inc(hrs_ready, 1)
                elif what == "m4":
                    pool.wait_ge(hsum_ready, T * (v + 1))
                    link(pool.tensor_scalar(hst[:, 1, :], hst[:, 0, :], 1.0 / A_DIM, EPS, ALU.mult, ALU.add))
                    pool.tensor_tensor(hst[:, 2, :], hst[:, 1, :], m.half[:, 0:T], ALU.pow).then_inc(hrstd_ready, 1)
                elif what == "b2":
                    pool.wait_ge(bvar_ready, 1)
                    link(pool.tensor_scalar(bvar[:, :], bmv[:, :, 1], EPS, None, ALU.add))
                    pool.tensor_tensor(brstd[:, :], bvar[:, :], m.half[:, 0:T], ALU.pow).then_inc(brstd_ready, 1)



FJ = E_FF // (P // CAP)
FB = FJ // P
E_COLS = 256
GK = 2
NS = 12
EARLY = 4


def expert_place(m, i):
    n = E_FF if i < 8 else E_COLS
    ring = m.ring[:, i * GK * E_FF:(i + 1) * GK * E_FF] if i < EARLY else m.e_ring[:, i - EARLY, :]
    return ring.rearrange("p (k n) -> p k n", n=n)


def load_expert(sp, m, I, e, i):
    if i < 8:
        w = I["w_e_gate"] if i < 4 else I["w_e_up"]
        r = (i % 4) * GK * P
        src = w[0, e, r:r + GK * P, :]
    else:
        src = I["w_e_down"][0, e, :, (i - 8) * E_COLS:(i - 7) * E_COLS]
    sp.dma_start(expert_place(m, i), src.rearrange("(k p) n -> p k n", p=P)).then_inc(m.e_landed[i], 16)


def experts(nc, m, I, st):
    with ExitStack() as ctx:
        def sb(name, shape, dt=F32):
            return ctx.enter_context(nc.sbuf_tensor("sb_" + name, shape, dt))

        def sem(name):
            return ctx.enter_context(nc.semaphore(name))

        ps = m.ps
        J = P // CAP
        NC = E_COLS
        ACC = (0, 1, 2, 3)
        GATE, UP, DOWN = 4, 5, (6, 7)
        NBANKS = [4, 5, 6, 7]
        BY_ACT, BY_DVE = (0, 1, 4, 5), (2, 3, 6, 7)
        LOGIT, AFF, SLOT = 0, 6, 7

        m.e_ring = sb("e_ring", [P, NS - EARLY, GK * E_FF])
        xgT = sb("xgT", [P, DC, N_EXP * CAP])
        xnT = xgT[:, :, 0:SEQ]
        wr = m.wr
        late = m.rows[:, 0:CAP]
        smx, ssum = sb("smx", [P, 2, T]), sb("ssum", [P, 2, T])
        aff = sb("aff", [P, T, N_EXP])
        affT, work, above, equal = (m.xs[0:N_EXP, 1, i * SEQ:(i + 1) * SEQ] for i in range(4))
        one = const(m, "ones")[0:N_EXP, 0:1].to_broadcast([N_EXP, SEQ])
        top8, cnt = sb("top8", [N_EXP, 8]), sb("cnt", [N_EXP, 2])
        hot = sb("hot", [P, T, N_EXP, CAP], F32R)
        hotg = m.xs[:, 0, :].rearrange("p (t e c) -> p t e c", t=T, e=N_EXP)
        xshi, xslo = sb("xshi", [P, T, D], F32R), sb("xslo", [P, T, D], F32R)
        at = CONSTS["causal"][0]
        xgs = m.consts[:, at:at + DC * CAP].rearrange("p (k c) -> p k c", k=DC)
        hotgs = sb("hotgs", [P, T, J, CAP])
        at = CONSTS["anti"][0]
        gs = m.consts[:, at:at + SEQ]
        sg, hT = sb("sg", [P, FJ]), sb("hT", [P, FB, P])
        hs = sg
        ysb = m.xs[:, 1, :]

        late_in = sem("late_in")
        landed = m.e_landed
        xnT_act, xnT_dve, logits_ps, smx_ready, exp_ready, aff_ready, affT_ps, slot_ready, slot_ps, hot_ready, hotg_ready = (
            sem(s) for s in ("xnT_act", "xnT_dve", "logits_ps", "smx_ready", "exp_ready", "aff_ready", "affT_ps", "slot_ready",
                             "slot_ps", "hot_ready", "hotg_ready"))
        dve_step = sem("e_dve_step")
        xshi_ready, xslo_ready = sem("xshi_ready"), sem("xslo_ready")
        gather_ps, xg_act, xg_dve = sem("gather_ps"), sem("xg_act"), sem("xg_dve")
        used, xgs_ready, g_ps, gs_ready, sg_ready, h_ready, hT_ps, hT_ready, y_act, y_dve, scattered = (
            sem(s) for s in ("e_used", "xgs_ready", "g_ps", "gs_ready", "sg_ready", "h_ready", "hT_ps", "hT_ready",
                             "y_act", "y_dve", "scattered"))

        def place(i):
            return expert_place(m, i)

        block = ctx.enter_context(nc.Block())

        @block.sync
        def _(sp):
            for i in range(EARLY, NS):
                load_expert(sp, m, I, 0, i)
                if i == EARLY:
                    sp.dma_start(late[:, :], I["c_late"][:, 3 * P:]).then_inc(late_in, 16)
            sp.sem_clear(m.mixer_sems)
            with sp.Fori(1, N_EXP) as e:
                for i in range(NS):
                    sp.wait_ge(used, e * NS + (i + 1 - NS))
                    load_expert(sp, m, I, e, i)
            sp.wait_ge(used, (N_EXP - 1) * NS + EARLY)
            for g in range(st.slots):
                st.load(sp, g)

        @block.scalar
        def _(act):
            gain = col(m, "ffn")
            for c in BY_ACT:
                act.wait_ge(m.xturn_ps, 4 + c // 2 + 1)
                act.activation(xnT[:, c, :], turned_ps(m, NBANKS, c), ACT.Copy, scale=gain[:, c:c + 1]).then_inc(xnT_act, 1)
            norm_act(act, m, 1)
            act.wait_ge(m.rstd_ready, 2)
            for t in range(T):
                act.activation(xshi[:, t, :], m.x[:, t, :], ACT.Copy, scale=m.rstd[:, t:t + 1]).then_inc(xshi_ready, 1)
            act.wait_ge(smx_ready, 1)
            for t in range(T):
                ins = act.activation(aff[:, t, :], ps[:, LOGIT, t * N_EXP:(t + 1) * N_EXP], ACT.Exp,
                                     bias=smx[:, 1, t:t + 1], scale=m.rstd[:, t:t + 1], accum_out=ssum[:, 0, t:t + 1])
            ins.then_inc(exp_ready, 1)
            for c in range(0, DC, 2):
                act.wait_ge(gather_ps, c + 1)
                act.activation(xgs[:, c, :], ps[:, 4 + c % 4, 0:CAP], ACT.Copy, scale=gain[:, c:c + 1])
                act.activation(xgT[:, c, :], ps[:, 4 + c % 4, :], ACT.Copy, scale=gain[:, c:c + 1]).then_inc(xg_act, 1)
            with act.Fori(0, N_EXP) as e:
                act.wait_ge(g_ps, e + 1)
                for t in range(T):
                    ins = act.activation(gs[:, t * P:(t + 1) * P], ps[:, GATE + t, FJ:FJ + P], ACT.Copy)
                ins.then_inc(gs_ready, 1)
                act.wait_ge(used, e * NS + 4)
                act.activation(sg[:, :], ps[:, GATE, 0:FJ], ACT.Silu).then_inc(sg_ready, 1)
                act.wait_ge(used, e * NS + 10)
                act.activation(ysb[:, 0:BANK], ps[:, DOWN[0], :], ACT.Copy).then_inc(y_act, 1)
            for h in range(2):
                act.wait_ge(scattered, 2 * (N_EXP - 1) + h + 1)
                act.activation(m.x[:, 0, h * BANK:(h + 1) * BANK], ps[:, ACC[h], :], ACT.Copy)

        @block.tensor
        def _(pe):
            turn_tokens(pe, m, m.x, NBANKS)
            pe.wait_ge(m.wr_in, 16)
            for t in range(T):
                for c in range(DC):
                    if t == 0:
                        pe.wait_ge(xnT_act if c in BY_ACT else xnT_dve, 2 * (c // 4) + c % 2 + 1)
                    mm = pe.matmul(ps[:, LOGIT, t * N_EXP:(t + 1) * N_EXP], xnT[:, c, t * P:(t + 1) * P], wr[:, c, :],
                                   start=c == 0, stop=c == DC - 1)
            mm.then_inc(logits_ps, 1)
            pe.wait_ge(aff_ready, T)
            for t in range(T):
                mm = pe.transpose(ps[0:N_EXP, AFF, t * P:(t + 1) * P], aff[:, t, :], m.ident)
            mm.then_inc(affT_ps, 1)
            for t in range(T):
                for h in range(2):
                    pe.matmul(ps[:, ACC[2 * t + h], :], m.ident, m.x[:, t, h * BANK:(h + 1) * BANK], start=True, stop=True)
            pe.wait_ge(slot_ready, 1)
            for t in range(T):
                mm = pe.transpose(ps[:, SLOT, t * N_EXP:(t + 1) * N_EXP], affT[:, t * P:(t + 1) * P], m.ident[0:N_EXP, 0:N_EXP])
            mm.then_inc(slot_ps, 1)
            pe.wait_ge(xslo_ready, T)
            pe.wait_ge(hot_ready, T)
            for c in range(DC):
                if c >= 4:
                    pe.wait_ge((xg_act, xg_dve)[c % 2], (c - 4) // 2 + 1)
                for t in range(T):
                    for part in (xshi, xslo):
                        mm = pe.matmul(ps[:, 4 + c % 4, :], part[:, t, c * P:(c + 1) * P],
                                       hot[:, t, :, :].rearrange("p e c -> p (e c)"),
                                       start=t == 0 and part is xshi, stop=t == T - 1 and part is xslo)
                mm.then_inc(gather_ps, 1)
            pe.wait_ge(xg_act, DC // 2)
            pe.wait_ge(xg_dve, DC // 2)
            def scatter(h):
                for t in range(T):
                    mm = pe.matmul(ps[:, ACC[2 * t + h], :], gs[:, t * P:(t + 1) * P], ysb[:, h * BANK:(h + 1) * BANK],
                                   start=False, stop=True, skip_group_check=True)
                mm.then_inc(scattered, 1)

            with pe.Fori(0, N_EXP) as e:
                pe.wait_ge(xgs_ready, e * 2 + 1)
                for t in range(T):
                    mm = pe.transpose(ps[:, GATE + t, FJ:FJ + P], hotgs[:, t, :, :].rearrange("p j c -> p (j c)"), m.ident)
                mm.then_inc(g_ps, 1)
                pe.wait_ge(gs_ready, e + 1)
                for i in range(8):
                    pe.wait_ge(landed[i], e * 16 + 16)
                    for q in range(GK):
                        k = (i % 4) * GK + q
                        for j in range(J):
                            mm = pe.matmul(ps[j * CAP:(j + 1) * CAP, GATE if i < 4 else UP, 0:FJ], xgs[:, k, :],
                                           place(i)[:, q, j * FJ:(j + 1) * FJ], start=k == 0, stop=k == DC - 1)
                    mm.then_inc(used, 1)
                pe.wait_ge(h_ready, e + 1)
                for b in range(FB):
                    mm = pe.transpose(ps[:, GATE, b * P:(b + 1) * P], hs[:, b * P:(b + 1) * P], m.ident)
                mm.then_inc(hT_ps, 1)
                pe.wait_ge(hT_ready, e + 1)
                for i in range(4):
                    pe.wait_ge(landed[8 + i], e * 16 + 16)
                    for b in range(FB):
                        for j in range(J):
                            mm = pe.matmul(ps[j * CAP:(j + 1) * CAP, DOWN[i // 2], (i % 2) * NC:(i % 2 + 1) * NC],
                                           hT[:, b, j * CAP:(j + 1) * CAP], place(8 + i)[:, j * FB + b, :],
                                           start=b == 0, stop=b == FB - 1)
                    mm.then_inc(used, 1)
                    if i == 2:
                        pe.wait_ge(y_act, e + 1)
                        scatter(0)
                pe.wait_ge(y_dve, e + 1)
                scatter(1)

        @block.vector
        def _(dve):
            n_step = [0]

            def link(ins):
                n_step[0] += 1
                ins.then_inc(dve_step, 1)
                dve.wait_ge(dve_step, n_step[0])

            gain = col(m, "ffn")
            for c in BY_DVE:
                dve.wait_ge(m.xturn_ps, 4 + c // 2 + 1)
                dve.tensor_scalar(xnT[:, c, :], turned_ps(m, NBANKS, c), gain[:, c:c + 1], None, ALU.mult).then_inc(xnT_dve, 1)
            dve.wait_ge(m.rstd_ready, 2)
            for t in range(T):
                dve.wait_ge(xshi_ready, t + 1)
                dve.scalar_tensor_tensor(xslo[:, t, :], m.x[:, t, :], m.rstd[:, t:t + 1], xshi[:, t, :].bitcast(F32),
                                         ALU.mult, ALU.subtract).then_inc(xslo_ready, 1)
            dve.wait_ge(logits_ps, 1)
            link(dve.tensor_reduce(smx[:, 0, :], ps[:, LOGIT, 0:T * N_EXP].rearrange("p (t e) -> p t e", t=T), AX.X, ALU.max))
            dve.scalar_tensor_tensor(smx[:, 1, :], smx[:, 0, :], -1.0, m.rstd[:, :], ALU.mult, ALU.mult).then_inc(smx_ready, 1)
            dve.wait_ge(exp_ready, 1)
            link(dve.reciprocal(ssum[:, 1, :], ssum[:, 0, :]))
            for t in range(T):
                dve.tensor_scalar(aff[:, t, :], aff[:, t, :], ssum[:, 1, t:t + 1], None, ALU.mult).then_inc(aff_ready, 1)
            dve.wait_ge(affT_ps, 1)
            link(dve.tensor_copy(affT[:, :], ps[0:N_EXP, AFF, 0:SEQ]))
            src = affT
            for r in range(CAP // 8):
                link(dve.max(top8[:, :], src[:, :]))
                if r < CAP // 8 - 1:
                    link(dve.match_replace(work[:, :], top8[:, :], src[:, :], -1.0))
                    src = work
            link(dve.tensor_scalar(above[:, :], affT[:, :], top8[:, 7:8], None, ALU.is_gt, ALU.add, accum_out=cnt[:, 0:1]))
            link(dve.tensor_scalar(equal[:, :], affT[:, :], top8[:, 7:8], None, ALU.is_equal))
            link(dve.tensor_scalar(cnt[:, 1:2], cnt[:, 0:1], -1.0, float(CAP), ALU.mult, ALU.add))
            link(dve.tensor_tensor_scan(work[:, :], one, equal[:, :], 0.0, ALU.mult, ALU.add))
            link(dve.scalar_tensor_tensor(equal[:, :], work[:, :], cnt[:, 1:2], equal[:, :], ALU.is_le, ALU.mult))
            link(dve.tensor_tensor(above[:, :], above[:, :], equal[:, :], ALU.add))
            link(dve.tensor_tensor_scan(work[:, :], one, above[:, :], 0.0, ALU.mult, ALU.add))
            dve.tensor_tensor(affT[:, :], work[:, :], above[:, :], ALU.mult).then_inc(slot_ready, 1)
            dve.wait_ge(slot_ps, 1)
            dve.wait_ge(late_in, 16)
            for t in range(T):
                slots = ps[:, SLOT, t * N_EXP:(t + 1) * N_EXP].unsqueeze(2).to_broadcast([P, N_EXP, CAP])
                dve.tensor_tensor(hot[:, t, :, :], slots, late[:, :].unsqueeze(1).to_broadcast([P, N_EXP, CAP]),
                                  ALU.is_equal).then_inc(hot_ready, 1)
            dve.wait_ge(hot_ready, T)
            for t in range(T):
                dve.tensor_tensor(hotg[:, t, :, :], hot[:, t, :, :].bitcast(F32), aff[:, t, :].unsqueeze(2).to_broadcast([P, N_EXP, CAP]),
                                  ALU.mult).then_inc(hotg_ready, 1)
            for c in range(1, DC, 2):
                dve.wait_ge(gather_ps, c + 1)
                dve.tensor_scalar(xgs[:, c, :], ps[:, 4 + c % 4, 0:CAP], gain[:, c:c + 1], None, ALU.mult)
                dve.tensor_scalar(xgT[:, c, :], ps[:, 4 + c % 4, :], gain[:, c:c + 1], None, ALU.mult).then_inc(xg_dve, 1)
            with dve.Fori(0, N_EXP) as e:
                dve.wait_ge(sg_ready, e + 1)
                dve.wait_ge(used, e * NS + 8)
                dve.tensor_tensor(hs[:, :], ps[:, UP, 0:FJ], sg[:, :], ALU.mult).then_inc(h_ready, 1)
                dve.wait_ge(hT_ps, e + 1)
                dve.tensor_copy(hT[:, :, :].rearrange("p b c -> p (b c)"), ps[:, GATE, 0:FJ]).then_inc(hT_ready, 1)
                dve.wait_ge(used, e * NS + 12)
                dve.tensor_copy(ysb[:, BANK:], ps[:, DOWN[1], :]).then_inc(y_dve, 1)
            for h in range(2):
                dve.wait_ge(scattered, 2 * (N_EXP - 1) + h + 1)
                dve.tensor_copy(m.x[:, 1, h * BANK:(h + 1) * BANK], ps[:, ACC[2 + h], :])

        @block.gpsimd
        def _(pool):
            norm_pool(pool, m, 1)

            def take_hot(e):
                pool.tensor_copy(hotgs[:, :, :, :],
                                 hotg[:, :, bass.ds(e, 1), :].to_broadcast([P, T, J, CAP])).then_inc(xgs_ready, 1)

            pool.wait_ge(hotg_ready, T)
            take_hot(0)
            with pool.Fori(0, N_EXP - 1) as e:
                pool.wait_ge(used, e * NS + 8)
                take_hot(e + 1)
                pool.tensor_copy(xgs[:, :, :], xgT[:, :, bass.ds((e + 1) * CAP, CAP)]).then_inc(xgs_ready, 1)



FW = 256
FN = D_FF // FW
FC = FW // P


def second_stream(m, ctx, nc, I):
    st = Stream(ctx, nc, "net", m.ring[:, :].rearrange("p (s n) -> p s n", n=2048), 3, 3)
    at = {}

    def dense(name, w, n0, by_dve=()):
        at[name] = [st.add([(0, 4, BANK, chunks(w, k, 4, n0, BANK))], k in by_dve) for k in (0, 4)]

    def ffn(l):
        gu, down = I["ffn_w_gu_2"][l], I["ffn_w_down_2"][l]
        at[f"ffn{l}"] = len(st.pieces)

        def gate_up(b):
            for k in (0, 4):
                st.add([(0, 4, FW, chunks(gu, k, 4, b * FW, FW)), (4 * FW, 4, FW, chunks(gu, k, 4, D_FF + b * FW, FW))],
                       by_dve=k == 4 or l == 1 and b == 0)

        for b in range(FN):
            gate_up(b)
            if b >= 1:
                st.add([(0, FC, D, chunks(down, (b - 1) * FC, FC, 0, D))], by_dve=True)
        st.add([(0, FC, D, chunks(down, (FN - 1) * FC, FC, 0, D))], by_dve=True)

    for name, n0 in (("v0", D), ("v1", D + BANK), ("u0", 0), ("u1", BANK)):
        dense(name, I["a_w_in_2"][0], n0, by_dve=(0, 4) if name[0] == "v" else ())
    for h in range(2):
        dense(f"go{h}", I["a_w_out_2"][0], h * BANK)
    ffn(0)
    for h in range(2):
        for name, w, n0 in (("q", I["b_w_q_2"][0], 0), ("k", I["kv_w_2"], 0), ("w", I["kv_w_2"], D)):
            dense(f"{name}{h}", w, n0 + h * BANK, by_dve=(0, 4) if name + str(h) == "q0" or h == 1 and name != "q" else ())
    at["o0"], at["o1"] = [], []
    for k in (0, 4):
        for h in range(2):
            at[f"o{h}"].append(st.add([(0, 4, BANK, chunks(I["b_w_o_2"][0], k, 4, h * BANK, BANK))], by_dve=True))
    ffn(1)
    return st, at


def add_to_x(dve, m, st, at, name, banks, h, done=None):
    dve.wait_ge(st.used, at[name][-1] + 1)
    for t in range(T):
        dst = m.x[:, t, h * BANK:(h + 1) * BANK]
        ins = dve.tensor_tensor(dst, m.ps[:, banks[t], :], dst, ALU.add)
    if done is not None:
        ins.then_inc(done, 1)


def gmlp(nc, m, I, st, at, use):
    with ExitStack() as ctx:
        def sb(name, shape, dt=F32):
            return ctx.enter_context(nc.sbuf_tensor("sb_" + name, shape, dt))

        def sem(name):
            return ctx.enter_context(nc.semaphore(name))

        ps = m.ps
        ut, vt = sb("g_u", [P, T, D]), sb("g_v", [P, T, D])
        wsp, gain = sb("wsp", [P, G_GROUPS, P]), sb("g_gain", [P, D])
        bst, bmv, bvar, brs = sb("g_bst", [P, T, 2, 6]), sb("g_bmv", [P, T, 2]), sb("g_bvar", [P, T]), sb("g_brs", [P, T])
        tmp = sb("g_tmp", [P, G_GROUPS, T, P])
        wsp_in, gain_in, wsp_ready = sem("wsp_in"), sem("gain_in"), sem("wsp_ready")
        z_act, var_ready, rs_ready, v_ready, sp_ps, mix_ready, mixT_ps, mhi, mlo, out_read = (
            sem(s) for s in ("g_z_act", "g_var_ready", "g_rs_ready", "g_v_ready", "sp_ps", "g_mix_ready", "g_mixT_ps",
                             "g_mhi", "g_mlo", "g_out_read"))
        dve_step, tmp_ready = sem("g_dve_step"), sem("g_tmp_ready")
        xhi_ready, xlo_ready = sem("g_xhi_ready"), sem("g_xlo_ready")
        order = ["v0", "v1", "u0", "u1"]
        first = at["v0"][0]
        last = at["go1"][-1]
        look = 2
        NB = [4, 5, 6, 7]
        block = ctx.enter_context(nc.Block())

        def zb(i):
            return [2 * (i % 2) + t for t in range(T)]

        @block.sync
        def _(sp):
            sp.dma_start(wsp[:, :, :], I["w_spT"]).then_inc(wsp_in, 16)
            sp.dma_start(gain[:, :], I["a_v_norm_2"][0].partition_broadcast(P)).then_inc(gain_in, 16)
            for g in range(first + st.slots, last + 1 + st.slots):
                st.load(sp, g)

        @block.scalar
        def _(act):
            def high_half(half):
                for c in range(4 * half, 4 * half + 4):
                    act.wait_ge(mixT_ps, c // 2 + 1)
                    act.activation(m.xhi[:, c, :], turned_ps(m, [0, 1, 2, 3], c), ACT.Copy).then_inc(mhi, 1)

            st.split_hi(act, first)
            norm_hi_act(act, m, use, NB, m.xhi, col(m, "gmlp"), xhi_ready, 0)
            st.split_hi(act, first + 1)
            norm_act(act, m, use)
            for i in range(BANK // P):
                act.activation(m.zero[:, i * P:(i + 1) * P], m.ident, ACT.Copy, scale=0.0)
            for i, name in enumerate(order):
                for g in at[name]:
                    st.split_hi(act, g + look)
                if i == 0:
                    act.wait_ge(m.rstd_ready, use + 1)
                if name == "u1":
                    high_half(0)
                act.wait_ge(st.used, at[name][-1] + 1)
                for t in range(T):
                    dst = (vt, ut)[i // 2][:, t, (i % 2) * BANK:(i % 2 + 1) * BANK]
                    act.activation(dst, ps[:, zb(i)[t], :], ACT.Gelu_apprx_tanh, scale=m.rstd[:, t:t + 1]).then_inc(z_act, 1)
            for i, g in enumerate(at["go0"] + at["go1"]):
                if i == 1:
                    high_half(1)
                if g + look <= last + 1:
                    st.split_hi(act, g + look)

        @block.gpsimd
        def _(pool):
            pool.wait_ge(wsp_in, 16)
            pool.tensor_tensor(wsp[:, :, :], wsp[:, :, :],
                               const(m, "upto").unsqueeze(1).to_broadcast([P, G_GROUPS, P]), ALU.mult).then_inc(wsp_ready, 1)
            norm_pool(pool, m, use)
            for i, name in enumerate(order + ["go0", "go1"]):
                for g in at[name] if i else []:
                    if g + look <= last + 1:
                        st.split_lo(pool, g + look)
                if name == "v1":
                    pool.wait_ge(var_ready, 1)
                    pool.tensor_scalar(bvar[:, :], bmv[:, :, 1], EPS, None, ALU.add).then_inc(rs_ready, 1)
                    pool.wait_ge(rs_ready, 1)
                    pool.tensor_tensor(brs[:, :], bvar[:, :], m.half[:, 0:T], ALU.pow).then_inc(rs_ready, 1)

        @block.tensor
        def _(pe):
            turn_tokens(pe, m, m.x, NB)
            def turn(half):
                pe.wait_ge(z_act, (3 + half) * T)
                for b in (2 * half, 2 * half + 1):
                    pe.wait_ge(mix_ready, 2 * b + 2)
                    for cc in range(2):
                        for t in range(T):
                            c = 2 * b + cc
                            mm = pe.transpose(ps[:, b, cc * SEQ + t * P:cc * SEQ + (t + 1) * P], ut[:, t, c * P:(c + 1) * P], m.ident)
                    mm.then_inc(mixT_ps, 1)

            for i, name in enumerate(order):
                if i >= 2:
                    pe.wait_ge(z_act, T * (i - 1))
                for j, g in enumerate(at[name]):
                    for part in ((0, 2), (2, 4)):
                        if name == "u1" and j == 1 and part[0]:
                            turn(0)
                        dense_granule(pe, st, g, [ps[:, b, :] for b in zb(i)], m.xhi, m.xlo, 4 * j, BANK, j == 0, j == 1,
                                      (xlo_ready, range(1, DC + 1)) if i == 0 else None, part)
                    if name == "u1" and j == 0:
                        pe.wait_ge(v_ready, T)
                        pe.wait_ge(wsp_ready, 1)
                        for q in range(G_GROUPS):
                            mm = pe.matmul(ps[:, 4 + q // 2, (q % 2) * SEQ:(q % 2 + 1) * SEQ], wsp[:, q, :],
                                           vt[:, :, q * P:(q + 1) * P], start=True, stop=True)
                            if q % 2:
                                mm.then_inc(sp_ps, 1)

            for h in range(2):
                for j, g in enumerate(at[f"go{h}"]):
                    for part in ((0, 3), (3, 4)):
                        if h == 0 and j == 0 and part[0]:
                            turn(1)
                        dense_granule(pe, st, g, [ps[:, 4 + 2 * h + t, :] for t in range(T)], m.xhi, m.xlo, 4 * j, BANK,
                                      j == 0, j == 1, (mlo, range(1, DC + 1)) if h == 0 else None, part)

        @block.vector
        def _(dve):
            n_step = [0]

            def link(ins):
                n_step[0] += 1
                ins.then_inc(dve_step, 1)
                dve.wait_ge(dve_step, n_step[0])

            st.split_lo(dve, first)
            norm_lo_dve(dve, m, use, NB, m.xhi, m.xlo, col(m, "gmlp"), xhi_ready, xlo_ready, 0)
            for i in range(1, 4):
                st.split_lo(dve, first + i)

            def low_half(half):
                for c in range(4 * half, 4 * half + 4):
                    dve.wait_ge(mhi, 2 * (c // 2) + 2)
                    dve.tensor_tensor(m.xlo[:, c, :], turned_ps(m, [0, 1, 2, 3], c), m.xhi[:, c, :].bitcast(F32),
                                      ALU.subtract).then_inc(mlo, 1)

            for i in range(2):
                dve.wait_ge(z_act, T * (i + 1))
                for t in range(T):
                    ins = dve.bn_stats(bst[:, t, i, :], vt[:, t, i * BANK:(i + 1) * BANK])
            link(ins)
            for t in range(T):
                ins = dve.bn_aggr(bmv[:, t, :], bst[:, t, :, :].rearrange("p i s -> p (i s)"))
            ins.then_inc(var_ready, 1)
            dve.wait_ge(rs_ready, 2)
            for t in range(T):
                dve.tensor_scalar(vt[:, t, :], vt[:, t, :], bmv[:, t, 0:1], brs[:, t:t + 1], ALU.subtract,
                                  ALU.mult).then_inc(v_ready, 1)
            dve.wait_ge(gain_in, 16)
            for half in range(2):
                groups = range(4 * half, 4 * half + 4)
                for q in groups:
                    dve.wait_ge(sp_ps, q // 2 + 1)
                    dve.tensor_tensor(tmp[:, q, :, :], ps[:, 4 + q // 2, (q % 2) * SEQ:(q % 2 + 1) * SEQ].rearrange("p (t d) -> p t d", t=T),
                                      gain[:, q * P:(q + 1) * P].unsqueeze(1).to_broadcast([P, T, P]), ALU.mult).then_inc(tmp_ready, 1)
                if half == 1:
                    low_half(0)
                dve.wait_ge(z_act, (3 + half) * T)
                dve.wait_ge(tmp_ready, 4 * half + 4)
                for q in groups:
                    sl = slice(q * P, (q + 1) * P)
                    dve.scalar_tensor_tensor(ut[:, :, sl], tmp[:, q, :, :], col(m, "b_sp")[:, q:q + 1], ut[:, :, sl],
                                             ALU.add, ALU.mult).then_inc(mix_ready, 1)
            low_half(1)
            for h in range(2):
                add_to_x(dve, m, st, at, f"go{h}", [4 + 2 * h + t for t in range(T)], h)


def swiglu(nc, m, I, st, at, l, use, final=False):
    with ExitStack() as ctx:
        def sb(name, shape, dt=F32):
            return ctx.enter_context(nc.sbuf_tensor(f"sb_f{l}_" + name, shape, dt))

        def sem(name):
            return ctx.enter_context(nc.semaphore(f"f{l}_" + name))

        ps = m.ps
        sg, ft = sb("sg", [P, T, FW]), sb("ft", [P, T, FW])
        ahi, alo = sb("ahi", [P, FC, SEQ], F32R), sb("alo", [P, FC, SEQ], F32R)
        zhi, zlo = sb("zhi", [P, FC, SEQ], F32R), sb("zlo", [P, FC, SEQ], F32R)
        xhi_ready, xlo_ready, silu_ready, ft_ready, turn_ps, ahi_ready, alo_ready, sums_ready, x_ready = (
            sem(s) for s in ("xhi_ready", "xlo_ready", "silu_ready", "ft_ready", "turn_ps", "ahi_ready", "alo_ready",
                             "sums_ready", "x_ready"))
        g0 = at[f"ffn{l}"]
        n_gran = 3 * FN
        gain = col(m, f"ffn{l}")
        ACC, GU, TURN = (0, 1, 2, 3), (4, 5), 6
        NB = list(ACC)
        ROUND, BLOCKS = 6, 2
        TURNS = (FN - 3) // BLOCKS
        look = 2

        def shift(it, n):
            return 0 if isinstance(it, int) and it == 0 else it * n

        def w_hi(act, i, it):
            g = g0 + i
            n = st.size(g)
            act.wait_ge(st.landed[g % st.slots], shift(it, 16 * len(st.pieces[g])) + st.arrive[g])
            act.wait_ge(st.used, shift(it, ROUND) + (g - st.hi_bufs + 1))
            act.activation(st.hi[:, g % st.hi_bufs, 0:n], st.ring[:, g % st.slots, 0:n], ACT.Copy).then_inc(st.hi_ready, 1)

        def is_down(i):
            return i >= 2 and (i - 2) % 3 == 2 or i == n_gran - 1

        def by_dve(i):
            return is_down(i) or (i == 1 if i < 2 else (i - 2) % 3 == 1)

        def w_lo(eng, i, it):
            g = g0 + i
            n = st.size(g)
            eng.wait_ge(st.hi_ready, shift(it, ROUND) + (g + 1))
            eng.tensor_tensor(st.lo[:, g % st.hi_bufs, 0:n], st.ring[:, g % st.slots, 0:n],
                              st.hi[:, g % st.hi_bufs, 0:n].bitcast(F32), ALU.subtract).then_inc(st.lows[g][0], 1)

        def lo_done(eng, i, it):
            s, n = st.lows[g0 + i]
            eng.wait_ge(s, shift(it, 2 * BLOCKS if by_dve(i) else BLOCKS) + n)

        def gu_index(b):
            return 0 if b == 0 else 2 + 3 * (b - 1)

        def down_index(b):
            return 4 + 3 * b if b < FN - 1 else n_gran - 1

        block = ctx.enter_context(nc.Block())

        @block.sync
        def _(sp):
            def load(i, it):
                g = g0 + i
                lo_done(sp, i - st.slots, it)
                for off, nk, n, src in pieces(i, it):
                    dst = st.ring[:, g % st.slots, off:off + nk * n].rearrange("p (k n) -> p k n", n=n)
                    sp.dma_start(dst, src).then_inc(st.landed[g % st.slots], 16)

            def pieces(i, it):
                if is_down(i):
                    b = (i - 2) // 3
                    src = I["ffn_w_down_2"][l, bass.ds(it * (BLOCKS * FW) + b * FW, FW), :].rearrange("(k p) n -> p k n", p=P)
                    return [(0, FC, D, src)]
                b, k = 1 + (i - 2) // 3, 4 * ((i - 2) % 3)
                rows = I["ffn_w_gu_2"][l, k * P:(k + 4) * P, :]
                return [(a * 4 * FW, 4, FW, rows[:, bass.ds(it * (BLOCKS * FW) + (a * D_FF + b * FW), FW)]
                         .rearrange("(k p) n -> p k n", p=P)) for a in range(2)]

            for i in range(st.slots, 2 + ROUND):
                st.load(sp, g0 + i)
            with sp.Fori(0, TURNS - 1) as it:
                for r in range(ROUND):
                    load(2 + ROUND + r, it)
            for i in range(2 + ROUND * TURNS, n_gran):
                st.load(sp, g0 + i)
            for g in range(g0 + n_gran, min(g0 + n_gran + st.slots, len(st.pieces))):
                st.load(sp, g)
            if final:
                sp.dma_start(m.final_gain[:, :], I["final_norm_2"].partition_broadcast(P)).then_inc(m.gain_in, 16)

        @block.scalar
        def _(act):
            norm_hi_act(act, m, use, NB, m.xhi, gain, xhi_ready, 0)
            w_hi(act, 1, 0)
            norm_act(act, m, use)

            def part(b, it):
                i = gu_index(b)
                for r in range(3 if b else 2):
                    if i + r + look < n_gran:
                        w_hi(act, i + r + look, it)
                    else:
                        st.split_hi(act, g0 + n_gran)
                    if r == 1:
                        act.wait_ge(st.used, shift(it, ROUND) + (g0 + i + 2))
                        for t in range(T):
                            act.activation(sg[:, t, :], ps[:, GU[t], 0:FW], ACT.Silu, scale=m.rstd[:, t:t + 1]).then_inc(silu_ready, 1)
                act.wait_ge(turn_ps, shift(it, BLOCKS) + (b + 1))
                hi = zhi if b == FN - 1 else ahi
                act.activation(hi[:, :, :].rearrange("p c s -> p (c s)"), ps[:, TURN, :], ACT.Copy).then_inc(ahi_ready, 1)

            act.wait_ge(m.rstd_ready, use + 1)
            part(0, 0)
            with act.Fori(0, TURNS) as it:
                for b in range(1, 1 + BLOCKS):
                    part(b, it)
            for b in range(FN - 2, FN):
                part(b, 0)
            st.split_hi(act, g0 + n_gran + 1)
            if final:
                act.wait_ge(x_ready, T)
                norm_act(act, m, use + 1, range(1))

        @block.gpsimd
        def _(pool):
            norm_pool(pool, m, use)
            for i in range(2, 2 + look):
                if not by_dve(i):
                    w_lo(pool, i, 0)
            with pool.Fori(0, TURNS) as it:
                for r in range(ROUND):
                    if not by_dve(2 + look + r):
                        w_lo(pool, 2 + look + r, it)
            for i in range(2 + look + ROUND * TURNS, n_gran):
                if not by_dve(i):
                    w_lo(pool, i, 0)
            for g in range(g0 + n_gran, min(g0 + n_gran + look, len(st.pieces))):
                if st.lows[g][0] is st.lo_pool:
                    st.split_lo(pool, g)
            if final:
                norm_pool_tile(pool, m, use + 1, 0)

        @block.tensor
        def _(pe):
            turn_tokens(pe, m, m.x, NB)

            def gate_up(b, it):
                for j in range(2):
                    i = gu_index(b) + j
                    lo_done(pe, i, it)
                    whi, wlo = [x[:, (g0 + i) % st.hi_bufs, :].rearrange("p (a k n) -> p k a n", a=2, n=FW) for x in (st.hi, st.lo)]
                    for k in range(4):
                        c = 4 * j + k
                        if b == 0:
                            pe.wait_ge(xlo_ready, c + 1)
                        for t in range(T):
                            mm = three_products(pe, ps[:, GU[t], :], m.xhi[:, c, t * P:(t + 1) * P], m.xlo[:, c, t * P:(t + 1) * P],
                                                whi[:, k, :, :], wlo[:, k, :, :], c == 0, c == DC - 1)
                    mm.then_inc(st.used, 1)

            def down(b, it):
                i = down_index(b)
                lo_done(pe, i, it)
                pe.wait_ge(alo_ready, shift(it, BLOCKS) + (b + 1))
                whi, wlo = [x[:, (g0 + i) % st.hi_bufs, :].rearrange("p (k n) -> p k n", n=D) for x in (st.hi, st.lo)]
                hi, lo = (zhi, zlo) if b == FN - 1 else (ahi, alo)
                for t in range(T):
                    if b == FN - 2 and t == 1:
                        turn(FN - 1, 0)
                    for h in range(2):
                        hs = slice(h * BANK, (h + 1) * BANK)
                        for k in range(FC):
                            at_, al_ = hi[:, k, t * P:(t + 1) * P], lo[:, k, t * P:(t + 1) * P]
                            out = ps[:, ACC[2 * t + h], :]
                            for a, w in ((at_, whi), (at_, wlo), (al_, whi)):
                                mm = pe.matmul(out, a, w[:, k, hs], start=False, stop=True, skip_group_check=True)
                        if b == FN - 1 and 2 * t + h < 3:
                            mm.then_inc(sums_ready, 1)
                mm.then_inc(st.used, 1)

            def turn(b, it):
                pe.wait_ge(ft_ready, shift(it, T * BLOCKS) + T * (b + 1))
                for c in range(FC):
                    for t in range(T):
                        mm = pe.transpose(ps[:, TURN, c * SEQ + t * P:c * SEQ + (t + 1) * P], ft[:, t, c * P:(c + 1) * P], m.ident)
                mm.then_inc(turn_ps, 1)

            gate_up(0, 0)
            for b in ACC:
                pe.matmul(ps[:, b, :], m.zero[:, 0:P], m.zero[:, :], start=True, stop=True)
            turn(0, 0)
            with pe.Fori(0, TURNS) as it:
                for b in range(1, 1 + BLOCKS):
                    gate_up(b, it)
                    down(b - 1, it)
                    turn(b, it)
            for b in range(FN - 2, FN):
                gate_up(b, 0)
                down(b - 1, 0)
                if b < FN - 1:
                    turn(b, 0)
            down(FN - 1, 0)

        @block.vector
        def _(dve):
            norm_lo_dve(dve, m, use, NB, m.xhi, m.xlo, gain, xhi_ready, xlo_ready, 0)
            w_lo(dve, 1, 0)

            def part(b, it):
                i = gu_index(b)
                ahead = [i + r + look for r in range(3 if b else 2) if i + r + look < n_gran and by_dve(i + r + look)]
                for j in ahead:
                    if is_down(j):
                        w_lo(dve, j, it)
                for t in range(T):
                    dve.wait_ge(silu_ready, shift(it, T * BLOCKS) + (T * b + t + 1))
                    dve.scalar_tensor_tensor(ft[:, t, :], ps[:, GU[t], FW:], m.rstd[:, t:t + 1], sg[:, t, :], ALU.mult,
                                             ALU.mult).then_inc(ft_ready, 1)
                for j in ahead:
                    if not is_down(j):
                        w_lo(dve, j, it)
                dve.wait_ge(ahi_ready, shift(it, BLOCKS) + (b + 1))
                hi, lo = (zhi, zlo) if b == FN - 1 else (ahi, alo)
                dve.tensor_tensor(lo[:, :, :].rearrange("p c s -> p (c s)"), ps[:, TURN, :],
                                  hi[:, :, :].rearrange("p c s -> p (c s)").bitcast(F32), ALU.subtract).then_inc(alo_ready, 1)

            dve.wait_ge(m.rstd_ready, use + 1)
            part(0, 0)
            with dve.Fori(0, TURNS) as it:
                for b in range(1, 1 + BLOCKS):
                    part(b, it)
            for b in range(FN - 2, FN):
                part(b, 0)
            for g in range(g0 + n_gran, min(g0 + n_gran + look, len(st.pieces))):
                if st.lows[g][0] is st.lo_dve:
                    st.split_lo(dve, g)
            for t in range(T):
                for h in range(2):
                    if 2 * t + h < 3:
                        dve.wait_ge(sums_ready, 2 * t + h + 1)
                    else:
                        dve.wait_ge(st.used, g0 + n_gran)
                    dst = m.x[:, t, h * BANK:(h + 1) * BANK]
                    dve.tensor_tensor(dst, ps[:, ACC[2 * t + h], :], dst, ALU.add).then_inc(x_ready, 1)


def diff_attention(nc, m, I, st, at, use):
    with ExitStack() as ctx:
        def sb(name, shape, dt=F32):
            return ctx.enter_context(nc.sbuf_tensor("sb_" + name, shape, dt))

        def sem(name):
            return ctx.enter_context(nc.semaphore(name))

        ps = m.ps
        khi, klo = sb("d_khi", [P, DC, SEQ], F32R), sb("d_klo", [P, DC, SEQ], F32R)
        yhi, ylo = sb("d_yhi", [P, DC, SEQ], F32R), sb("d_ylo", [P, DC, SEQ], F32R)
        qt, kt, vt = sb("d_q", [P, T, D]), sb("d_k", [P, T, D]), sb("d_v", [P, T, D])
        dist, lam_in_ = sb("dist", [P, 3 * P]), sb("lam_in", [P, N_LAM])
        lam, lamw = sb("lam", [P, 8]), sb("lamw", [P, 2 * D_DIM])
        sub = sb("sub", [P, 1])
        qkT = sb("d_qkT", [P, 2, SEQ])
        bias = sb("d_bias", [P, 2, 3 * P])
        e = sb("d_e", [P, 2, 3 * P])
        eT = sb("d_eT", [P, 3 * P])
        mx, sm = sb("d_mx", [P, 2, 4]), sb("d_sm", [P, 2, 8])
        ratio = sb("d_ratio", [P, T])
        ost, on = sb("d_ost", [P, 3, T]), sb("d_on", [P, T, D_V])
        xhi_ready, xlo_ready, z_act, dist_in, lam_in, dve_step, pool_step = (
            sem(s) for s in ("d_xhi_ready", "d_xlo_ready", "d_z_act", "d_dist_in", "d_lam_in", "d_dve_step", "d_pool_step"))
        lsum_ready, lexp_ready, lam_ready = sem("lsum_ready"), sem("lexp_ready"), sem("lam_ready")
        bias_ready, qk_ps, qkT_ready, s_ps, mx_ready, e_ready, a_ready, aT_ps, aT_ready, o_ps, osum_ready, ors_ready, on_ready, oT_ps, ohi, olo = (
            sem(s) for s in ("bias_ready", "d_qk_ps", "d_qkT_ready", "s_ps", "d_mx_ready", "e_ready", "a_ready", "aT_ps",
                             "aT_ready", "o_ps", "osum_ready", "ors_ready", "on_ready", "oT_ps", "ohi", "olo"))
        order = ["q0", "k0", "w0", "q1", "k1", "w1"]
        fill = [[("q1", 0, None), ("q1", 1, None)]]
        fill += [[(name, j, (0, 1)), (name, j, (1, 4))]
                 for name, j in (("k1", 0), ("k1", 1), ("w1", 0), ("w1", 1), ("o0", 0), ("o1", 0))]
        fill += [[None, ("o0", 1, (0, 2))], [("o0", 1, (2, 3)), ("o1", 1, (0, 2))]]
        tail = (("o1", 1, (2, 3)), ("o0", 1, (3, 4)), ("o1", 1, (3, 4)))
        first, last = at["q0"][0], at["o1"][-1]
        look = 2
        NB = [4, 5, 6, 7]
        QK, S, AO = 4, (5, 6), 7
        SCALE = float(D_DIM) ** -0.5
        slopes = [2.0 ** (-8.0 * (h + 1) / D_HEADS) for h in range(D_HEADS)]
        spans = [slice(0, P), slice(P, 3 * P)]
        block = ctx.enter_context(nc.Block())

        def zb(name):
            i = order.index(name) if name in order else int(name[1])
            return [2 * (i % 2) + t for t in range(T)]

        def z_done(name):
            return T * (order.index(name) + 1)

        splits = [[8, 9], [10], [11], [12], [13], [14], [15], [16], []]

        @block.sync
        def _(sp):
            sp.dma_start(dist[:, :], I["c_late"][:, 0:3 * P]).then_inc(dist_in, 16)
            sp.dma_start(lam_in_[:, :], I["v_lam"]).then_inc(lam_in, 16)
            for g in range(first + st.slots, last + 1 + st.slots):
                st.load(sp, g)

        @block.scalar
        def _(act):
            def evac(name):
                act.wait_ge(st.used, at[name][-1] + 1)
                for t in range(T):
                    dst = {"q": qt, "k": kt, "w": vt}[name[0]][:, t, int(name[1]) * BANK:(int(name[1]) + 1) * BANK]
                    act.activation(dst, ps[:, zb(name)[t], :], ACT.Copy, scale=m.rstd[:, t:t + 1]).then_inc(z_act, 1)

            for b in range(4):
                act.wait_ge(m.xturn_ps, 4 * use + b + 1)
                for hi, name in ((m.xhi, "bq"), (khi, "kv")):
                    for c in (2 * b, 2 * b + 1):
                        act.activation(hi[:, c, :], turned_ps(m, NB, c), ACT.Copy,
                                       scale=col(m, name)[:, c:c + 1]).then_inc(xhi_ready, 1)
            st.split_hi(act, first + look)
            norm_act(act, m, use)
            act.wait_ge(lsum_ready, 1)
            act.activation(lam[:, 2:4], lam[:, 0:2], ACT.Exp).then_inc(lexp_ready, 1)
            for name in order[:3]:
                for g in at[name]:
                    if g > first:
                        st.split_hi(act, g + look)
                if name == order[0]:
                    act.wait_ge(m.rstd_ready, use + 1)
                evac(name)
            for s in range(D_HEADS + 1):
                if s < D_HEADS:
                    act.wait_ge(qk_ps, s + 1)
                    if s >= 1:
                        act.wait_ge(s_ps, s)
                    act.activation(qkT[:, :, :].rearrange("p a s -> p (a s)"), ps[:, QK, :], ACT.Copy).then_inc(qkT_ready, 1)
                if s >= 1:
                    act.wait_ge(aT_ps, s)
                    act.activation(eT[:, :], ps[:, S[0], 0:3 * P], ACT.Copy).then_inc(aT_ready, 1)
                    if fill[s - 1][1][0] in order and fill[s - 1][1][1] == 1:
                        evac(fill[s - 1][1][0])
                for g in splits[s] if s >= 1 else splits[0][:1]:
                    st.split_hi(act, first + g)
                if s >= 1:
                    act.wait_ge(o_ps, s)
                    for t in range(T):
                        act.activation(on[:, t, :], ps[:, AO, t * P:(t + 1) * P], ACT.Square,
                                       scale=sm[:, (s - 1) % 2, 4 + t:5 + t], accum_out=ost[:, 0, t:t + 1]).then_inc(osum_ready, 1)
                if s < D_HEADS:
                    act.wait_ge(mx_ready, s + 1)
                    for i in range(2):
                        for t in range(T):
                            act.activation(e[:, i, spans[t]], e[:, i, spans[t]], ACT.Exp, bias=mx[:, 1, 2 * i + t:2 * i + t + 1],
                                           scale=SCALE, accum_out=sm[:, s % 2, 2 * i + t:2 * i + t + 1]).then_inc(e_ready, 1)
                if s >= 1:
                    act.wait_ge(oT_ps, s)
                    act.activation(yhi[:, s - 1, :], ps[:, AO, SEQ:], ACT.Copy, scale=sub[:, 0:1]).then_inc(ohi, 1)
                else:
                    st.split_hi(act, first + splits[0][1])

        @block.gpsimd
        def _(pool):
            n_step = [0]

            def link(ins):
                n_step[0] += 1
                ins.then_inc(pool_step, 1)
                pool.wait_ge(pool_step, n_step[0])

            def bias_of(h):
                if h >= 2:
                    pool.wait_ge(mx_ready, h - 1)
                pool.tensor_scalar(bias[:, h % 2, :], dist[:, :], slopes[h] / SCALE, None, ALU.mult).then_inc(bias_ready, 1)

            st.split_lo(pool, first + look)
            norm_pool(pool, m, use)
            for g in range(first + 1, at["w0"][-1] + 1):
                st.split_lo(pool, g + look)
            pool.wait_ge(dist_in, 16)
            bias_of(0)
            bias_of(1)
            for s in range(1, D_HEADS + 1):
                pool.wait_ge(osum_ready, T * s)
                link(pool.tensor_scalar(ost[:, 1, :], ost[:, 0, :], 1.0 / D_V, EPS, ALU.mult, ALU.add))
                pool.tensor_tensor(ost[:, 2, :], ost[:, 1, :], m.half[:, 0:T], ALU.pow).then_inc(ors_ready, 1)
                if s + 1 < D_HEADS:
                    bias_of(s + 1)

        @block.tensor
        def _(pe):
            def granule(name, j, part=None):
                if j == 0 and name[0] == "o":
                    pe.wait_ge(z_act, z_done(("k1", "w1")[int(name[1])]))
                elif j == 0 and order.index(name) >= 2:
                    pe.wait_ge(z_act, z_done(order[order.index(name) - 2]))
                if name[0] == "o":
                    pe.wait_ge(olo, 4 * j + (part[1] if part else 4))
                hi, lo = {"q": (m.xhi, m.xlo), "o": (yhi, ylo)}.get(name[0], (khi, klo))
                turned = {"q0": (xlo_ready, [4 * (c // 2) + c % 2 + 1 for c in range(DC)]),
                          "k0": (xlo_ready, [4 * (c // 2) + c % 2 + 3 for c in range(DC)])}.get(name)
                dense_granule(pe, st, at[name][j], [ps[:, b, :] for b in zb(name)], hi, lo, 4 * j, BANK, j == 0, j == 1, turned, part)

            turn_tokens(pe, m, m.x, NB)
            for name in order[:3]:
                for j in range(2):
                    granule(name, j)
            pe.wait_ge(xlo_ready, 2 * DC)
            for s in range(D_HEADS + 1):
                if s < D_HEADS:
                    pe.wait_ge(z_act, z_done("k1" if s >= 4 else "k0"))
                    if s >= 1:
                        pe.wait_ge(qkT_ready, s)
                    for a, src in ((0, qt), (1, kt)):
                        for t in range(T):
                            mm = pe.transpose(ps[:, QK, a * SEQ + t * P:a * SEQ + (t + 1) * P], src[:, t, s * P:(s + 1) * P], m.ident)
                    mm.then_inc(qk_ps, 1)
                if s >= 1:
                    pe.wait_ge(a_ready, s)
                    for n in range(3):
                        mm = pe.transpose(ps[:, S[0], n * P:(n + 1) * P], e[:, 0, n * P:(n + 1) * P], m.ident)
                    mm.then_inc(aT_ps, 1)
                if fill[s][0] is not None:
                    granule(*fill[s][0])
                if s < D_HEADS:
                    pe.wait_ge(qkT_ready, s + 1)
                    if s >= 1:
                        pe.wait_ge(aT_ready, s)
                    for i in range(2):
                        r = slice(i * D_DIM, (i + 1) * D_DIM)
                        for t in range(T):
                            mm = pe.matmul(ps[:, S[i], spans[t]], qkT[r, 0, t * P:(t + 1) * P], qkT[r, 1, 0:(t + 1) * P],
                                           start=True, stop=True)
                    mm.then_inc(s_ps, 1)
                if s >= 1:
                    h = s - 1
                    pe.wait_ge(aT_ready, s)
                    if s >= 2:
                        pe.wait_ge(olo, s - 1)
                    pe.wait_ge(z_act, z_done("w1" if h >= 4 else "w0"))
                    v = [vt[:, k, h * P:(h + 1) * P] for k in range(T)]
                    pe.matmul(ps[:, AO, 0:P], eT[:, 0:P], v[0], start=True, stop=True)
                    pe.matmul(ps[:, AO, P:2 * P], eT[:, P:2 * P], v[0], start=True, stop=False)
                    pe.matmul(ps[:, AO, P:2 * P], eT[:, 2 * P:], v[1], start=False, stop=True).then_inc(o_ps, 1)
                granule(*fill[s][1])
                if s >= 1:
                    pe.wait_ge(on_ready, T * s)
                    for t in range(T):
                        mm = pe.transpose(ps[:, AO, SEQ + t * P:SEQ + (t + 1) * P], on[:, t, :], m.ident)
                    mm.then_inc(oT_ps, 1)
            for f in tail:
                granule(*f)

        @block.vector
        def _(dve):
            n_step = [0]

            def link(ins):
                n_step[0] += 1
                ins.then_inc(dve_step, 1)
                dve.wait_ge(dve_step, n_step[0])

            for b in range(4):
                dve.wait_ge(xhi_ready, 4 * b + 4)
                for hi, lo, name in ((m.xhi, m.xlo, "bq"), (khi, klo, "kv")):
                    for c in (2 * b, 2 * b + 1):
                        dve.scalar_tensor_tensor(lo[:, c, :], turned_ps(m, NB, c), col(m, name)[:, c:c + 1],
                                                 hi[:, c, :].bitcast(F32), ALU.mult, ALU.subtract).then_inc(xlo_ready, 1)
            dve.wait_ge(lam_in, 16)
            for i in range(2):
                a = lam_in_[:, 2 * i * D_DIM:(2 * i + 1) * D_DIM]
                b = lam_in_[:, (2 * i + 1) * D_DIM:(2 * i + 2) * D_DIM]
                ins = dve.tensor_tensor_reduce(lamw[:, i * D_DIM:(i + 1) * D_DIM], a, b, 1.0, 0.0, ALU.mult, ALU.add, lam[:, i:i + 1])
            ins.then_inc(lsum_ready, 1)
            dve.wait_ge(lexp_ready, 1)
            link(dve.tensor_tensor(lam[:, 4:5], lam[:, 3:4], lam[:, 2:3], ALU.subtract))
            link(dve.tensor_scalar(lam[:, 5:6], lam[:, 4:5], -LAMBDA_INIT, None, ALU.add))
            dve.tensor_scalar(sub[:, :], col(m, "subln"), 1.0 - LAMBDA_INIT, None, ALU.mult).then_inc(lam_ready, 1)
            dve.wait_ge(lam_ready, 1)
            st.split_lo(dve, first + splits[0][0])
            for s in range(D_HEADS + 1):
                if s < D_HEADS:
                    dve.wait_ge(s_ps, s + 1)
                    dve.wait_ge(bias_ready, s + 1)
                    if s >= 1:
                        dve.wait_ge(aT_ps, s)
                    for i in range(2):
                        for t in range(T):
                            ins = dve.tensor_tensor_reduce(e[:, i, spans[t]], ps[:, S[i], spans[t]], bias[:, s % 2, spans[t]], 1.0,
                                                           -3e38, ALU.add, ALU.max, mx[:, 0, 2 * i + t:2 * i + t + 1])
                    link(ins)
                    dve.tensor_scalar(mx[:, 1, :], mx[:, 0, :], -SCALE, None, ALU.mult).then_inc(mx_ready, 1)
                if s >= 1:
                    dve.wait_ge(ors_ready, s)
                    for t in range(T):
                        dve.tensor_scalar(on[:, t, :], ps[:, AO, t * P:(t + 1) * P], ost[:, 2, t:t + 1],
                                          sm[:, (s - 1) % 2, 4 + t:5 + t], ALU.mult, ALU.mult).then_inc(on_ready, 1)
                if s < D_HEADS:
                    dve.wait_ge(e_ready, 4 * (s + 1))
                    link(dve.reciprocal(sm[:, s % 2, 4:8], sm[:, s % 2, 0:4]))
                    link(dve.scalar_tensor_tensor(ratio[:, :], sm[:, s % 2, 0:2], lam[:, 5:6], sm[:, s % 2, 6:8], ALU.mult, ALU.mult))
                    for t in range(T):
                        ins = dve.scalar_tensor_tensor(e[:, 0, spans[t]], e[:, 1, spans[t]], ratio[:, t:t + 1], e[:, 0, spans[t]],
                                                       ALU.mult, ALU.add)
                    ins.then_inc(a_ready, 1)
                if s >= 1:
                    dve.wait_ge(ohi, s)
                    dve.scalar_tensor_tensor(ylo[:, s - 1, :], ps[:, AO, SEQ:], sub[:, 0:1], yhi[:, s - 1, :].bitcast(F32),
                                             ALU.mult, ALU.subtract).then_inc(olo, 1)
                for g in splits[s] if s >= 1 else splits[0][1:]:
                    st.split_lo(dve, first + g)
            for h in range(2):
                add_to_x(dve, m, st, at, f"o{h}", zb(f"o{h}"), h)


def final_norm(nc, m, I, out, use):
    with ExitStack() as ctx:
        y_ready = ctx.enter_context(nc.semaphore("y_ready"))
        y = ctx.enter_context(nc.sbuf_tensor("sb_y", [P, T, D], F32))
        block = ctx.enter_context(nc.Block())
        dram = out[0].rearrange("(t p) d -> p t d", p=P)

        @block.sync
        def _(sp):
            for t in range(T):
                sp.wait_ge(y_ready, t + 1)
                sp.dma_start(dram[:, t, :], y[:, t, :]).then_inc(m.out_done, 16)
            sp.wait_ge(m.out_done, 16 * T)

        @block.scalar
        def _(act):
            norm_act(act, m, use, range(1, T))

        @block.gpsimd
        def _(pool):
            norm_pool_tile(pool, m, use, 1)

        @block.vector
        def _(dve):
            dve.wait_ge(m.gain_in, 16)
            for t in range(T):
                dve.wait_ge(m.rstd_ready, use + t + 1)
                dve.scalar_tensor_tensor(y[:, t, :], m.x[:, t, :], m.rstd[:, t:t + 1], m.final_gain[:, :], ALU.mult,
                                         ALU.mult).then_inc(y_ready, 1)



def program(nc, I, out):
    m = Shared()
    with ExitStack() as ctx:
        def sb(name, shape, dt=F32):
            return ctx.enter_context(nc.sbuf_tensor("sb_" + name, shape, dt))

        def sem(name):
            return ctx.enter_context(nc.semaphore(name))

        m.ps = ctx.enter_context(nc.psum_tensor("ps", [P, 8, BANK], F32))
        m.x, m.xs = sb("x", [P, T, D]), sb("xs", [P, T, D])
        m.sumsq, m.meansq, m.rstd = sb("sumsq", [P, T]), sb("meansq", [P, T]), sb("rstd", [P, T])
        m.consts, m.cols, m.rows = sb("consts", [P, N_CONSTS]), sb("cols", [P, N_COLS]), sb("rows", [P, N_ROWS])
        m.ident, m.half = const(m, "ident"), const(m, "half")
        m.sumsq_ready, m.meansq_ready, m.rstd_ready = sem("sumsq_ready"), sem("meansq_ready"), sem("rstd_ready")
        m.wr, m.wr_in = sb("wr", [P, DC, N_EXP]), sem("wr_in")
        m.xturn_ps, m.out_done = sem("xturn_ps"), sem("out_done")
        m.ring = sb("ring", [P, EARLY * GK * E_FF])
        m.e_landed = [sem(f"e_landed{i}") for i in range(NS)]
        st, at = second_stream(m, ctx, nc, I)
        mixer(nc, m, I)
        experts(nc, m, I, st)
        m.xhi, m.xlo = sb("xhi2", [P, DC, SEQ], F32R), sb("xlo2", [P, DC, SEQ], F32R)
        st.place_halves(ctx, nc, "net")
        m.zero = sb("zero", [P, BANK], F32R)
        gmlp(nc, m, I, st, at, 2)
        swiglu(nc, m, I, st, at, 0, 3)
        diff_attention(nc, m, I, st, at, 4)
        m.final_gain, m.gain_in = sb("final_gain", [P, D]), sem("final_gain_in")
        swiglu(nc, m, I, st, at, 1, 5, final=True)
        final_norm(nc, m, I, out, 6)


_INS = ["x", "w_in", "w_a_out", "w_b_out", "w_uq", "w_ukv", "w_c_out", "w_out", "w_router", "w_e_gate", "w_e_up",
        "w_e_down", "a_w_in_2", "a_v_norm_2", "a_w_out_2", "ffn_w_gu_2", "ffn_w_down_2", "kv_w_2",
        "b_w_q_2", "b_w_o_2", "final_norm_2"]


def constants():
    import numpy as np

    i = np.arange(P)
    a, b = i[:, None], i[None, :]
    z = np.zeros((P, P))
    ang = (np.arange(SEQ, dtype=np.float32)[:, None]
           * (np.float32(10000.0) ** (-np.arange(0, C_ROPE, 2, dtype=np.float32) / C_ROPE))[None, :])
    turn = lambda y: y.reshape(T, P, 16).transpose(1, 0, 2).reshape(P, T * 16)
    c = {
        "ident": a == b, "upto": a <= b, "from": a >= b, "ones": z + 1,
        "causal": np.concatenate([z, np.where(b <= a, 0, NEG)], 1),
        "anti": np.concatenate([np.where(b >= a, 0, NEG), z], 1),
        "cos": turn(np.cos(ang)), "sin": turn(np.sin(ang)),
        "half": z[:, :8] - 0.5,
    }
    dist = np.concatenate([np.where(b <= a, b - a, NEG), b - a - P, np.where(b <= a, b - a, NEG)], 1)
    late = np.concatenate([dist, z[:, :CAP] + np.arange(1, CAP + 1)], 1)
    sel = np.zeros((8, 8, P), np.float32)
    sel[np.arange(8), np.arange(8)] = 1
    return np.concatenate([c[n] for n in CONSTS], 1).astype(np.float32), sel, late.astype(np.float32)


def arrays_of(inputs):
    import numpy as np

    f = {k: np.asarray(v) for k, v in inputs.items()}
    vec = {"mix": f["mix_norm_g"], "a_norm": f["a_norm_g"], "conv_w": f["conv_w"], "conv_b": f["conv_b"],
           "ln_g": f["conv_ln_g"], "ln_b": f["conv_ln_b"], "cq": f["cq_norm_g"], "ckv": f["ckv_norm_g"],
           "ffn": f["ffn_norm_g"], "gmlp": f["a_norm_2"], "ffn0": f["ffn_norm_2"][0], "ffn1": f["ffn_norm_2"][1],
           "kv": f["kv_norm_2"], "bq": f["b_norm_2"], "b_sp": f["a_b_sp_2"], "subln": f["b_subln_2"]}
    rows = {"b_if": f["b_if"], "q_g": f["q_norm_g"], "k_g": f["k_norm_g"]}
    arrays = {n: np.ascontiguousarray(f[n]) for n in _INS}
    arrays["w_spT"] = np.ascontiguousarray(f["a_w_sp_2"][0].transpose(2, 0, 1))
    arrays["v_cols"] = np.ascontiguousarray(np.concatenate([vec[n].reshape(-1, P).T for n in COLS], 1))
    line = np.concatenate([rows[n].reshape(-1) for n in ROWS])
    arrays["v_rows"] = np.ascontiguousarray(np.broadcast_to(line, (P, N_ROWS)))
    arrays["v_lam"] = np.ascontiguousarray(np.broadcast_to(f["b_lambda_2"].reshape(-1), (P, N_LAM)))
    arrays["c_consts"], arrays["c_sel"], arrays["c_late"] = constants()
    return arrays


def kernel(**inputs):
    import numpy as np
    import concourse.bacc as bacc
    from concourse.bass_utils import run_bass_kernel_spmd

    nc = bacc.Bacc("TRN2", target_bir_lowering=False, num_devices=1)
    arrays = arrays_of(inputs)
    I = {n: nc.dram_tensor(n, a.shape, mybir.dt.from_np(a.dtype), kind="ExternalInput").ap() for n, a in arrays.items()}
    out = nc.dram_tensor("out", (1, SEQ, D), F32, kind="ExternalOutput").ap()
    program(nc, I, out)
    return run_bass_kernel_spmd(nc, [arrays], core_ids=[0]).results[0]["out"]
```
